# Optimizing a Trainium2 kernel written in Bass

```python
import jax, jax.numpy as jnp
from jax import lax
import numpy as np

D_MODEL = 1024
BATCH = 1
SEQ = 512
DEPTH = 1

MEM_LEN = 256
HG_HEADS = 4
HG_KEY_DIM = 128
HG_VAL_DIM = 128
HG_KW = HG_HEADS * HG_KEY_DIM
HG_VW = HG_HEADS * HG_VAL_DIM
HG_CHUNK = 64
ATT_Q_HEADS = 8
ATT_KV_HEADS = 2
ATT_GROUP = ATT_Q_HEADS // ATT_KV_HEADS
ATT_HEAD_DIM = 64
ATT_QW = ATT_Q_HEADS * ATT_HEAD_DIM
ATT_KVW = ATT_KV_HEADS * ATT_HEAD_DIM
WINDOW = 128
ATT_BLOCK = 128
ROPE_THETA = 500000.0
ROT_DIM = ATT_HEAD_DIM // 4
MEM_HEADS = 4
MEM_HEAD_DIM = D_MODEL // MEM_HEADS
D_FF = 2816
CONV_WIDTH = 3
NORM_EPS = 1e-6
IN_SPLITS = (HG_KW, HG_KW, HG_KW, HG_VW, HG_VW, ATT_QW, ATT_KVW, ATT_KVW, D_MODEL, D_MODEL)
IN_COLS = sum(IN_SPLITS)
SPLIT_IDX = [int(c) for c in np.cumsum(IN_SPLITS)[:-1]]


def rms_norm(x, g):
    xf = x.astype(jnp.float32)
    y = xf * lax.rsqrt(jnp.mean(xf * xf, axis=-1, keepdims=True) + NORM_EPS) * g.astype(jnp.float32)
    return y.astype(x.dtype)

def partial_rotary(t, positions):
    half = ROT_DIM // 2
    inv_freq = 1.0 / (ROPE_THETA ** (jnp.arange(0, ROT_DIM, 2, dtype=jnp.float32) / ROT_DIM))
    ang = positions.astype(jnp.float32)[..., None] * inv_freq
    cos, sin = jnp.cos(ang)[:, :, None, :], jnp.sin(ang)[:, :, None, :]
    tf = t.astype(jnp.float32)
    t1, t2 = tf[..., :half], tf[..., half:ROT_DIM]
    out = jnp.concatenate([t1 * cos - t2 * sin, t2 * cos + t1 * sin, tf[..., ROT_DIM:]], axis=-1)
    return out.astype(t.dtype)

def gla_chunkwise(q, k, log_f, v):
    B, S, H, K = q.shape
    V = v.shape[-1]
    n_chunks = S // HG_CHUNK

    def chunks(t):
        return t.reshape(B, n_chunks, HG_CHUNK, H, t.shape[-1]).transpose(1, 0, 3, 2, 4)

    incl = jnp.tril(jnp.ones((HG_CHUNK, HG_CHUNK), dtype=bool))[:, :, None]

    def step(state, inp):
        qc, kc, gc, vc = inp
        b = jnp.cumsum(gc, axis=2)
        o_inter = jnp.einsum('bhtk,bhkv->bhtv', qc * jnp.exp(b), state)
        decay = jnp.exp(jnp.where(incl, b[:, :, :, None, :] - b[:, :, None, :, :], -jnp.inf))
        scores = jnp.einsum('bhtk,bhtsk->bhts', qc, decay * kc[:, :, None, :, :])
        o_intra = jnp.einsum('bhts,bhsv->bhtv', scores, vc)
        b_end = b[:, :, -1, :]
        new_state = (jnp.exp(b_end)[..., None] * state
                     + jnp.einsum('bhsk,bhsv->bhkv', kc * jnp.exp(b_end[:, :, None, :] - b), vc))
        return new_state, o_inter + o_intra

    state0 = jnp.zeros((B, H, K, V), jnp.float32)
    _, o = lax.scan(step, state0, (chunks(q), chunks(k), chunks(log_f), chunks(v)))
    return o.transpose(1, 0, 3, 2, 4).reshape(B, S, H, V)

def window_gqa_sink(q, k, v, sink):
    B, S = q.shape[0], q.shape[1]
    nb = S // ATT_BLOCK
    qb = q.reshape(B, nb, ATT_BLOCK, ATT_KV_HEADS, ATT_GROUP, ATT_HEAD_DIM)

    def band(t):
        tp = jnp.pad(t.reshape(B, nb, ATT_BLOCK, ATT_KV_HEADS, ATT_HEAD_DIM),
                     ((0, 0), (1, 1), (0, 0), (0, 0), (0, 0)))
        return jnp.concatenate([tp[:, :-2], tp[:, 1:-1], tp[:, 2:]], axis=2)

    kb, vb = band(k), band(v)
    s = jnp.einsum('bnqhgd,bnkhd->bnhgqk', qb, kb).astype(jnp.float32) * (ATT_HEAD_DIM ** -0.5)
    blk = jnp.arange(nb)[:, None, None]
    qi = blk * ATT_BLOCK + jnp.arange(ATT_BLOCK)[None, :, None]
    kj = (blk - 1) * ATT_BLOCK + jnp.arange(3 * ATT_BLOCK)[None, None, :]
    valid = (jnp.abs(qi - kj) <= WINDOW) & (kj >= 0) & (kj < S)
    s = jnp.where(valid[None, :, None, None], s, -jnp.inf)
    sk = sink.astype(jnp.float32).reshape(ATT_KV_HEADS, ATT_GROUP)[None, None, :, :, None, None]
    m = jnp.maximum(jnp.max(s, axis=-1, keepdims=True), sk)
    p = jnp.exp(s - m)
    p = p / (jnp.sum(p, axis=-1, keepdims=True) + jnp.exp(sk - m))
    o = jnp.einsum('bnhgqk,bnkhd->bnqhgd', p.astype(v.dtype), vb)
    return o.reshape(B, S, ATT_QW)

def token_mixers(n, positions, w_in, lb_fwd, lb_bwd, hg_norm, sink, w_br_rec, w_br_att, w_out):
    B, S, _ = n.shape
    f32 = jnp.float32
    proj = n @ w_in
    q_r, fz_f, fz_b, i_r, g_r, q_a, k_a, v_a, gate_r, gate_a = jnp.split(proj, SPLIT_IDX, axis=-1)

    qh = jax.nn.silu(q_r.astype(f32)).reshape(B, S, HG_HEADS, HG_KEY_DIM) * (HG_KEY_DIM ** -0.5)
    vh = i_r.astype(f32).reshape(B, S, HG_HEADS, HG_VAL_DIM)

    def forget(z, lb):
        f = lb + (1.0 - lb) * jax.nn.sigmoid(z.astype(f32))
        return ((1.0 - f).reshape(B, S, HG_HEADS, HG_KEY_DIM),
                jnp.log(f).reshape(B, S, HG_HEADS, HG_KEY_DIM))

    k_f, lf_f = forget(fz_f, lb_fwd)
    k_b, lf_b = forget(fz_b, lb_bwd)
    o_f = gla_chunkwise(qh, k_f, lf_f, vh)
    o_b = gla_chunkwise(qh[:, ::-1], k_b[:, ::-1], lf_b[:, ::-1], vh[:, ::-1])[:, ::-1]
    o = o_f + o_b
    o = (o * lax.rsqrt(jnp.mean(o * o, axis=-1, keepdims=True) + NORM_EPS)
         * hg_norm.astype(f32).reshape(HG_HEADS, HG_VAL_DIM))
    o = o.reshape(B, S, HG_VW) * jax.nn.silu(g_r.astype(f32))
    y_rec = o.astype(n.dtype) @ w_br_rec

    qa = partial_rotary(q_a.reshape(B, S, ATT_Q_HEADS, ATT_HEAD_DIM), positions)
    ka = partial_rotary(k_a.reshape(B, S, ATT_KV_HEADS, ATT_HEAD_DIM), positions)
    va = v_a.reshape(B, S, ATT_KV_HEADS, ATT_HEAD_DIM)
    y_att = window_gqa_sink(qa, ka, va, sink) @ w_br_att

    merged = jax.nn.sigmoid(gate_r) * y_rec + jax.nn.sigmoid(gate_a) * y_att
    return merged @ w_out

def memory_cross_attention(n, mem_n, w_q, w_kv, w_o):
    B, S, _ = n.shape
    M = mem_n.shape[1]
    q = (n @ w_q).reshape(B, S, MEM_HEADS, MEM_HEAD_DIM)
    k, v = jnp.split(mem_n @ w_kv, 2, axis=-1)
    k = k.reshape(B, M, MEM_HEADS, MEM_HEAD_DIM)
    v = v.reshape(B, M, MEM_HEADS, MEM_HEAD_DIM)
    s = jnp.einsum('bshd,bmhd->bhsm', q, k).astype(jnp.float32) * (MEM_HEAD_DIM ** -0.5)
    p = jax.nn.softmax(s, axis=-1).astype(v.dtype)
    o = jnp.einsum('bhsm,bmhd->bshd', p, v).reshape(B, S, D_MODEL)
    return o @ w_o

def conv_ffn(n, w_up, conv_w, conv_b, w_down):
    S = n.shape[1]
    u, g = jnp.split(n @ w_up, 2, axis=-1)
    pad = CONV_WIDTH // 2
    gp = jnp.pad(g, ((0, 0), (pad, pad), (0, 0)))
    gc = sum(gp[:, j:j + S] * conv_w[j] for j in range(CONV_WIDTH)) + conv_b
    return (jax.nn.silu(gc) * u) @ w_down

def first_inputs(seed: int = 0) -> dict:
    key = jax.random.key(seed)
    ks = jax.random.split(key, 24)

    def nrm(k, shape, scale):
        return jax.random.normal(k, shape, jnp.float32) * scale

    def gain(k, shape):
        return 1.0 + 0.02 * jax.random.normal(k, shape, jnp.float32)

    L, D = DEPTH, D_MODEL
    return {
        'x': nrm(ks[0], (BATCH, SEQ, D), 1.0),
        'mem': nrm(ks[1], (BATCH, MEM_LEN, D), 1.0),
        'positions': jnp.broadcast_to(jnp.arange(SEQ, dtype=jnp.int32), (BATCH, SEQ)),
        'norm_mix': gain(ks[2], (L, D)),
        'w_in': nrm(ks[3], (L, D, IN_COLS), D ** -0.5),
        'lower_bounds': nrm(ks[4], (2, L + 1, HG_KW), 0.5),
        'hg_norm': gain(ks[5], (L, HG_VW)),
        'attn_sink': nrm(ks[6], (L, ATT_Q_HEADS), 0.5),
        'w_br_rec': nrm(ks[7], (L, HG_VW, D), HG_VW ** -0.5),
        'w_br_att': nrm(ks[8], (L, ATT_QW, D), ATT_QW ** -0.5),
        'w_mix_out': nrm(ks[9], (L, D, D), D ** -0.5),
        'norm_mem': gain(ks[10], (L, D)),
        'norm_mem_kv': gain(ks[11], (L, D)),
        'w_mem_q': nrm(ks[12], (L, D, D), D ** -0.5),
        'w_mem_kv': nrm(ks[13], (L, D, 2 * D), D ** -0.5),
        'w_mem_o': nrm(ks[14], (L, D, D), D ** -0.5),
        'norm_ffn': gain(ks[15], (L, D)),
        'w_up': nrm(ks[16], (L, D, 2 * D_FF), D ** -0.5),
        'conv_w': nrm(ks[17], (L, CONV_WIDTH, D_FF), CONV_WIDTH ** -0.5),
        'conv_b': nrm(ks[18], (L, D_FF), 0.01),
        'w_down': nrm(ks[19], (L, D_FF, D), D_FF ** -0.5),
        'final_norm': gain(ks[20], (D,)),
    }

def first_block(x, mem, positions, norm_mix, w_in, lower_bounds, hg_norm, attn_sink, w_br_rec,
              w_br_att, w_mix_out, norm_mem, norm_mem_kv, w_mem_q, w_mem_kv, w_mem_o, norm_ffn,
              w_up, conv_w, conv_b, w_down, final_norm):
    lb_table = jnp.cumsum(jax.nn.softmax(lower_bounds.astype(jnp.float32), axis=1), axis=1)
    h = x
    for l in range(DEPTH):
        n = rms_norm(h, norm_mix[l])
        h = h + token_mixers(n, positions, w_in[l], lb_table[0, l], lb_table[1, l], hg_norm[l],
                             attn_sink[l], w_br_rec[l], w_br_att[l], w_mix_out[l])
        n = rms_norm(h, norm_mem[l])
        mem_n = rms_norm(mem, norm_mem_kv[l])
        h = h + memory_cross_attention(n, mem_n, w_mem_q[l], w_mem_kv[l], w_mem_o[l])
        n = rms_norm(h, norm_ffn[l])
        h = h + conv_ffn(n, w_up[l], conv_w[l], conv_b[l], w_down[l])
    return rms_norm(h, final_norm)


CHUNK = 64
Q_BLOCK = 128
EPS = 1e-6
MLA_HEADS = 8
MLA_NOPE = 64
MLA_ROPE = 32
MLA_V = 64
MLA_Q_RANK = 384
MLA_KV_RANK = 256
ROPE_BASE = 10000.0
MLA_WIDTH = MLA_HEADS * MLA_V
DSA_HEADS = 8
DSA_HEAD_DIM = 64
DSA_WIDTH = DSA_HEADS * DSA_HEAD_DIM
IDX_HEADS = 8
IDX_DIM = 32
TOPK_MAX = 256
REL_BUCKETS = 32
REL_MAX_DIST = 128

IN_SPLITS_2 = (MLA_Q_RANK, MLA_KV_RANK, MLA_ROPE, MLA_WIDTH,
             DSA_WIDTH, DSA_WIDTH, DSA_WIDTH, DSA_WIDTH,
             IDX_HEADS * IDX_DIM, IDX_DIM, IDX_HEADS,
             D_MODEL, D_MODEL)
IN_TOTAL = sum(IN_SPLITS_2)


def rmsnorm(x, g):
    xf = x.astype(jnp.float32)
    y = xf * lax.rsqrt(jnp.mean(xf * xf, axis=-1, keepdims=True) + EPS)
    return (y * g.astype(jnp.float32)).astype(x.dtype)

def rope(x, pos):
    half = x.shape[-1] // 2
    freqs = ROPE_BASE ** (-jnp.arange(half, dtype=jnp.float32) / half)
    ang = pos.astype(jnp.float32)[:, None] * freqs[None, :]
    cos = jnp.cos(ang)[None, :, None, :].astype(x.dtype)
    sin = jnp.sin(ang)[None, :, None, :].astype(x.dtype)
    x1, x2 = x[..., :half], x[..., half:]
    return jnp.concatenate([x1 * cos - x2 * sin, x1 * sin + x2 * cos], axis=-1)

def t5_bucket(rel):
    nb = REL_BUCKETS // 2
    max_exact = nb // 2
    ret = (rel > 0).astype(jnp.int32) * nb
    n = jnp.abs(rel)
    nf = jnp.maximum(n, 1).astype(jnp.float32)
    large = max_exact + (jnp.log(nf / max_exact) / np.log(REL_MAX_DIST / max_exact)
                         * (nb - max_exact)).astype(jnp.int32)
    large = jnp.minimum(large, nb - 1)
    return ret + jnp.where(n < max_exact, n, large)

def to_blocks(a):
    return jnp.moveaxis(a.reshape((a.shape[0], -1, Q_BLOCK) + a.shape[2:]), 1, 0)

def from_blocks(a):
    a = jnp.moveaxis(a, 0, 1)
    return a.reshape((a.shape[0], -1) + a.shape[3:])

def mla_attention(q_nope, q_pe, k_nope, k_pe, v, pos):
    scale = (MLA_NOPE + MLA_ROPE) ** -0.5
    key_chunk = pos // CHUNK

    def block(args):
        qn, qp, qpos = args
        logits = (jnp.einsum('bqhd,bkhd->bhqk', qn, k_nope)
                  + jnp.einsum('bqhr,bkr->bhqk', qp, k_pe))
        logits = logits.astype(jnp.float32) * scale
        mask = key_chunk[None, :] <= (qpos // CHUNK)[:, None]
        logits = jnp.where(mask[None, None], logits, -jnp.inf)
        p = jax.nn.softmax(logits, axis=-1).astype(v.dtype)
        return jnp.einsum('bhqk,bkhd->bqhd', p, v)

    out = lax.map(block, (to_blocks(q_nope), to_blocks(q_pe), pos.reshape(-1, Q_BLOCK)))
    return from_blocks(out)

def dsa_attention(q, k, v, q_idx, k_idx, w_idx, rel_bias, pos, topk):
    scale = DSA_HEAD_DIM ** -0.5
    key_chunk = pos // CHUNK
    gather = jax.vmap(lambda src, ids: src[ids])

    def block(args):
        qb, qi, wi, qpos = args
        qchunk = qpos // CHUNK
        s = jnp.einsum('bqhd,bkd->bqhk', qi, k_idx).astype(jnp.float32) * (IDX_DIM ** -0.5)
        score = jnp.einsum('bqhk,bqh->bqk', jax.nn.relu(s),
                           wi.astype(jnp.float32) * (IDX_HEADS ** -0.5))
        admissible = key_chunk[None, :] <= qchunk[:, None]
        score = jnp.where(admissible[None], score, -jnp.inf)
        _, idx = lax.top_k(score, topk)
        valid = (idx // CHUNK) <= qchunk[None, :, None]
        k_sel = gather(k, idx)
        v_sel = gather(v, idx)
        logits = jnp.einsum('bqhd,bqkhd->bhqk', qb, k_sel).astype(jnp.float32) * scale
        bias = rel_bias[t5_bucket(idx - qpos[None, :, None])]
        logits = logits + jnp.transpose(bias, (0, 3, 1, 2)).astype(jnp.float32)
        logits = jnp.where(valid[:, None], logits, -jnp.inf)
        p = jax.nn.softmax(logits, axis=-1).astype(v.dtype)
        return jnp.einsum('bhqk,bqkhd->bqhd', p, v_sel)

    out = lax.map(block, (to_blocks(q), to_blocks(q_idx), to_blocks(w_idx),
                          pos.reshape(-1, Q_BLOCK)))
    return from_blocks(out)

def second_inputs(seed: int = 0) -> dict:
    key = jax.random.key(seed)
    ks = jax.random.split(key, 13)

    def dense(k, shape):
        return jax.random.normal(k, shape, jnp.float32) * shape[-2] ** -0.5

    def gain(k, shape):
        return 1.0 + 0.05 * jax.random.normal(k, shape, jnp.float32)

    return {
        'x': jax.random.normal(ks[0], (BATCH, SEQ, D_MODEL), jnp.float32),
        'norm_g': gain(ks[1], (DEPTH, D_MODEL)),
        'w_in': dense(ks[2], (DEPTH, D_MODEL, IN_TOTAL)),
        'g_q_lat': gain(ks[3], (DEPTH, MLA_Q_RANK)),
        'w_uq': dense(ks[4], (DEPTH, MLA_Q_RANK, MLA_HEADS * (MLA_NOPE + MLA_ROPE))),
        'g_kv_lat': gain(ks[5], (DEPTH, MLA_KV_RANK)),
        'w_ukv': dense(ks[6], (DEPTH, MLA_KV_RANK, MLA_HEADS * (MLA_NOPE + MLA_V))),
        'w_o_a': dense(ks[7], (DEPTH, MLA_WIDTH, D_MODEL)),
        'w_o_b': dense(ks[8], (DEPTH, DSA_WIDTH, D_MODEL)),
        'w_out': dense(ks[9], (DEPTH, D_MODEL, D_MODEL)),
        'rel_bias': 0.5 * jax.random.normal(ks[10], (REL_BUCKETS, DSA_HEADS), jnp.float32),
        'final_g': gain(ks[11], (D_MODEL,)),
    }

def second_block(x, norm_g, w_in, g_q_lat, w_uq, g_kv_lat, w_ukv, w_o_a, w_o_b, w_out,
              rel_bias, final_g):
    B, S, _ = x.shape
    pos = jnp.arange(S, dtype=jnp.int32)
    topk = min(TOPK_MAX, S // 4)
    cuts = np.cumsum(IN_SPLITS_2)[:-1].tolist()
    for l in range(DEPTH):
        h = rmsnorm(x, norm_g[l])
        (q_lat, c_kv, k_rope, z_a, q_b, k_b, v_b, z_b,
         q_idx, k_idx, w_idx, gate_a, gate_b) = jnp.split(h @ w_in[l], cuts, axis=-1)

        q = (rmsnorm(q_lat, g_q_lat[l]) @ w_uq[l]).reshape(B, S, MLA_HEADS, MLA_NOPE + MLA_ROPE)
        q_nope, q_pe = q[..., :MLA_NOPE], rope(q[..., MLA_NOPE:], pos)
        kv = (rmsnorm(c_kv, g_kv_lat[l]) @ w_ukv[l]).reshape(B, S, MLA_HEADS, MLA_NOPE + MLA_V)
        k_nope, v_a = kv[..., :MLA_NOPE], kv[..., MLA_NOPE:]
        k_pe = rope(k_rope[:, :, None, :], pos)[:, :, 0, :]
        y_a = mla_attention(q_nope, q_pe, k_nope, k_pe, v_a, pos).reshape(B, S, MLA_WIDTH)
        y_a = y_a * jax.nn.silu(z_a)

        y_b = dsa_attention(q_b.reshape(B, S, DSA_HEADS, DSA_HEAD_DIM),
                            k_b.reshape(B, S, DSA_HEADS, DSA_HEAD_DIM),
                            v_b.reshape(B, S, DSA_HEADS, DSA_HEAD_DIM),
                            q_idx.reshape(B, S, IDX_HEADS, IDX_DIM), k_idx, w_idx,
                            rel_bias, pos, topk).reshape(B, S, DSA_WIDTH)
        y_b = y_b * jax.nn.silu(z_b)

        merged = (jax.nn.sigmoid(gate_a) * (y_a @ w_o_a[l])
                  + jax.nn.sigmoid(gate_b) * (y_b @ w_o_b[l]))
        x = x + merged @ w_out[l]
    return rmsnorm(x, final_g)


def setup_inputs(seed=0):
    out = dict(first_inputs(seed))
    for name, value in second_inputs(seed + 1).items():
        if name != "x":
            out[name + "_2"] = value
    return out


def reference(
    x, mem, positions, norm_mix, w_in, lower_bounds, hg_norm, attn_sink, w_br_rec, w_br_att,
    w_mix_out, norm_mem, norm_mem_kv, w_mem_q, w_mem_kv, w_mem_o, norm_ffn, w_up, conv_w,
    conv_b, w_down, final_norm, norm_g_2, w_in_2, g_q_lat_2, w_uq_2, g_kv_lat_2, w_ukv_2,
    w_o_a_2, w_o_b_2, w_out_2, rel_bias_2, final_g_2,
):
    x = first_block(
        x, mem, positions, norm_mix, w_in, lower_bounds, hg_norm, attn_sink, w_br_rec, w_br_att,
        w_mix_out, norm_mem, norm_mem_kv, w_mem_q, w_mem_kv, w_mem_o, norm_ffn, w_up, conv_w,
        conv_b, w_down, final_norm,
    )
    return second_block(
        x, norm_g_2, w_in_2, g_q_lat_2, w_uq_2, g_kv_lat_2, w_ukv_2, w_o_a_2, w_o_b_2, w_out_2,
        rel_bias_2, final_g_2,
    )


_drawn_inputs = setup_inputs


def setup_inputs(seed=0):
    import zlib

    import numpy as np

    out = dict(_drawn_inputs(seed))
    spreads = {}
    factors = {'norm_mix': 4.625,
     'lower_bounds': 3.299,
     'hg_norm': 6.87,
     'attn_sink': 8.0,
     'norm_mem': 8.0,
     'norm_mem_kv': 8.0,
     'norm_ffn': 3.68,
     'conv_b': 8.0,
     'final_norm': 2.766,
     'norm_g_2': 4.432,
     'g_q_lat_2': 8.0,
     'g_kv_lat_2': 8.0}
    for name, (base, spread) in spreads.items():
        noise = np.random.default_rng([zlib.crc32(name.encode()), seed]).standard_normal(out[name].shape)
        drawn = base * np.exp(spread * noise) if base else spread * noise
        out[name] = __import__('jax').numpy.asarray(drawn.astype(out[name].dtype))
    for name, factor in factors.items():
        out[name] = (out[name] * factor).astype(out[name].dtype)
    return out
```

```python
from contextlib import ExitStack

import numpy as np

import concourse.bass as bass
from concourse import mybir

F32, F32R, I32 = mybir.dt.float32, mybir.dt.float32r, mybir.dt.int32
ACT = mybir.ActivationFunctionType
ALU = mybir.AluOpType
AX = mybir.AxisListType

P = 128
S = 512
ST = S // P
D = 1024
DC = D // P
MEM = 256
EPS = 1e-6
NEG = -1e30
TAKEN = -3e38
LOWEST = -3.4e38

HG_HEADS = 4
HG_SCALE = 128 ** -0.5
LEVELS = 7
HALF = P // 2
LQ = LEVELS * HALF
UNITS = ST + 1
LN_FLOOR = 1e-19

ATT_SCALE = 64 ** -0.5
ROT_HALF = 8
ROPE_THETA = 500000.0
MEM_HEADS = 4
MEM_SCALE = 256 ** -0.5
FF = 2816
FC = FF // P

MLA_SCALE = 96 ** -0.5
IDX_HEADS = 8
IDX_SCALE = 32 ** -0.5
IDXW_SCALE = IDX_HEADS ** -0.5
TOPK = 128
REL_BUCKETS = 32
REL_MAX = 128
TOEP = 640

BLK = 8
RAW = 4
SPL = 2

TWO_PI = 2 * np.pi
PI_A = 6.28125
PI_B = int((TWO_PI - PI_A) * 2 ** 20) / 2 ** 20
PI_C = TWO_PI - PI_A - PI_B
ROUND = 12582912.0

STREAM = [
    ("q_r", [1] * 4), ("fz", [1] * 8), ("i_r", [1] * 4), ("g_r", [1] * 4),
    ("q_a", [1] * 4), ("k_a", [1]), ("v_a", [1]),
    ("gates", [1, 1, 1, 0] * DC), ("mix_out", [1] * DC),
    ("mem_k", [1] * DC), ("mem_v", [1] * DC), ("mem_q", [1] * DC), ("mem_o", [1] * DC),
    ("up", [1] * (2 * FC)), ("down", [3] * DC),
    ("q_idx", [1] * 2), ("k_idx", [1]), ("w_idx", [1]), ("q_lat", [1] * 3), ("c_kv", [1] * 2),
    ("k_rope", [1]), ("uq", [1, 0] * 3), ("ukv_k", [1, 0] * 2), ("ukv_v", [1, 0] * 2), ("z_a", [1] * 4),
    ("q_b", [1] * 4), ("k_b", [1] * 4), ("v_b", [1] * 4), ("z_b", [1] * 4),
    ("gates2", [1, 1, 1, 0] * DC), ("out2", [1] * DC),
]
FIRST, ENDS = {}, []
_slots = 0
for _name, _need in STREAM:
    FIRST[_name] = len(ENDS)
    for _k in _need:
        _slots += _k
        ENDS.append(_slots)
SLOTS = -(-_slots // RAW) * RAW


def running(table):
    at, n = {}, 0
    for name, count in table:
        at[name] = n
        n += count
    return at, n


SPLIT, _ = running([("mix", DC), ("rec", 4), ("att", 4), ("merged", DC), ("memory", DC), ("mem", DC),
                    ("mem_out", DC), ("ffn", DC), ("hidden", FC), ("mix2", DC), ("q_lat", 3),
                    ("c_kv", 2), ("y_a", 4), ("y_b", 4), ("merged2", DC)])
NORMS = ["mix", "memory", "mem", "ffn", "final", "mix2", "q_lat", "c_kv", "out"]
SQUARE, _ = running([(n, {"q_lat": 3, "c_kv": 2}.get(n, DC)) for n in NORMS])
SILU, _ = running([("q_r", 4), ("g_r", 4), ("z_a", 4), ("z_b", 4)])
ROTATE, _ = running([("first", 5), ("second", 3)])

def band(i):
    return max(0, i - 1), min(ST, i + 2)


def causal(i):
    return 0, i + 1


KINDS = {
    "window": dict(heads=[0, 4, 1, 5, 2, 6, 3, 7], keys=band, per_round=8, banks=1, out="att"),
    "memory": dict(heads=list(range(MEM_HEADS)), keys=lambda i: (0, 2), per_round=4, banks=2, out="mem_out"),
    "mla": dict(heads=list(range(8)), keys=causal, per_round=8, banks=1, out="y_a"),
    "dsa": dict(heads=list(range(8)), keys=causal, per_round=8, banks=1, out="y_b"),
}
_u = 0
for _k in KINDS.values():
    _k["units"] = [(h, i) for h in _k["heads"] for i in range(ST)]
    _k["first"] = _u
    _u += len(_k["units"])
NORM_LAG, TURN_LAG, PV_LAG, OUT_LAG = 1, 2, 3, 4

VEC, VEC_COLS = running([
    ("norm_mix", 8), ("norm_mem", 8), ("norm_mem_kv", 8), ("norm_ffn", 8), ("final_norm", 8),
    ("norm_g_2", 8), ("final_g_2", 8), ("g_q_lat_2", 3), ("g_kv_lat_2", 2), ("hg_norm", 4),
    ("conv_w", 3 * FC), ("conv_b", FC), ("lower", 16), ("inv_freq", 1)])
CONST_A = [("Qf", LQ), ("Qb", LQ), ("Kf", LQ), ("Kb", LQ), ("Pf", P), ("Uf", P), ("Pb", P), ("Ub", P),
           ("level", 8 * P), ("perm", P), ("band", 3 * P)]
CONST_D = [("perm", P), ("cos", S), ("sin", S), ("causal", S), ("onehot", TOEP)]
AT_A, COLS_A = running(CONST_A)
AT_D, COLS_D = running(CONST_D)


def build(nc, stream, xT, memT, pos, vecs, ident_d, const_a, const_d, sink_d, relb_d, gvec, outT):
    with ExitStack() as ctx:
        def sem(name):
            return ctx.enter_context(nc.semaphore(name))

        top = [1152]

        def place(name, shape, dt=F32, at=None):
            size = 4 * int(np.prod(shape[1:]))
            off = -(-top[0] // 32) * 32 if at is None else at
            assert off + size <= 229344, (name, off + size)
            if at is None:
                top[0] = off + size
            return nc.alloc_sbuf_tensor_at(name, shape, dt, offset=off)

        hT = place("hT", [P, DC, S])
        nH = place("nH", [P, DC, S], F32R)
        nL = place("nL", [P, DC, S], F32R)
        ring = place("ring", [P, RAW, BLK * P])
        wH = place("wH", [P, SPL, BLK * P], F32R)
        wL = place("wL", [P, SPL, BLK * P], F32R)
        ident = place("ident", [P, P])
        ones = place("ones", [P, P])
        vec = place("vec", [P, VEC_COLS])
        sq = place("sq", [P, 2, S])
        std = place("std", [P, S])
        rstd = place("rstd", [P, S])
        nt = place("nt", [P, 2, S])
        sgb = place("sgb", [P, 2, S])
        stat = place("stat", [P, 4, 8])
        lbs = place("lbs", [P, 64])
        sinks = place("sinks", [P, 8])
        tick = place("tick", [P, 2])
        OVER = top[0]

        cA = place("cA", [P, COLS_A])
        mix0 = top[0]
        qT = place("qT", [P, HG_HEADS, S])
        kk = place("kk", [P, 2, HG_HEADS, S])
        vr = place("vr", [P, ST, S])
        recH = place("recH", [P, 4, S], F32R)
        recL = place("recL", [P, 4, S], F32R)
        gla0 = top[0]
        lf = place("lf", [P, 2, S])
        lft = place("lft", [P, 2, ST, P])
        E = place("E", [P, 2, 4, S])
        X = place("X", [P, 2, 2, LEVELS * P])
        Sg = place("Sg", [P, ST, S])
        kfb = place("kfb", [P, S])
        lev = place("lev", [P, 8, P])
        top[0] = gla0
        attH = place("attH", [P, 4, S], F32R)
        attL = place("attL", [P, 4, S], F32R)
        qa = place("qa", [P, 4, S])
        ka = place("ka", [P, S])
        va = place("va", [P, ST, P])
        cosA = place("cosA", [P, S])
        sinA = place("sinA", [P, S])
        posi = place("posi", [P, S], I32)
        ang = place("ang", [P, S])
        turn = place("turn", [P, S])
        wx = place("wx", [P, 4, S])
        wPT = place("wPT", [P, 2, S])
        assert top[0] <= 229344
        gate0 = gla0 + 2 * 4 * S * 4
        sgA = place("sgA", [P, 2, 2, S], at=gate0)
        mtA = place("mtA", [P, 2, 2, S], at=gate0 + 16 * S)
        mgH = place("mgH", [P, DC, S], F32R, at=mix0)
        mgL = place("mgL", [P, DC, S], F32R, at=mix0 + 4 * DC * S)

        top[0] = OVER
        memx = place("memx", [P, DC, MEM])
        mnH = place("mnH", [P, DC, MEM], F32R)
        mnL = place("mnL", [P, DC, MEM], F32R)
        mk = place("mk", [P, DC, MEM])
        mv = place("mv", [P, 2, D])
        mq = place("mq", [P, DC, S])
        moH = place("moH", [P, DC, S], F32R)
        moL = place("moL", [P, DC, S], F32R)
        mx = place("mx", [P, 4, S])
        mPT = place("mPT", [P, 2, S])
        nomask = place("nomask", [P, MEM])

        top[0] = OVER
        aH = place("aH", [P, FC, S], F32R)
        aL = place("aL", [P, FC, S], F32R)
        gpad = place("gpad", [P, 2, S + 2])
        cv = place("cv", [P, 2, S])
        fu = place("fu", [P, 2, S])

        top[0] = OVER
        cD = place("cD", [P, COLS_D])
        selm = place("selm", [P, 9 * P])
        wtok = place("wtok", [P, ST, IDX_HEADS])
        gv = place("gv", [8, TOEP])
        relb = place("relb", [REL_BUCKETS, 8])
        best = place("best", [P, 8])
        yaH = place("yaH", [P, 4, S], F32R)
        yaL = place("yaL", [P, 4, S], F32R)
        dx = place("dx", [P, 4, S])
        dPT = place("dPT", [P, 2, S])
        rl = place("rl", [P, 2, S])
        d0 = top[0]
        qi = place("qi", [P, 2, S])
        ki = place("ki", [P, S])
        qlat = place("qlat", [P, 3, S])
        ckv = place("ckv", [P, 2, S])
        qlH = place("qlH", [P, 3, S], F32R)
        qlL = place("qlL", [P, 3, S], F32R)
        ckH = place("ckH", [P, 2, S], F32R)
        ckL = place("ckL", [P, 2, S], F32R)
        kp = place("kp", [P, S])
        qn = place("qn", [P, 4, S])
        qp = place("qp", [P, 2, S])
        kn = place("kn", [P, 4, S])
        vA = place("vA", [P, ST, S])
        za = place("za", [P, 4, S])
        top[0] = d0
        qb = place("qb", [P, 4, S])
        kb = place("kb", [P, 4, S])
        vB = place("vB", [P, ST, S])
        zb = place("zb", [P, 4, S])
        toep = place("toep", [P, 8, S])
        ybH = place("ybH", [P, 4, S], F32R)
        ybL = place("ybL", [P, 4, S], F32R)
        mg2H = place("mg2H", [P, DC, S], F32R, at=d0)
        mg2L = place("mg2L", [P, DC, S], F32R, at=d0 + 4 * DC * S)
        sgD = place("sgD", [P, 2, 2, S], at=d0 + 8 * DC * S)
        mtD = place("mtD", [P, 2, 2, S], at=d0 + 8 * DC * S + 16 * S)

        pair = [ctx.enter_context(nc.psum_tensor(f"pair{i}", [P, 2 * S], F32)) for i in range(4)]

        def bank(b):
            return pair[b // 2][:, S * (b % 2):S * (b % 2) + S]

        def vcol(name, c):
            i = VEC[name] + c
            return vec[:, i:i + 1]

        def c_a(name, a, b):
            return cA[:, AT_A[name] + a:AT_A[name] + b]

        def c_d(name, a, b):
            return cD[:, AT_D[name] + a:AT_D[name] + b]

        landed = [sem(f"landed{i}") for i in range(RAW)]
        high_done = sem("high_done")
        split_done = sem("split_done")
        multiplied = sem("multiplied")
        freed = [sem("freed0"), sem("freed1")]
        phase = sem("phase")
        ld_x, ld_vec, ld_a, ld_pos, ld_mem, ld_d, ld_toep, st_gvec, st_out = (
            sem(n) for n in ("ld_x", "ld_vec", "ld_a", "ld_pos", "ld_mem", "ld_d", "ld_toep", "st_gvec", "st_out"))
        ones_set, borders, angle_s, angle_c, tables, lb_diff, lb_exp = (
            sem(n) for n in ("ones_set", "borders", "angle_s", "angle_c", "tables", "lb_diff", "lb_exp"))
        dve_own = sem("dve_own")
        sq_made, sq_used, std_made, r_made = (sem(n) for n in ("sq_made", "sq_used", "std_made", "r_made"))
        nt_made, nh_made, nl_made = sem("nt_made"), sem("nh_made"), sem("nl_made")
        sg_made = sem("sg_made")
        x1_made, y_made = sem("x1_made"), sem("y_made")
        rot_done, rot_used, rotated = sem("rot_done"), sem("rot_used"), sem("rotated")
        f_made, lf_made, lf_turned, lft_made = (sem(n) for n in ("f_made", "lf_made", "lf_turned", "lft_made"))
        dec_done, exp_done, x_made, k_made = (sem(n) for n in ("dec_done", "exp_done", "x_made", "k_made"))
        sc_done, masked, s_made = sem("sc_done"), sem("masked"), sem("s_made")
        cross_done, cross_out, o_done, o_out = (sem(n) for n in ("cross_done", "cross_out", "o_done", "o_out"))
        o_sq, o_sum, o_std, o_norm = (sem(n) for n in ("o_sq", "o_sum", "o_std", "o_norm"))
        conv_made, fsg_made = sem("conv_made"), sem("fsg_made")
        a_sc, a_max, a_neg, a_exp, a_prob, a_turn, a_pt, a_pv = (
            sem("a_" + n) for n in ("sc", "max", "neg", "exp", "prob", "turn", "pt", "pv"))
        t_sc, t_relu, t_acc = sem("t_sc"), sem("t_relu"), sem("t_acc")
        gv_done, gv_out = sem("gv_done"), sem("gv_out")

        def out_of_bank(eng, g):
            eng.wait_ge(freed[g % 2], g // 2 + 1)

        block = ctx.enter_context(nc.Block())

        @block.sync
        def _(sp):
            for c in range(0, DC, 2):
                sp.dma_start(hT[:, c:c + 2, :], xT[:, c:c + 2, :]).then_inc(ld_x, 16)
            slots = stream.rearrange("(n r) p m -> n r p m", r=RAW)
            for r in range(RAW):
                sp.dma_start(ring[:, r, :], slots[0, r]).then_inc(landed[r], 16)
            with sp.Fori(0, SLOTS // RAW - 1) as n:
                for r in range(RAW):
                    sp.wait_ge(split_done, RAW * n + r + 1)
                    sp.dma_start(ring[:, r, :], slots[n + 1, r]).then_inc(landed[r], 16)

        @block.gpsimd
        def _(pool):
            pool.memset(ones[:, :], 1.0).then_inc(ones_set, 1)
            pool.memset(tick[:, :], 0.0).then_inc(ones_set, 1)
            pool.wait_ge(ones_set, 2)

            def split(r, turn_, n, used):
                pool.wait_ge(landed[r], 16 * turn_)
                if used is not None:
                    pool.wait_ge(multiplied, used)
                pool.tensor_tensor(tick[:, 1:2], tick[:, 0:1], tick[:, 0:1], ALU.add).then_inc(high_done, 1)
                pool.tensor_scalar(wH[:, r % SPL, :], ring[:, r, :], 1.0, 0.0, ALU.mult, ALU.add).then_inc(high_done, 1)
                pool.wait_ge(high_done, 2 * n)
                pool.tensor_tensor(wL[:, r % SPL, :], ring[:, r, :], wH[:, r % SPL, :].bitcast(F32),
                                   ALU.subtract).then_inc(split_done, 1)

            for r in range(RAW):
                split(r, 1, r + 1, r - SPL + 1 if r >= SPL else None)
            with pool.Fori(1, SLOTS // RAW) as n:
                for r in range(RAW):
                    split(r, n + 1, RAW * n + r + 1, RAW * n + r - SPL + 1)

        @block.tensor
        def _(pe):
            mm = nc.tensor.matmul
            n_slot, n_phase = [0], [0]

            def barrier():
                n_phase[0] += 1
                pe.drain().then_inc(phase, 1)
                pe.wait_ge(phase, 3 * n_phase[0])

            def norm_sums(name, chunks, width):
                if NORMS.index(name):
                    pe.wait_ge(std_made, NORMS.index(name))
                for c in range(chunks):
                    q = SQUARE[name] + c
                    pe.wait_ge(sq_made, q + 1)
                    mm(bank(7)[:, :width], ones[:, :], sq[:, q % 2, :width],
                       start=c == 0, stop=c == chunks - 1).then_inc(sq_used, 1)

            def open_slot():
                r = n_slot[0] % SPL
                n_slot[0] += 1
                pe.wait_ge(split_done, n_slot[0])
                return r

            def open_bank(g):
                if g >= 2:
                    out_of_bank(pe, g - 2)
                return bank(g % 2)

            def three(out, a, b, first, last):
                mm(out, a[0], b[0], start=first, stop=False)
                mm(out, a[0], b[1], start=False, stop=False)
                return mm(out, a[1], b[0], start=False, stop=last)

            def weight(r, j):
                return wH[:, r, P * j:P * j + P], wL[:, r, P * j:P * j + P]

            def parts(h, l, n):
                return [(h[:, k, :], l[:, k, :]) for k in range(n)]

            def project(stage, c0, n, xs, width=S, inputs=None):
                for c in range(c0, c0 + n):
                    out = open_bank(FIRST[stage] + c)[:, :width]
                    for k, x in enumerate(xs):
                        if k % BLK == 0:
                            r = open_slot()
                        if inputs is not None and c == c0:
                            pe.wait_ge(nl_made, SPLIT[inputs] + k + 1)
                        last = three(out, weight(r, k % BLK), x, k == 0, k == len(xs) - 1)
                        if k % BLK == BLK - 1 or k == len(xs) - 1:
                            last.then_inc(multiplied, 1)

            def project_tokens(stage, n, h, l, tiles):
                for c in range(n):
                    out = open_bank(FIRST[stage] + c)
                    r = open_slot()
                    for t in range(tiles):
                        ts = slice(P * t, P * t + P)
                        for k in range(DC):
                            last = three(out[:, ts], (h[:, k, ts], l[:, k, ts]), weight(r, k), k == 0, k == DC - 1)
                    last.then_inc(multiplied, 1)

            def halves(stage, n_slots, k_n, xs):
                for s in range(n_slots):
                    g = FIRST[stage] + 2 * s
                    outs = [open_bank(g), open_bank(g + 1)]
                    r = open_slot()
                    for half in range(2):
                        for cols, terms in xs(r, half):
                            for k, (a, b) in enumerate(terms):
                                last = three(outs[half][:, cols], a, b, k == 0, k == len(terms) - 1)
                    last.then_inc(multiplied, 1)

            def rotate(name, n, src, raw, perm):
                m = ROTATE[name] + n
                out_of_bank(pe, raw)
                if m >= 2:
                    pe.wait_ge(rot_used, m - 1)
                mm(bank(2 + m % 2), perm, src, start=True, stop=True).then_inc(rot_done, 1)

            def recurrence():
                def tok(d, i):
                    return lft[:, d, i, :]

                def tri(name):
                    return c_a(name, 0, P)

                def cross_decays(h):
                    n = UNITS * h
                    pe.wait_ge(lft_made, 2 * (h + 1))
                    if n:
                        pe.wait_ge(exp_done, n)
                    for i in range(ST):
                        cs = slice(P * i, P * i + P)
                        d = 0 if i % 2 else 1
                        mm(bank(2)[:, cs], tok(d, i), tri("Pb" if d else "Pf"), start=True, stop=True)
                        mm(bank(3)[:, cs], tok(1 - d, i), tri("Uf" if d else "Ub"), start=True, stop=True)
                        d = 0 if i >= 2 else 1
                        far = {3: 2, 0: 1}.get(i)
                        for b, dd, name in ((4, d, "Pb" if d else "Pf"), (5, 1 - d, "Uf" if d else "Ub")):
                            last = mm(bank(b)[:, cs], tok(dd, i), tri(name), start=True, stop=far is None)
                            if far is not None:
                                last = mm(bank(b)[:, cs], tok(dd, far), ones[:, :], start=False, stop=True)
                    last.then_inc(dec_done, 1)

                def tile_decays(h, i):
                    pe.wait_ge(exp_done, UNITS * h + 1 + i)
                    for b, (d, name) in enumerate([(0, "Qf"), (1, "Qb"), (0, "Kf"), (1, "Kb")]):
                        last = mm(bank(2 + b)[:, :LQ], tok(d, i), c_a(name, 0, LQ), start=True, stop=True)
                    last.then_inc(dec_done, 1)

                def tile_scores(h, i):
                    n = ST * h + i
                    pe.wait_ge(x_made, UNITS * h + 2 + i)
                    if n:
                        pe.wait_ge(masked, n)
                    for l in range(LEVELS):
                        cs = slice(P * l, P * l + P)
                        mm(pair[3][:, cs], X[:, n % 2, 1, cs], X[:, n % 2, 0, cs], start=True, stop=True)
                    cs = slice(P * i, P * i + P)
                    if i == 0:
                        pe.wait_ge(k_made, h + 1)
                    mm(pair[3][:, P * LEVELS:], kfb[:, cs], qT[:, h, cs], start=True, stop=True).then_inc(sc_done, 1)

                def cross_scores(h):
                    b = (UNITS * h) % 2
                    pe.wait_ge(x_made, UNITS * h + 1)
                    for j in range(ST):
                        if j >= 2:
                            pe.wait_ge(cross_out, ST * h + j - 1)
                        out, cs, t = bank(j % 2), slice(P * j, P * j + P), j ^ 1
                        ts = slice(P * t, P * t + P)
                        mm(out[:, ts], E[:, b, 1, cs], E[:, b, 0, ts], start=True, stop=True)
                        far = slice(2 * P, 4 * P) if j < 2 else slice(0, 2 * P)
                        mm(out[:, far], E[:, b, 3, cs], E[:, b, 2, far], start=True, stop=True).then_inc(cross_done, 1)

                for h in range(HG_HEADS):
                    pe.wait_ge(lf_made, h + 1)
                    if h:
                        pe.wait_ge(o_out, h)
                    else:
                        for g in (FIRST["g_r"] - 2, FIRST["g_r"] - 1):
                            out_of_bank(pe, g)
                    for d in range(2):
                        for i in range(ST):
                            cs = slice(P * i, P * i + P)
                            last = nc.tensor.transpose(bank(d)[:, cs], lf[:, d, cs], ident[:, :])
                        last.then_inc(lf_turned, 1)
                    cross_decays(h)
                    tile_decays(h, 0)
                    cross_scores(h)
                    for i in range(1, ST):
                        tile_decays(h, i)
                        tile_scores(h, i - 1)
                    tile_scores(h, ST - 1)
                    pe.wait_ge(cross_out, ST * (h + 1))
                    pe.wait_ge(s_made, ST * (h + 1))
                    for j in range(ST):
                        last = mm(bank(0), vr[:, j, P * h:P * h + P], Sg[:, j, :], start=j == 0, stop=j == ST - 1)
                    last.then_inc(o_done, 1)
                for h in range(HG_HEADS):
                    pe.wait_ge(o_sq, h + 1)
                    if h:
                        pe.wait_ge(o_std, h)
                    mm(bank(7), ones[:, :], sq[:, h % 2, :], start=True, stop=True).then_inc(o_sum, 1)

            def attention(name, terms, value, probs, turned):
                kind = KINDS[name]
                units, u0, n = kind["units"], kind["first"], len(kind["units"])
                per, banks, k0 = kind["per_round"], kind["banks"], SPLIT[kind["out"]]

                def scores(x):
                    (h, i), u = units[x], u0 + x
                    a, b = kind["keys"](i)
                    if x >= 2:
                        pe.wait_ge(a_max, u - 1)
                    pairs = terms(h, i, slice(P * a, P * b))
                    for t, (w, m) in enumerate(pairs):
                        last = mm(bank(2 + u % 2)[:, :P * (b - a)], w, m, start=t == 0, stop=t == len(pairs) - 1)
                    last.then_inc(a_sc, 1)

                def turn_probs(x):
                    (h, i), u = units[x], u0 + x
                    a, b = kind["keys"](i)
                    pe.wait_ge(a_prob, u + 1)
                    if x >= 2:
                        pe.wait_ge(a_pt, u - 1)
                    for t in range(b - a):
                        cs = slice(P * t, P * t + P)
                        last = nc.tensor.transpose(bank(4 + u % 2)[:, cs], probs[:, u % 4, cs], ident[:, :])
                    last.then_inc(a_turn, 1)

                def weigh(x):
                    (h, i), u = units[x], u0 + x
                    a, b = kind["keys"](i)
                    rnd = x // per
                    pe.wait_ge(a_pt, u + 1)
                    ahead = 2 if banks == 1 else 1
                    if x % per == 0 and rnd >= ahead:
                        pe.wait_ge(nt_made, k0 + banks * (rnd - ahead + 1))
                    for bk in range(banks):
                        out = bank(6 + (rnd % 2 if banks == 1 else bk))
                        for t in range(a, b):
                            w, rows = value(h, t, bk)
                            last = mm(out[rows, P * i:P * i + P], w, turned[:, u % 2, P * (t - a):P * (t - a) + P],
                                      start=t == a, stop=t == b - 1)
                    last.then_inc(a_pv, 1)

                for x in range(n + PV_LAG):
                    if x < n:
                        scores(x)
                    if 0 <= x - TURN_LAG < n:
                        turn_probs(x - TURN_LAG)
                    if 0 <= x - PV_LAG < n:
                        weigh(x - PV_LAG)

            def gated(stage, branches):
                for c in range(DC):
                    project(stage, 4 * c, 2, n_parts)
                    g = FIRST[stage] + 4 * c + 2
                    outs = [open_bank(g), open_bank(g + 1)]
                    r = open_slot()
                    for half in range(2):
                        for k in range(4):
                            last = three(outs[half], weight(r, 4 * half + k), branches[half][k], k == 0, k == 3)
                    last.then_inc(multiplied, 1)

            def head_rows(h):
                return slice(64 * (h % 2), 64 * (h % 2) + 64)

            n_parts = parts(nH, nL, DC)

            pe.wait_ge(ones_set, 2)
            norm_sums("mix", DC, S)
            project("q_r", 0, 4, n_parts, inputs="mix")
            project("fz", 0, 8, n_parts)
            project_tokens("i_r", 4, nH, nL, ST)
            pe.wait_ge(ld_a, 48)
            recurrence()
            pe.wait_ge(o_out, HG_HEADS)
            project("g_r", 0, 4, n_parts)
            barrier()
            project("q_a", 0, 4, n_parts)
            project("k_a", 0, 1, n_parts)
            project_tokens("v_a", 1, nH, nL, ST)
            for c in range(4):
                rotate("first", c, qa[:, c, :], FIRST["q_a"] + c, c_a("perm", 0, P))
            rotate("first", 4, ka[:, :], FIRST["k_a"], c_a("perm", 0, P))
            barrier()

            def window_terms(h, i, keys):
                rows = slice(64 * (h // 4), 64 * (h // 4) + 64)
                return [(qa[rows, h % 4, P * i:P * i + P], ka[rows, keys])]

            def window_value(h, t, bk):
                rows = slice(64 * (h // 4), 64 * (h // 4) + 64)
                return va[:, t, rows], rows

            attention("window", window_terms, window_value, wx, wPT)
            barrier()
            gated("gates", (parts(recH, recL, 4), parts(attH, attL, 4)))
            project("mix_out", 0, DC, parts(mgH, mgL, DC), inputs="merged")
            barrier()

            norm_sums("memory", DC, MEM)
            norm_sums("mem", DC, S)
            project("mem_k", 0, DC, parts(mnH, mnL, DC), MEM, inputs="memory")
            project_tokens("mem_v", DC, mnH, mnL, 2)
            project("mem_q", 0, DC, n_parts, inputs="mem")
            barrier()

            def mem_terms(h, i, keys):
                return [(mq[:, 2 * h + b, P * i:P * i + P], mk[:, 2 * h + b, :]) for b in range(2)]

            def mem_value(h, t, bk):
                return mv[:, t, 256 * h + P * bk:256 * h + P * bk + P], slice(0, P)

            attention("memory", mem_terms, mem_value, mx, mPT)
            project("mem_o", 0, DC, parts(moH, moL, DC), inputs="mem_out")
            barrier()

            norm_sums("ffn", DC, S)
            project("up", 0, 2 * FC, n_parts, inputs="ffn")
            project("down", 0, DC, parts(aH, aL, FC), inputs="hidden")
            barrier()

            norm_sums("final", DC, S)
            norm_sums("mix2", DC, S)
            project("q_idx", 0, 2, n_parts, inputs="mix2")
            project("k_idx", 0, 1, n_parts)
            project_tokens("w_idx", 1, nH, nL, ST)
            pe.wait_ge(ld_d, 32)
            rows = slice(0, REL_BUCKETS)
            mm(bank(4)[0:8, :], relb[:, :], c_d("onehot", 0, S)[rows, :], start=True, stop=True)
            mm(bank(5)[0:8, :TOEP - S], relb[:, :], c_d("onehot", S, TOEP)[rows, :], start=True, stop=True).then_inc(gv_done, 1)
            project("q_lat", 0, 3, n_parts)
            project("c_kv", 0, 2, n_parts)
            project("k_rope", 0, 1, n_parts)
            n = 0
            for i in range(1, ST):
                for h in range(IDX_HEADS):
                    rows = slice(32 * (h % 4), 32 * (h % 4) + 32)
                    if n >= 2:
                        pe.wait_ge(t_relu, n - 1)
                    mm(bank(2 + n % 2)[:, :P * (i + 1)], qi[rows, h // 4, P * i:P * i + P], ki[rows, :P * (i + 1)],
                       start=True, stop=True).then_inc(t_sc, 1)
                    n += 1
            norm_sums("q_lat", 3, S)
            norm_sums("c_kv", 2, S)
            ql, ck = parts(qlH, qlL, 3), parts(ckH, ckL, 2)
            pe.wait_ge(nl_made, SPLIT["c_kv"] + 2)
            halves("uq", 3, 3, lambda r, half: [(slice(0, S), [(weight(r, 3 * half + k), ql[k]) for k in range(3)])])
            halves("ukv_k", 2, 2, lambda r, half: [(slice(0, S), [(weight(r, 2 * half + k), ck[k]) for k in range(2)])])

            def value_tiles(r, half):
                for t in range(ST):
                    ts = slice(P * t, P * t + P)
                    yield ts, [((ckH[:, k, ts], ckL[:, k, ts]), weight(r, 2 * half + k)) for k in range(2)]

            halves("ukv_v", 2, 2, value_tiles)
            project("z_a", 0, 4, n_parts)
            rotate("second", 0, kp[:, :], FIRST["k_rope"], c_d("perm", 0, P))
            for c in range(2):
                rotate("second", 1 + c, qp[:, c, :], FIRST["uq"] + 4 + c, c_d("perm", 0, P))
            barrier()

            def mla_terms(h, i, keys):
                qs, pe_rows = slice(P * i, P * i + P), slice(32 * (h % 4), 32 * (h % 4) + 32)
                return [(qn[head_rows(h), h // 2, qs], kn[head_rows(h), h // 2, keys]),
                        (qp[pe_rows, h // 4, qs], kp[pe_rows, keys])]

            attention("mla", mla_terms, lambda h, t, bk: (vA[:, t, 64 * h:64 * h + 64], head_rows(h)), dx, dPT)
            barrier()
            project("q_b", 0, 4, n_parts)
            project("k_b", 0, 4, n_parts)
            project_tokens("v_b", 4, nH, nL, ST)
            project("z_b", 0, 4, n_parts)
            barrier()

            def dsa_terms(h, i, keys):
                return [(qb[head_rows(h), h // 2, P * i:P * i + P], kb[head_rows(h), h // 2, keys])]

            attention("dsa", dsa_terms, lambda h, t, bk: (vB[:, t, 64 * h:64 * h + 64], head_rows(h)), dx, dPT)
            barrier()
            gated("gates2", (parts(yaH, yaL, 4), parts(ybH, ybL, 4)))
            project("out2", 0, DC, parts(mg2H, mg2L, DC), inputs="merged2")
            norm_sums("out", DC, S)

        @block.scalar
        def _(act):
            A = nc.scalar.activation
            n_phase = [0]

            def barrier():
                n_phase[0] += 1
                act.drain().then_inc(phase, 1)
                act.wait_ge(phase, 3 * n_phase[0])

            def product(stage, c):
                g = FIRST[stage] + c
                act.wait_ge(multiplied, ENDS[g])
                return bank(g % 2), freed[g % 2]

            def copy_out(stage, c, dst, cols=None, scale=1.0):
                b, free = product(stage, c)
                A(dst, b if cols is None else cols(b), ACT.Copy, scale=scale).then_inc(free, 1)

            def norm(name, x, chunks, width, features, ready):
                for c in range(chunks):
                    q = SQUARE[name] + c
                    ready(c)
                    if q >= 2:
                        act.wait_ge(sq_used, q - 1)
                    A(sq[:, q % 2, :width], x[:, c, :], ACT.Square).then_inc(sq_made, 1)
                act.wait_ge(sq_used, SQUARE[name] + chunks)
                if NORMS.index(name):
                    act.wait_ge(r_made, NORMS.index(name))
                A(std[:, :width], bank(7)[:, :width], ACT.Sqrt, scale=1.0 / features, bias=EPS).then_inc(std_made, 1)

            def high(name, c, dst, width=S):
                k = SPLIT[name] + c
                act.wait_ge(nt_made, k + 1)
                A(dst, nt[:, k % 2, :width], ACT.Copy).then_inc(nh_made, 1)

            def highs(name, dst, chunks, width=S):
                for c in range(chunks):
                    high(name, c, dst[:, c, :], width)

            def sigmoids(stage, n):
                for c in range(n):
                    b, _ = product(stage, c)
                    y = SILU[stage] + c
                    if c >= 2:
                        out_of_bank(act, FIRST[stage] + c - 2)
                    A(sgb[:, y % 2, :], b, ACT.Sigmoid).then_inc(sg_made, 1)

            def recurrence():
                def decays(n, width):
                    act.wait_ge(dec_done, n + 1)
                    if n >= 2:
                        act.wait_ge(x_made, n - 1)
                        if (n - 2) % UNITS == 0:
                            act.wait_ge(cross_done, ST * ((n - 2) // UNITS + 1))
                    for b in range(4):
                        last = A(E[:, n % 2, b, :width], bank(2 + b)[:, :width], ACT.Exp)
                    last.then_inc(exp_done, 1)

                for h in range(HG_HEADS):
                    act.wait_ge(f_made, h + 1)
                    A(lf[:, :, :], lf[:, :, :], ACT.Ln).then_inc(lf_made, 1)
                    act.wait_ge(lf_turned, 2 * h + 1)
                    if h:
                        act.wait_ge(dec_done, UNITS * h)
                    A(lft[:, 0, :, :], bank(0).rearrange("p (t k) -> p t k", k=P), ACT.Copy).then_inc(lft_made, 1)
                    decays(UNITS * h, S)
                    decays(UNITS * h + 1, LQ)
                    for j in range(ST):
                        act.wait_ge(cross_done, ST * h + j + 1)
                        if h and j == 0:
                            act.wait_ge(o_done, h)
                        for a, b in ((0, P * j), (P * j + P, S)):
                            if b > a:
                                last = A(Sg[:, j, a:b], bank(j % 2)[:, a:b], ACT.Copy)
                        last.then_inc(cross_out, 1)
                    for i in range(1, ST):
                        decays(UNITS * h + 1 + i, LQ)
                    act.wait_ge(o_done, h + 1)
                    A(qT[:, h, :], bank(0), ACT.Copy).then_inc(o_out, 1)
                for h in range(HG_HEADS):
                    act.wait_ge(o_out, h + 1)
                    if h >= 2:
                        act.wait_ge(o_sum, h - 1)
                    A(sq[:, h % 2, :], qT[:, h, :], ACT.Square).then_inc(o_sq, 1)
                    act.wait_ge(o_sum, h + 1)
                    A(E[:, 0, h, :], bank(7), ACT.Sqrt, scale=1.0 / P, bias=EPS).then_inc(o_std, 1)

            def attention(name, probs, turned, dst, sink=False):
                kind = KINDS[name]
                units, u0, n = kind["units"], kind["first"], len(kind["units"])
                per, banks = kind["per_round"], kind["banks"]

                for x in range(n + OUT_LAG + 2):
                    if x < n:
                        (h, i), u = units[x], u0 + x
                        a, b = kind["keys"](i)
                        st = stat[:, u % 4, :]
                        act.wait_ge(a_neg, u + 1)
                        if sink:
                            A(st[:, 3:4], sinks[:, h:h + 1], ACT.Exp, bias=st[:, 1:2])
                        px = probs[:, u % 4, :P * (b - a)]
                        A(px, px, ACT.Exp, bias=st[:, 1:2], accum_out=st[:, 2:3]).then_inc(a_exp, 1)
                    y = x - TURN_LAG
                    if 0 <= y < n:
                        (h, i), u = units[y], u0 + y
                        a, b = kind["keys"](i)
                        act.wait_ge(a_turn, u + 1)
                        if y >= 2:
                            act.wait_ge(a_pv, u - 1)
                        A(turned[:, u % 2, :P * (b - a)], bank(4 + u % 2)[:, :P * (b - a)], ACT.Copy).then_inc(a_pt, 1)
                    y = x - OUT_LAG - 1
                    if 0 <= y < n and y % per == per - 1:
                        for bk in range(banks):
                            c = (y // per) * banks + bk
                            high(kind["out"], c, dst[:, c, :])

            def gated(stage, sg, dst, name):
                for c in range(DC):
                    for b in range(2):
                        bk, free = product(stage, 4 * c + b)
                        if c >= 2:
                            out_of_bank(act, FIRST[stage] + 4 * (c - 2) + 2 + b)
                        A(sg[:, c % 2, b, :], bk, ACT.Sigmoid).then_inc(free, 1)
                    if c >= 1:
                        high(name, c - 1, dst[:, c - 1, :])
                high(name, DC - 1, dst[:, DC - 1, :])

            def residual(stage):
                return lambda c: out_of_bank(act, FIRST[stage] + c)

            act.dma_start(vec[:, :], vecs).then_inc(ld_vec, 16)
            act.dma_start(ident[:, :], ident_d).then_inc(ld_a, 16)
            act.dma_start(sinks[:, :], sink_d.partition_broadcast(P)).then_inc(ld_a, 16)
            act.dma_start(cA[:, :], const_a).then_inc(ld_a, 16)

            act.wait_ge(lb_diff, 1)
            A(lbs[:, 16:32], lbs[:, 16:32], ACT.Exp).then_inc(lb_exp, 1)
            norm("mix", hT, DC, S, D, lambda c: act.wait_ge(ld_x, 16 * DC // 2) if c == 0 else None)
            highs("mix", nH, DC)
            sigmoids("q_r", 4)
            for c in range(8):
                b, free = product("fz", c)
                A(kk[:, c // 4, c % 4, :], b, ACT.Sigmoid).then_inc(free, 1)
            for c in range(4):
                copy_out("i_r", c, vr[:, :, P * c:P * c + P], lambda b: b.rearrange("p (t k) -> p t k", k=P))
            recurrence()
            sigmoids("g_r", 4)
            highs("rec", recH, 4)
            barrier()
            act.dma_start(posi[:, :], pos.partition_broadcast(P)).then_inc(ld_pos, 16)
            for c in range(4):
                copy_out("q_a", c, qa[:, c, :])
            copy_out("k_a", 0, ka[:, :])
            copy_out("v_a", 0, va[:, :, :], lambda b: b.rearrange("p (t k) -> p t k", k=P))
            act.wait_ge(angle_s, 1)
            A(sinA[:, :], sinA[:, :], ACT.Sin).then_inc(tables, 1)
            act.wait_ge(angle_c, 1)
            A(cosA[:, :], cosA[:, :], ACT.Sin, bias=float(np.pi / 2)).then_inc(tables, 1)
            barrier()
            attention("window", wx, wPT, attH, sink=True)
            barrier()
            gated("gates", sgA, mgH, "merged")
            barrier()

            act.dma_start(memx[:, :, :], memT).then_inc(ld_mem, 16)
            norm("memory", memx, DC, MEM, D, lambda c: act.wait_ge(ld_mem, 16))
            norm("mem", hT, DC, S, D, lambda c: None)
            highs("memory", mnH, DC, MEM)
            highs("mem", nH, DC)
            for c in range(DC):
                copy_out("mem_k", c, mk[:, c, :], lambda b: b[:, :MEM])
            for c in range(DC):
                copy_out("mem_v", c, mv[:, :, P * c:P * c + P], lambda b: b[:, :MEM].rearrange("p (t k) -> p t k", k=P))
            for c in range(DC):
                copy_out("mem_q", c, mq[:, c, :])
            barrier()
            attention("memory", mx, mPT, moH)
            barrier()

            norm("ffn", hT, DC, S, D, lambda c: None)
            highs("ffn", nH, DC)
            act.wait_ge(borders, 2)
            for j in range(FC):
                if j >= 2:
                    act.wait_ge(conv_made, j - 1)
                copy_out("up", 2 * j, gpad[:, j % 2, 1:S + 1])
                act.wait_ge(conv_made, j + 1)
                if j >= 2:
                    out_of_bank(act, FIRST["up"] + 2 * (j - 2) + 1)
                A(sgb[:, j % 2, :], cv[:, j % 2, :], ACT.Sigmoid).then_inc(fsg_made, 1)
                if j >= 1:
                    high("hidden", j - 1, aH[:, j - 1, :])
            high("hidden", FC - 1, aH[:, FC - 1, :])
            barrier()

            act.dma_start(cD[:, :], const_d).then_inc(ld_d, 16)
            act.dma_start(relb[:, :], relb_d).then_inc(ld_d, 16)
            norm("final", hT, DC, S, D, lambda c: None)
            norm("mix2", hT, DC, S, D, lambda c: act.wait_ge(x1_made, c + 1))
            highs("mix2", nH, DC)
            for c in range(2):
                copy_out("q_idx", c, qi[:, c, :])
            copy_out("k_idx", 0, ki[:, :])
            copy_out("w_idx", 0, wtok[:, :, :],
                     lambda b: b.rearrange("p (t k) -> p t k", k=P)[:, :, :IDX_HEADS], IDXW_SCALE)
            act.wait_ge(gv_done, 1)
            A(gv[:, :S], bank(4)[0:8, :], ACT.Copy).then_inc(gv_out, 1)
            A(gv[:, S:], bank(5)[0:8, :TOEP - S], ACT.Copy).then_inc(gv_out, 1)
            act.wait_ge(gv_out, 2)
            act.dma_start(gvec, gv[:, None, :].broadcast_to([8, P, TOEP])).then_inc(st_gvec, 16)
            for c in range(3):
                copy_out("q_lat", c, qlat[:, c, :])
            for c in range(2):
                copy_out("c_kv", c, ckv[:, c, :])
            copy_out("k_rope", 0, kp[:, :])
            n = 0
            for i in range(1, ST):
                for h in range(IDX_HEADS):
                    act.wait_ge(t_sc, n + 1)
                    if n >= 2:
                        act.wait_ge(t_acc, n - 1)
                    A(rl[:, n % 2, :P * (i + 1)], bank(2 + n % 2)[:, :P * (i + 1)], ACT.Relu,
                      scale=IDX_SCALE).then_inc(t_relu, 1)
                    n += 1
            norm("q_lat", qlat, 3, S, 3 * P, lambda c: out_of_bank(act, FIRST["q_lat"] + c))
            norm("c_kv", ckv, 2, S, 2 * P, lambda c: out_of_bank(act, FIRST["c_kv"] + c))
            highs("q_lat", qlH, 3)
            highs("c_kv", ckH, 2)
            for c in range(6):
                copy_out("uq", c, qn[:, c, :] if c < 4 else qp[:, c - 4, :])
            for c in range(4):
                copy_out("ukv_k", c, kn[:, c, :])
            for c in range(4):
                copy_out("ukv_v", c, vA[:, :, P * c:P * c + P], lambda b: b.rearrange("p (t k) -> p t k", k=P))
            sigmoids("z_a", 4)
            barrier()
            attention("mla", dx, dPT, yaH)
            barrier()
            act.wait_ge(st_gvec, 16)
            for h in range(8):
                act.dma_start(toep[:, h, :], bass.AP(gvec.tensor, h * P * TOEP + P - 1, [[TOEP - 1, P], [1, S]])).then_inc(ld_toep, 16)
            for c in range(4):
                copy_out("q_b", c, qb[:, c, :])
            for c in range(4):
                copy_out("k_b", c, kb[:, c, :])
            for c in range(4):
                copy_out("v_b", c, vB[:, :, P * c:P * c + P], lambda b: b.rearrange("p (t k) -> p t k", k=P))
            sigmoids("z_b", 4)
            barrier()
            attention("dsa", dx, dPT, ybH)
            barrier()
            gated("gates2", sgD, mg2H, "merged2")
            norm("out", hT, DC, S, D, residual("out2"))
            for c in range(DC):
                act.wait_ge(y_made, c + 1)
                act.dma_start(outT[:, c, :], hT[:, c, :]).then_inc(st_out, 16)
            act.wait_ge(st_out, 16 * DC)

        @block.vector
        def _(dve):
            V = nc.vector
            n_phase, n_own = [0], [0]

            def barrier():
                n_phase[0] += 1
                dve.drain().then_inc(phase, 1)
                dve.wait_ge(phase, 3 * n_phase[0])

            def own(ins):
                n_own[0] += 1
                ins.then_inc(dve_own, 1)
                dve.wait_ge(dve_own, n_own[0])

            def product(stage, c):
                g = FIRST[stage] + c
                dve.wait_ge(multiplied, ENDS[g])
                return bank(g % 2), freed[g % 2]

            def open_split(name, c, width=S):
                k = SPLIT[name] + c
                if k >= 2:
                    dve.wait_ge(nl_made, k - 1)
                return nt[:, k % 2, :width]

            def low(name, c, hi, lo, width=S):
                k = SPLIT[name] + c
                dve.wait_ge(nh_made, k + 1)
                V.tensor_tensor(lo[:, c, :], nt[:, k % 2, :width], hi[:, c, :].bitcast(F32),
                                ALU.subtract).then_inc(nl_made, 1)

            def inverse(name, width):
                i = NORMS.index(name)
                dve.wait_ge(std_made, i + 1)
                V.reciprocal(rstd[:, :width], std[:, :width]).then_inc(r_made, 1)
                dve.wait_ge(r_made, i + 1)

            def normed(out, x, gain, c, width):
                return V.scalar_tensor_tensor(out=out, in0=x[:, c, :], scalar=vcol(gain, c), in1=rstd[:, :width],
                                              op0=ALU.mult, op1=ALU.mult)

            def norm(name, x, gain, chunks, width, hi, lo):
                inverse(name, width)
                for c in range(chunks):
                    normed(open_split(name, c, width), x, gain, c, width).then_inc(nt_made, 1)
                    if c:
                        low(name, c - 1, hi, lo, width)
                low(name, chunks - 1, hi, lo, width)

            def silu(stage, n, dst, scale=None):
                for c in range(n):
                    dve.wait_ge(sg_made, SILU[stage] + c + 1)
                    b, free = product(stage, c)
                    sg = sgb[:, (SILU[stage] + c) % 2, :]
                    if scale is None:
                        V.tensor_tensor(dst[:, c, :], b, sg, ALU.mult).then_inc(free, 1)
                    else:
                        V.scalar_tensor_tensor(out=dst[:, c, :], in0=b, scalar=scale, in1=sg,
                                               op0=ALU.mult, op1=ALU.mult).then_inc(free, 1)

            def rotate(name, n, x, cos, sin):
                m = ROTATE[name] + n
                dve.wait_ge(rot_done, m + 1)
                if m:
                    dve.wait_ge(rotated, m)
                V.tensor_tensor(sgb[:, m % 2, :], bank(2 + m % 2), sin, ALU.mult).then_inc(rot_used, 1)
                own(V.tensor_tensor(x, x, cos, ALU.mult))
                V.tensor_tensor(x, x, sgb[:, m % 2, :], ALU.add).then_inc(rotated, 1)

            def residual(stage):
                for c in range(DC):
                    b, free = product(stage, c)
                    V.tensor_tensor(hT[:, c, :], b, hT[:, c, :], ALU.add).then_inc(free, 1)

            def lower_bounds():
                dve.wait_ge(ld_vec, 16)
                a = vec[:, VEC["lower"]:VEC["lower"] + 16].rearrange("p (d l h) -> p d l h", d=2, l=2)
                m = lbs[:, 0:8].rearrange("p (d h) -> p d h", d=2)
                e = lbs[:, 16:32].rearrange("p (d l h) -> p d l h", d=2, l=2)
                own(V.tensor_tensor(m, a[:, :, 0, :], a[:, :, 1, :], ALU.max))
                own(V.tensor_tensor(e[:, :, 0, :], a[:, :, 0, :], m, ALU.subtract))
                V.tensor_tensor(e[:, :, 1, :], a[:, :, 1, :], m, ALU.subtract).then_inc(lb_diff, 1)
                dve.wait_ge(lb_exp, 1)
                own(V.tensor_tensor(m, e[:, :, 0, :], e[:, :, 1, :], ALU.add))
                own(V.reciprocal(m, m))
                own(V.tensor_tensor(lbs[:, 32:40].rearrange("p (d h) -> p d h", d=2), e[:, :, 0, :], m, ALU.mult))
                own(V.tensor_scalar(lbs[:, 40:48], lbs[:, 32:40], -1.0, 1.0, ALU.mult, ALU.add))
                own(V.tensor_scalar(lbs[:, 48:56], lbs[:, 32:40], 1.0, None, ALU.subtract))

            def lb(which, d, h):
                i = 32 + 8 * which + 4 * d + h
                return lbs[:, i:i + 1]

            def recurrence():
                def forget(h):
                    for d in range(2):
                        out_of_bank(dve, FIRST["fz"] + 4 * d + h)
                        own(V.tensor_scalar(lf[:, d, :], kk[:, d, h, :], lb(1, d, h), lb(0, d, h), ALU.mult, ALU.add))
                    V.tensor_scalar(lf[:, :, :], lf[:, :, :], LN_FLOOR, None, ALU.max).then_inc(f_made, 1)

                def keys(h):
                    for d in range(2):
                        own(V.tensor_scalar(kk[:, d, h, :], kk[:, d, h, :], lb(2, d, h), lb(1, d, h), ALU.mult, ALU.add))
                    if h:
                        dve.wait_ge(sc_done, ST * h)
                    V.tensor_tensor(kfb[:, :], kk[:, 0, h, :], kk[:, 1, h, :], ALU.add).then_inc(k_made, 1)

                def cross(h):
                    n = UNITS * h
                    dve.wait_ge(exp_done, n + 1)
                    e = E[:, n % 2, :, :]
                    V.tensor_tensor(e[:, 0, :], e[:, 0, :], qT[:, h, :], ALU.mult)
                    V.tensor_tensor(e[:, 2, :], e[:, 2, :], qT[:, h, :], ALU.mult)
                    for b, view in ((1, "p (a two k) -> p two a k"), (3, "p (two a k) -> p two a k")):
                        for d in range(2):
                            x = e[:, b, :].rearrange(view, two=2, k=P)[:, d]
                            last = V.tensor_tensor(x, x, kk[:, d, h, :].rearrange(view, two=2, k=P)[:, d], ALU.mult)
                    last.then_inc(x_made, 1)

                def tile(h, i):
                    n, m = UNITS * h + 1 + i, ST * h + i
                    dve.wait_ge(exp_done, n + 1)
                    if m >= 2:
                        dve.wait_ge(sc_done, m - 1)
                    cs = slice(P * i, P * i + P)
                    for l in range(LEVELS):
                        c = 1 << l

                        def two(x):
                            return x.rearrange("p (b two c) -> p two b c", two=2, c=c)

                        ls, xs = slice(HALF * l, HALF * l + HALF), slice(P * l, P * l + P)
                        for kind, half, b, src in ((0, 1, 0, qT[:, h, cs]), (0, 0, 1, qT[:, h, cs]),
                                                   (1, 0, 2, kk[:, 0, h, cs]), (1, 1, 3, kk[:, 1, h, cs])):
                            last = V.tensor_tensor(two(X[:, m % 2, kind, xs])[:, half],
                                                   E[:, n % 2, b, ls].rearrange("p (b c) -> p b c", c=c),
                                                   two(src)[:, half], ALU.mult)
                    last.then_inc(x_made, 1)

                def select(h, i):
                    m = ST * h + i
                    dve.wait_ge(sc_done, m + 1)
                    if m:
                        dve.wait_ge(s_made, m)
                    V.tensor_tensor(lev[:, :, :], pair[3][:, :].rearrange("p (l t) -> p l t", l=8),
                                    c_a("level", 0, 8 * P).rearrange("p (l t) -> p l t", l=8),
                                    ALU.mult).then_inc(masked, 1)
                    dve.wait_ge(masked, m + 1)
                    if h and i == 0:
                        dve.wait_ge(o_done, h)
                    V.tensor_reduce(Sg[:, i, P * i:P * i + P], lev[:, :, :].rearrange("p l t -> p t l"),
                                    AX.X, ALU.add).then_inc(s_made, 1)

                for h in range(HG_HEADS):
                    if h == 0:
                        forget(0)
                    dve.wait_ge(lf_turned, 2 * h + 2)
                    V.tensor_copy(lft[:, 1, :, :], bank(1).rearrange("p (t k) -> p t k", k=P)).then_inc(lft_made, 1)
                    keys(h)
                    cross(h)
                    for i in range(ST):
                        tile(h, i)
                        if i:
                            select(h, i - 1)
                        if i == 2 and h + 1 < HG_HEADS:
                            forget(h + 1)
                    select(h, ST - 1)
                for h in range(HG_HEADS):
                    dve.wait_ge(o_std, h + 1)
                    own(V.reciprocal(E[:, 0, h, :], E[:, 0, h, :]))
                    V.scalar_tensor_tensor(out=qT[:, h, :], in0=qT[:, h, :], scalar=vcol("hg_norm", h), in1=E[:, 0, h, :],
                                           op0=ALU.mult, op1=ALU.mult).then_inc(o_norm, 1)

            def rotary_angles():
                dve.wait_ge(ld_pos, 16)
                own(V.tensor_copy(ang[:, :], posi[:, :]))
                own(V.tensor_scalar(ang[:, :], ang[:, :], vcol("inv_freq", 0), None, ALU.mult))
                pi = float(np.float32(3.1415925))
                for out, shift, lo, hi, done in ((sinA, 0.0, -pi, pi, angle_s),
                                                 (cosA, 0.25, -1.5 * np.pi + 1e-6, 0.5 * np.pi - 1e-6, angle_c)):
                    own(V.tensor_scalar(turn[:, :], ang[:, :], 1.0 / TWO_PI, shift, ALU.mult, ALU.add))
                    own(V.tensor_scalar(turn[:, :], turn[:, :], ROUND, None, ALU.add))
                    own(V.tensor_scalar(turn[:, :], turn[:, :], ROUND, None, ALU.subtract))
                    src = ang
                    for part in (PI_A, PI_B, PI_C):
                        own(V.scalar_tensor_tensor(out=out[:, :], in0=turn[:, :], scalar=-part, in1=src[:, :],
                                                   op0=ALU.mult, op1=ALU.add))
                        src = out
                    V.tensor_scalar(out[:, :], out[:, :], lo, hi, ALU.max, ALU.min).then_inc(done, 1)

            def attention(name, x_buf, scale, mask, hi, lo, bias=None, sink=False, gate=None):
                kind = KINDS[name]
                units, u0, n = kind["units"], kind["first"], len(kind["units"])
                per, banks = kind["per_round"], kind["banks"]

                def row_max(x):
                    (h, i), u = units[x], u0 + x
                    a, b = kind["keys"](i)
                    w, st = P * (b - a), stat[:, u % 4, :]
                    dve.wait_ge(a_sc, u + 1)
                    if x >= 4:
                        dve.wait_ge(a_turn, u - 3)
                    sx, src, by = x_buf[:, u % 4, :w], bank(2 + u % 2)[:, :w], scale
                    if bias is not None:
                        own(V.scalar_tensor_tensor(out=sx, in0=src, scalar=scale, in1=bias(h, i),
                                                   op0=ALU.mult, op1=ALU.add))
                        src, by = sx, 1.0
                    V.tensor_tensor_reduce(out=sx, in0=src, in1=mask(i), scale=by, scalar=LOWEST, op0=ALU.add,
                                           op1=ALU.max, accum_out=st[:, 0:1]).then_inc(a_max, 1)
                    dve.wait_ge(a_max, u + 1)
                    if sink:
                        V.tensor_scalar(st[:, 1:2], st[:, 0:1], sinks[:, h:h + 1], -1.0, ALU.max, ALU.mult).then_inc(a_neg, 1)
                    else:
                        V.tensor_scalar(st[:, 1:2], st[:, 0:1], -1.0, None, ALU.mult).then_inc(a_neg, 1)

                def normalise(x):
                    (h, i), u = units[x], u0 + x
                    a, b = kind["keys"](i)
                    px, st = x_buf[:, u % 4, :P * (b - a)], stat[:, u % 4, :]
                    dve.wait_ge(a_exp, u + 1)
                    total = st[:, 2:3]
                    if sink:
                        own(V.tensor_tensor(st[:, 4:5], st[:, 2:3], st[:, 3:4], ALU.add))
                        total = st[:, 4:5]
                    own(V.reciprocal(st[:, 5:6], total))
                    V.tensor_scalar(px, px, st[:, 5:6], None, ALU.mult).then_inc(a_prob, 1)

                for x in range(n + OUT_LAG + 3):
                    if x < n:
                        row_max(x)
                    if 0 <= x - NORM_LAG < n:
                        normalise(x - NORM_LAG)
                    y = x - OUT_LAG
                    if 0 <= y < n and y % per == per - 1:
                        rnd = y // per
                        for bk in range(banks):
                            c = rnd * banks + bk
                            out = open_split(kind["out"], c)
                            dve.wait_ge(a_pv, u0 + y + 1)
                            src = bank(6 + (rnd % 2 if banks == 1 else bk))
                            if gate is None:
                                V.tensor_copy(out, src).then_inc(nt_made, 1)
                            else:
                                V.tensor_tensor(out, src, gate[:, c, :], ALU.mult).then_inc(nt_made, 1)
                    y = x - OUT_LAG - 2
                    if 0 <= y < n and y % per == per - 1:
                        for bk in range(banks):
                            low(kind["out"], (y // per) * banks + bk, hi, lo)

            def gated(stage, sg, mt, name, hi, lo):
                for c in range(DC):
                    g = FIRST[stage] + 4 * c
                    out = open_split(name, c)
                    for b in range(2):
                        out_of_bank(dve, g + b)
                        src, free = product(stage, 4 * c + 2 + b)
                        V.tensor_tensor(mt[:, c % 2, b, :], src, sg[:, c % 2, b, :], ALU.mult).then_inc(free, 1)
                    out_of_bank(dve, g + 2)
                    out_of_bank(dve, g + 3)
                    V.tensor_tensor(out, mt[:, c % 2, 0, :], mt[:, c % 2, 1, :], ALU.add).then_inc(nt_made, 1)
                    if c:
                        low(name, c - 1, hi, lo)
                low(name, DC - 1, hi, lo)

            lower_bounds()
            norm("mix", hT, "norm_mix", DC, S, nH, nL)
            silu("q_r", 4, qT, HG_SCALE)
            dve.wait_ge(ld_a, 48)
            out_of_bank(dve, FIRST["q_r"] + 3)
            recurrence()
            for c in range(4):
                y, g = SILU["g_r"] + c, FIRST["g_r"] + c
                dve.wait_ge(sg_made, y + 1)
                b, free = product("g_r", c)
                out = open_split("rec", c)
                V.tensor_tensor(X[:, c % 2, 0, :S], b, sgb[:, y % 2, :], ALU.mult).then_inc(free, 1)
                out_of_bank(dve, g)
                dve.wait_ge(o_norm, c + 1)
                V.tensor_tensor(out, X[:, c % 2, 0, :S], qT[:, c, :], ALU.mult).then_inc(nt_made, 1)
                if c:
                    low("rec", c - 1, recH, recL)
            low("rec", 3, recH, recL)
            barrier()
            rotary_angles()
            dve.wait_ge(tables, 2)
            for c in range(4):
                rotate("first", c, qa[:, c, :], cosA[:, :], sinA[:, :])
            rotate("first", 4, ka[:, :], cosA[:, :], sinA[:, :])
            barrier()

            def band_mask(i):
                a, b = band(i)
                return c_a("band", P * (a - i + 1), P * (b - i + 1))

            attention("window", wx, ATT_SCALE, band_mask, attH, attL, sink=True)
            barrier()
            gated("gates", sgA, mtA, "merged", mgH, mgL)
            residual("mix_out")
            barrier()

            own(V.memset(nomask[:, :], 0.0))
            norm("memory", memx, "norm_mem_kv", DC, MEM, mnH, mnL)
            norm("mem", hT, "norm_mem", DC, S, nH, nL)
            barrier()
            attention("memory", mx, MEM_SCALE, lambda i: nomask[:, :], moH, moL)
            residual("mem_o")
            barrier()

            for c in (0, S + 1):
                V.memset(gpad[:, :, c:c + 1], 0.0).then_inc(borders, 1)
            dve.wait_ge(borders, 2)
            norm("ffn", hT, "norm_ffn", DC, S, nH, nL)
            for j in range(FC):
                w = [vcol("conv_w", 3 * j + t) for t in range(3)]
                x, y = gpad[:, j % 2, :], cv[:, j % 2, :]
                out_of_bank(dve, FIRST["up"] + 2 * j)
                own(V.tensor_scalar(y, x[:, 1:S + 1], w[1], vcol("conv_b", j), ALU.mult, ALU.add))
                own(V.scalar_tensor_tensor(out=y, in0=x[:, 0:S], scalar=w[0], in1=y, op0=ALU.mult, op1=ALU.add))
                V.scalar_tensor_tensor(out=y, in0=x[:, 2:S + 2], scalar=w[2], in1=y,
                                       op0=ALU.mult, op1=ALU.add).then_inc(conv_made, 1)
                dve.wait_ge(fsg_made, j + 1)
                out = open_split("hidden", j)
                b, free = product("up", 2 * j + 1)
                V.tensor_tensor(fu[:, j % 2, :], b, sgb[:, j % 2, :], ALU.mult).then_inc(free, 1)
                out_of_bank(dve, FIRST["up"] + 2 * j + 1)
                V.tensor_tensor(out, fu[:, j % 2, :], y, ALU.mult).then_inc(nt_made, 1)
                if j:
                    low("hidden", j - 1, aH, aL)
            low("hidden", FC - 1, aH, aL)
            residual("down")
            barrier()

            inverse("final", S)
            for c in range(DC):
                normed(hT[:, c, :], hT, "final_norm", c, S).then_inc(x1_made, 1)
            norm("mix2", hT, "norm_g_2", DC, S, nH, nL)
            dve.wait_ge(ld_d, 32)
            out_of_bank(dve, FIRST["w_idx"])
            n = 0
            for i in range(1, ST):
                w, acc = P * (i + 1), dx[:, i, :P * (i + 1)]
                for h in range(IDX_HEADS):
                    dve.wait_ge(t_relu, n + 1)
                    if h:
                        dve.wait_ge(t_acc, n)
                    V.scalar_tensor_tensor(out=acc, in0=rl[:, n % 2, :w], scalar=wtok[:, i, h:h + 1],
                                           in1=acc if h else c_d("causal", S - w, S),
                                           op0=ALU.mult, op1=ALU.add).then_inc(t_acc, 1)
                    n += 1
            norm("q_lat", qlat, "g_q_lat_2", 3, S, qlH, qlL)
            norm("c_kv", ckv, "g_kv_lat_2", 2, S, ckH, ckL)
            dve.wait_ge(t_acc, n)
            for i in range(1, ST):
                w, acc, at = P * (i + 1), dx[:, i, :P * (i + 1)], {1: 0, 2: 2 * P, 3: 5 * P}[i]
                for _r in range(TOPK // 8):
                    own(V.max(best[:, :], acc))
                    own(V.match_replace(acc, best[:, :], acc, TAKEN))
                own(V.tensor_scalar(selm[:, at:at + w], acc, 0.9 * TAKEN, NEG, ALU.is_gt, ALU.mult))
            silu("z_a", 4, za)
            for c in (2, 3):
                out_of_bank(dve, FIRST["z_a"] + c)
            rotate("second", 0, kp[:, :], c_d("cos", 0, S), c_d("sin", 0, S))
            for c in range(2):
                rotate("second", 1 + c, qp[:, c, :], c_d("cos", 0, S), c_d("sin", 0, S))
            barrier()

            def causal_mask(i):
                return c_d("causal", S - P * (i + 1), S)

            attention("mla", dx, MLA_SCALE, causal_mask, yaH, yaL, gate=za)
            barrier()
            silu("z_b", 4, zb)
            dve.wait_ge(ld_toep, 16 * 8)
            barrier()

            def top_mask(i):
                if i == 0:
                    return causal_mask(0)
                at = {1: 0, 2: 2 * P, 3: 5 * P}[i]
                return selm[:, at:at + P * (i + 1)]

            attention("dsa", dx, ATT_SCALE, top_mask, ybH, ybL, gate=zb,
                      bias=lambda h, i: toep[:, h, S - P * (i + 1):])
            barrier()
            gated("gates2", sgD, mtD, "merged2", mg2H, mg2L)
            residual("out2")
            inverse("out", S)
            for c in range(DC):
                normed(hT[:, c, :], hT, "final_g_2", c, S).then_inc(y_made, 1)


def level_constants():
    out = {n: np.zeros((P, LQ), np.float32) for n in ("Qf", "Qb", "Kf", "Kb")}
    masks = np.zeros((P, 8, P), np.float32)
    u = np.arange(P)
    for l in range(LEVELS):
        c = 1 << l
        for b in range(HALF // c):
            mid = 2 * c * b + c
            for j in range(c):
                col, late, early = l * HALF + b * c + j, mid + j, mid - c + j
                out["Qf"][:, col] = (u >= mid) & (u <= late)
                out["Qb"][:, col] = (u >= early) & (u < mid)
                out["Kf"][:, col] = (u > early) & (u < mid)
                out["Kb"][:, col] = (u >= mid) & (u < late)
            lo, hi = slice(mid - c, mid), slice(mid, mid + c)
            masks[lo, l, hi] = 1.0
            masks[hi, l, lo] = 1.0
    masks[:, LEVELS, :] = np.eye(P)
    s, t = u[:, None], u[None, :]
    out["Pf"], out["Uf"] = s <= t, s > t
    out["Pb"], out["Ub"] = s >= t, s < t
    out["level"] = masks.reshape(P, -1)
    return out


def rotary_partners(group, half):
    m = np.zeros((P, P), np.float32)
    for g in range(0, P, group):
        for r in range(half):
            m[g + half + r, g + r] = -1.0
            m[g + r, g + half + r] = 1.0
    return m


def constants_a():
    c = level_constants()
    c["perm"] = rotary_partners(64, ROT_HALF)
    q, k = np.arange(P)[:, None], np.arange(3 * P)[None, :] - P
    c["band"] = np.where(np.abs(q - k) <= 128, 0.0, NEG)
    return np.concatenate([np.asarray(c[n], np.float32) for n, _ in CONST_A], 1)


def constants_d():
    c = {"perm": rotary_partners(32, 16)}
    freqs = np.float32(10000.0) ** (-np.arange(16, dtype=np.float32) / np.float32(16))
    angle = np.arange(S, dtype=np.float32)[None, :] * freqs[np.arange(P) % 16][:, None]
    c["cos"], c["sin"] = np.cos(angle), np.sin(angle)
    q, k = np.arange(P)[:, None], np.arange(S)[None, :] - (S - P)
    c["causal"] = np.where((k < 0) | (k // 64 <= q // 64), 0.0, NEG)
    rel = np.arange(TOEP) - (S - 1)
    nb, exact = REL_BUCKETS // 2, REL_BUCKETS // 4
    n = np.abs(rel)
    far = np.log(np.maximum(n, 1).astype(np.float32) / np.float32(exact)) / np.log(REL_MAX / exact) * (nb - exact)
    far = np.minimum(exact + far.astype(np.float32).astype(np.int32), nb - 1)
    bucket = (rel > 0) * nb + np.where(n < exact, n, far)
    onehot = np.zeros((P, TOEP), np.float32)
    onehot[bucket, np.arange(TOEP)] = 1.0
    c["onehot"] = onehot
    return np.concatenate([np.asarray(c[n], np.float32) for n, _ in CONST_D], 1)


def blocks(w, pad_to=None):
    k, n = w.shape
    x = w.reshape(k // P, P, n // P, P).transpose(2, 1, 0, 3).reshape(n // P, P, k)
    if pad_to is not None:
        x = np.concatenate([x, np.zeros((n // P, P, pad_to - k), w.dtype)], 2)
    return x


def wide(w):
    return np.concatenate([w, np.zeros((w.shape[0], P - w.shape[1]), w.dtype)], 1)


def weight_stream(a):
    SLOT = BLK * P

    def per_slot(x, count):
        n, p, k = x.shape
        x = x.reshape(n // count, count, p, k).transpose(0, 2, 1, 3).reshape(n // count, p, count * k)
        return np.concatenate([x, np.zeros((n // count, p, SLOT - count * k), x.dtype)], 2)

    def gates(wa, wb, w1, w2):
        ga, gb, y1, y2 = blocks(wa), blocks(wb), blocks(w1), blocks(w2)
        return np.stack([ga, gb, np.concatenate([y1, y2], 2)], 1).reshape(-1, P, SLOT)

    w = a["w_in"][0]
    cuts = np.cumsum([512] * 6 + [128, 128, 1024])
    q_r, fz_f, fz_b, i_r, g_r, q_a, k_a, v_a, gate_r, gate_a = np.split(w, cuts, 1)
    q_a = q_a.reshape(D, 2, 4, 64).transpose(0, 2, 1, 3).reshape(D, 512)
    br_att = a["w_br_att"][0].reshape(2, 4, 64, D).transpose(1, 0, 2, 3).reshape(512, D)
    mem_k, mem_v = np.split(a["w_mem_kv"][0], 2, 1)
    up, gate = (blocks(x) for x in np.split(a["w_up"][0], 2, 1))
    w2 = a["w_in_2"][0]
    cuts = np.cumsum([384, 256, 32, 512, 512, 512, 512, 512, 256, 32, 8, 1024])
    q_lat, c_kv, k_rope, z_a, q_b, k_b, v_b, z_b, q_idx, k_idx, w_idx, gate_a2, gate_b2 = np.split(w2, cuts, 1)
    uq = a["w_uq_2"][0].reshape(384, 8, 96)
    uq = np.concatenate([uq[:, :, :64].reshape(384, 512), uq[:, :, 64:].reshape(384, 256)], 1)
    ukv = a["w_ukv_2"][0].reshape(256, 8, 128)
    ukv_k, ukv_v = ukv[:, :, :64].reshape(256, 512), ukv[:, :, 64:].reshape(256, 512)
    parts = {
        "q_r": blocks(q_r), "fz": blocks(np.concatenate([fz_f, fz_b], 1)), "i_r": blocks(i_r), "g_r": blocks(g_r),
        "q_a": blocks(q_a), "k_a": blocks(k_a), "v_a": blocks(v_a),
        "gates": gates(gate_r, gate_a, a["w_br_rec"][0], br_att), "mix_out": blocks(a["w_mix_out"][0]),
        "mem_k": blocks(mem_k), "mem_v": blocks(mem_v), "mem_q": blocks(a["w_mem_q"][0]),
        "mem_o": blocks(a["w_mem_o"][0]),
        "up": np.stack([gate, up], 1).reshape(-1, P, SLOT),
        "down": blocks(a["w_down"][0], 3 * SLOT).reshape(DC, P, 3, SLOT).transpose(0, 2, 1, 3).reshape(-1, P, SLOT),
        "q_idx": blocks(q_idx), "k_idx": blocks(np.tile(k_idx, (1, 4))), "w_idx": blocks(wide(w_idx)),
        "q_lat": blocks(q_lat), "c_kv": blocks(c_kv), "k_rope": blocks(np.tile(k_rope, (1, 4))),
        "uq": per_slot(blocks(uq), 2), "ukv_k": per_slot(blocks(ukv_k), 2), "ukv_v": per_slot(blocks(ukv_v), 2),
        "z_a": blocks(z_a), "q_b": blocks(q_b), "k_b": blocks(k_b), "v_b": blocks(v_b), "z_b": blocks(z_b),
        "gates2": gates(gate_a2, gate_b2, a["w_o_a_2"][0], a["w_o_b_2"][0]), "out2": blocks(a["w_out_2"][0]),
    }
    out = [parts[name] for name, _ in STREAM]
    n = sum(len(x) for x in out)
    return np.concatenate(out + [np.zeros((SLOTS - n, P, SLOT), np.float32)], 0)


def columns(x):
    return np.asarray(x).reshape(-1, P).T


def feature_vectors(a):
    inv = np.zeros((P, 1), np.float32)
    freq = (1.0 / (np.float32(ROPE_THETA) ** (np.arange(0, 16, 2, dtype=np.float32) / np.float32(16)))).astype(np.float32)
    for g in (0, 64):
        for r in range(2):
            inv[g + ROT_HALF * r:g + ROT_HALF * (r + 1), 0] = freq
    conv = a["conv_w"][0].reshape(3, FC, P).transpose(2, 1, 0).reshape(P, 3 * FC)
    lower = a["lower_bounds"].reshape(2, 2, HG_HEADS, P).transpose(3, 0, 1, 2).reshape(P, 16)
    named = {n: columns(a[n]) for n, _ in [("norm_mix", 0), ("norm_mem", 0), ("norm_mem_kv", 0), ("norm_ffn", 0),
                                            ("final_norm", 0), ("norm_g_2", 0), ("final_g_2", 0), ("g_q_lat_2", 0),
                                            ("g_kv_lat_2", 0), ("hg_norm", 0), ("conv_b", 0)]}
    named.update(conv_w=conv, lower=lower, inv_freq=inv)
    return np.concatenate([named[n] for n in VEC], 1)


def features_first(x):
    x = np.asarray(x)[0]
    return np.ascontiguousarray(x.T.reshape(-1, P, x.shape[0]).transpose(1, 0, 2))


def kernel(**inputs):
    import concourse.bacc as bacc
    from concourse.bass_utils import run_bass_kernel_spmd

    a = {k: np.asarray(v) for k, v in inputs.items()}
    arrays = {
        "stream": weight_stream(a), "xT": features_first(a["x"]), "memT": features_first(a["mem"]),
        "pos": a["positions"].astype(np.int32).reshape(S), "vecs": feature_vectors(a),
        "ident": np.eye(P, dtype=np.float32), "const_a": constants_a(), "const_d": constants_d(),
        "sink": a["attn_sink"].reshape(8), "relb": a["rel_bias_2"],
    }
    arrays = {k: np.ascontiguousarray(v) for k, v in arrays.items()}
    nc = bacc.Bacc("TRN2", target_bir_lowering=False, num_devices=1, dynamic_dma_scratch_size=1024)
    ins = [nc.dram_tensor(k, v.shape, mybir.dt.from_np(v.dtype), kind="ExternalInput").ap() for k, v in arrays.items()]
    gvec = nc.dram_tensor("gvec", (8, P, TOEP), F32).ap()
    outT = nc.dram_tensor("outT", (P, DC, S), F32, kind="ExternalOutput").ap()
    build(nc, *ins, gvec, outT)
    r = run_bass_kernel_spmd(nc, [arrays], core_ids=[0])
    y = r.results[0]["outT"]
    return np.ascontiguousarray(y.transpose(2, 1, 0).reshape(1, S, D))
```

```python
from contextlib import ExitStack

import numpy as np

import concourse.bass as bass
from concourse import mybir

F32, F32R, I32 = mybir.dt.float32, mybir.dt.float32r, mybir.dt.int32
ACT = mybir.ActivationFunctionType
ALU = mybir.AluOpType
AX = mybir.AxisListType

P = 128
S = 512
ST = S // P
D = 1024
DC = D // P
MEM = 256
EPS = 1e-6
NEG = -1e30
TAKEN = -3e38
LOWEST = -3.4e38

HG_HEADS = 4
HG_SCALE = 128 ** -0.5
LEVELS = 7
HALF = P // 2
LQ = LEVELS * HALF
UNITS = ST + 1
LN_FLOOR = 1e-19

ATT_SCALE = 64 ** -0.5
ROT_HALF = 8
ROPE_THETA = 500000.0
MEM_HEADS = 4
MEM_SCALE = 256 ** -0.5
FF = 2816
FC = FF // P

MLA_SCALE = 96 ** -0.5
IDX_HEADS = 8
IDX_SCALE = 32 ** -0.5
IDXW_SCALE = IDX_HEADS ** -0.5
TOPK = 128
REL_BUCKETS = 32
REL_MAX = 128
TOEP = 640

BLK = 8
RAW = 4
SPL = 2

TWO_PI = 2 * np.pi
PI_A = 6.28125
PI_B = int((TWO_PI - PI_A) * 2 ** 20) / 2 ** 20
PI_C = TWO_PI - PI_A - PI_B
ROUND = 12582912.0

VALUES = [1, 1, 0, 1, 0, 1, 0, 0]
RAW_AT, TURN_AT = [0, 1, 3, 5], [2, 4, 6, 7]
MIX = [1, 1, 1, 0] * (DC // 2)
MEM_HEAD = [1, 1, 1, 1, 0, 1, 0, 1]
HEAD = [1, 1, 1, 1, 0]
STREAM = [
    ("head0", HEAD), ("head1", HEAD), ("head2", HEAD), ("head3", HEAD), ("q_a", [1] * 4), ("g_r", [1] * 4),
    ("k_a", [1]), ("v_a", [1, 0]),
    ("rec_mix", MIX), ("att_mix", MIX), ("mix_out", [1] * DC),
    ("mem0", MEM_HEAD), ("mem1", MEM_HEAD), ("mem2", MEM_HEAD), ("mem3", MEM_HEAD), ("mem_o", [1] * DC),
    ("up", [1] * (2 * FC)), ("down", [3] * DC),
    ("q_idx", [1] * 2), ("w_idx", [1]), ("k_idx", [1]), ("w_turn", [0]), ("q_lat", [1] * 3), ("c_kv", [1] * 2),
    ("k_rope", [1]), ("uq", [1, 0] * 3), ("ukv_k", [1, 0] * 2), ("ukv_v", [1, 0, 0, 0] * 2), ("z_a", [1] * 4),
    ("q_b", [1] * 4), ("k_b", [1] * 4), ("v_b", VALUES), ("z_b", [1] * 4),
    ("a_mix", MIX), ("b_mix", MIX), ("out2", [1] * DC),
]
FIRST, ENDS = {}, []
_slots = 0
for _name, _need in STREAM:
    FIRST[_name] = len(ENDS)
    for _k in _need:
        _slots += _k
        ENDS.append(_slots)
SLOTS = -(-_slots // RAW) * RAW


def running(table):
    at, n = {}, 0
    for name, count in table:
        at[name] = n
        n += count
    return at, n


SPLIT, _ = running([("mix", DC), ("rec", 4), ("att", 4), ("merged", DC), ("memory", DC), ("mem", DC),
                    ("mem_out", DC), ("ffn", DC), ("hidden", FC), ("mix2", DC), ("q_lat", 3),
                    ("c_kv", 2), ("y_a", 4), ("y_b", 4), ("merged2", DC)])
NORMS = ["mix", "memory", "mem", "ffn", "final", "mix2", "q_lat", "c_kv", "out"]
CHUNKS = {n: {"q_lat": 3, "c_kv": 2}.get(n, DC) for n in NORMS}
SQUARE, _ = running([(n, CHUNKS[n]) for n in NORMS])
ADDED, _ = running([(n, CHUNKS[n] - 1) for n in NORMS])
TURNED, _ = running([(f"head{h}", 1) for h in range(HG_HEADS)] + [("v_a", 1)] + [(f"mem{h}", 2) for h in range(MEM_HEADS)]
                    + [("w_idx", 1), ("ukv_v", 4), ("v_b", 4)])
SILU, _ = running([("q_r", 4), ("g_r", 4), ("z_a", 4), ("z_b", 4)])
ROTATE, _ = running([("first", 5), ("second", 3)])

def band(i):
    return max(0, i - 1), min(ST, i + 2)


def causal(i):
    return 0, i + 1


KINDS = {
    "window": dict(heads=[0, 4, 1, 5, 2, 6, 3, 7], keys=band, per_round=8, banks=1, out="att"),
    "memory": dict(heads=list(range(MEM_HEADS)), keys=lambda i: (0, 2), per_round=4, banks=2, out="mem_out"),
    "mla": dict(heads=list(range(8)), keys=causal, per_round=8, banks=1, out="y_a"),
    "dsa": dict(heads=list(range(8)), keys=causal, per_round=8, banks=1, out="y_b"),
}
KINDS["window"]["serves"] = [(1, slice(0, S)), (0, slice(0, 2 * P)), (2, slice(P, S)), (3, slice(2 * P, S))]
KINDS["memory"]["serves"] = [(0, slice(0, S)), (1, slice(0, S))]
for _n in ("mla", "dsa"):
    KINDS[_n]["serves"] = [(t, slice(P * t, S)) for t in range(ST)]
_u = 0
for _k in KINDS.values():
    _k["units"] = [(h, i) for h in _k["heads"] for i in range(ST)]
    _k["first"], _k["first_head"] = _u, _u // ST
    _u += len(_k["units"])
NORM_LAG, TURN_LAG, PV_LAG, OUT_LAG = 1, 2, 3, 4

VEC, VEC_COLS = running([
    ("norm_mix", 8), ("norm_mem", 8), ("norm_mem_kv", 8), ("norm_ffn", 8), ("final_norm", 8),
    ("norm_g_2", 8), ("final_g_2", 8), ("g_q_lat_2", 3), ("g_kv_lat_2", 2), ("hg_norm", 4),
    ("conv_w", 3 * FC), ("conv_b", FC), ("lower", 16), ("inv_freq", 1)])
CONST_R = [("Qf", LQ), ("Qb", LQ), ("Kf", LQ), ("Kb", LQ), ("Pf", P), ("Uf", P), ("Pb", P), ("Ub", P), ("all", P)]
CONST_A = [("level", 8 * P), ("perm", P), ("band", 3 * P)]
CONST_D = [("perm", P), ("cos", S), ("sin", S), ("causal", S), ("onehot", TOEP), ("group", 4)]
AT_R, COLS_R = running(CONST_R)
AT_A, COLS_A = running(CONST_A)
AT_D, COLS_D = running(CONST_D)


def build(nc, stream, xT, memT, pos, vecs, ident_d, const_r, const_a, const_d, sink_d, relb_d, gvec, outT):
    with ExitStack() as ctx:
        def sem(name):
            return ctx.enter_context(nc.semaphore(name))

        top = [1152]

        def place(name, shape, dt=F32, at=None):
            size = 4 * int(np.prod(shape[1:]))
            off = -(-top[0] // 32) * 32 if at is None else at
            assert off + size <= 229344, (name, off + size)
            if at is None:
                top[0] = off + size
            return nc.alloc_sbuf_tensor_at(name, shape, dt, offset=off)

        hT = place("hT", [P, DC, S])
        nH = place("nH", [P, DC, S], F32R)
        nL = place("nL", [P, DC, S], F32R)
        ring = place("ring", [P, RAW, BLK * P])
        wH = place("wH", [P, SPL, BLK * P], F32R)
        wL = place("wL", [P, SPL, BLK * P], F32R)
        ident = place("ident", [P, P])
        ones = place("ones", [P, P])
        vec = place("vec", [P, VEC_COLS])
        sq = place("sq", [P, 2, S])
        sums = place("sums", [P, S])
        std = place("std", [P, S])
        rstd = place("rstd", [P, S])
        nt = place("nt", [P, 2, S])
        sgb = place("sgb", [P, 2, S])
        vraw = place("vraw", [P, 2, S])
        stat = place("stat", [P, 4, 8])
        lbs = place("lbs", [P, 64])
        sinks = place("sinks", [P, 8])
        tick = place("tick", [P, 2])
        OVER = top[0]

        cA = place("cA", [P, COLS_A])
        cR = place("cR", [P, COLS_R], F32R)
        q0 = top[0]
        qT = place("qT", [P, HG_HEADS, S])
        kk = place("kk", [P, 2, HG_HEADS, S])
        vr = place("vr", [P, ST, S])
        qa0 = top[0]
        qa = place("qa", [P, 4, S])
        ka = place("ka", [P, S], at=-(-q0 // 32) * 32)
        va = place("va", [P, ST, P])
        cosA = place("cosA", [P, S])
        sinA = place("sinA", [P, S])
        gla0 = top[0]
        lf = place("lf", [P, 2, S])
        lftH = place("lftH", [P, 2, ST, P], F32R)
        lftL = place("lftL", [P, 2, ST, P], F32R)
        landing = place("landing", [P, COLS_R], at=top[0])
        E = place("E", [P, 2, 4, S])
        X = place("X", [P, 2, 2, LEVELS * P])
        Sg = place("Sg", [P, ST, S])
        kfb = place("kfb", [P, S])
        lev = place("lev", [P, 8, P])
        top[0] = gla0
        recH = place("recH", [P, 4, S], F32R)
        recL = place("recL", [P, 4, S], F32R)
        attH = place("attH", [P, 4, S], F32R)
        attL = place("attL", [P, 4, S], F32R)
        wx0 = top[0]
        wx = place("wx", [P, 4, S])
        wPT = place("wPT", [P, 2, ST, S])
        posi = place("posi", [P, S], I32, at=wx0)
        ang = place("ang", [P, S], at=wx0 + 4 * S)
        turn = place("turn", [P, S], at=wx0 + 8 * S)
        mtA = place("mtA", [P, DC, S], at=qa0 - 4 * 12 * S)
        sgA = place("sgA", [P, 4, S], at=qa0 - 4 * 4 * S)
        mgH = place("mgH", [P, DC, S], F32R, at=qa0)
        mgL = place("mgL", [P, DC, S], F32R, at=wx0)

        top[0] = OVER
        memx = place("memx", [P, DC, MEM])
        mnH = place("mnH", [P, DC, MEM], F32R)
        mnL = place("mnL", [P, DC, MEM], F32R, at=wx0 + 4 * DC * S)
        addA = place("addA", [P, 2, S])
        mk = place("mk", [P, DC, MEM])
        mv = place("mv", [P, 2, D])
        mq = place("mq", [P, DC, S])
        moH = place("moH", [P, DC, S], F32R)
        moL = place("moL", [P, DC, S], F32R)
        mx = place("mx", [P, 4, S])
        mPT = place("mPT", [P, 2, 2, S])
        nomask = place("nomask", [P, MEM])
        assert top[0] <= wx0 + 4 * DC * S

        top[0] = OVER
        aH = place("aH", [P, FC, S], F32R)
        aL = place("aL", [P, FC, S], F32R)
        gpad = place("gpad", [P, 2, S + 2])
        cv = place("cv", [P, 2, S])
        fu = place("fu", [P, 2, S])

        top[0] = OVER
        cD = place("cD", [P, COLS_D])
        selm = place("selm", [P, 9 * P])
        wtok = place("wtok", [P, ST, IDX_HEADS])
        gv = place("gv", [8, TOEP])
        relb = place("relb", [REL_BUCKETS, 8])
        best = place("best", [P, 8])
        rl = place("rl", [P, 2, S])
        late0 = top[0]
        yaH = place("yaH", [P, 4, S], F32R)
        yaL = place("yaL", [P, 4, S], F32R)
        dx = place("dx", [P, 4, S])
        dPT = place("dPT", [P, 2, ST, S])
        d0 = top[0]
        top[0] = late0
        qlat = place("qlat", [P, 3, S])
        ckv = place("ckv", [P, 2, S])
        qlH = place("qlH", [P, 3, S], F32R)
        qlL = place("qlL", [P, 3, S], F32R)
        ckH = place("ckH", [P, 2, S], F32R)
        ckL = place("ckL", [P, 2, S], F32R)
        qi = place("qi", [P, 2, S])
        assert top[0] <= d0
        top[0] = d0
        qn = place("qn", [P, 4, S])
        qp = place("qp", [P, 2, S])
        kn = place("kn", [P, 4, S])
        kpz = place("kpz", [P, 4, S])
        vA = place("vA", [P, ST, S])
        za = place("za", [P, 4, S])
        kp = place("kp", [P, S])
        ki = place("ki", [P, S])
        kiz = place("kiz", [P, 4, S])
        top[0] = d0
        qb = place("qb", [P, 4, S])
        kb = place("kb", [P, 4, S])
        vB = place("vB", [P, ST, S])
        zb = place("zb", [P, 4, S])
        toep = place("toep", [P, 4, S])
        ybH = place("ybH", [P, 4, S], F32R)
        ybL = place("ybL", [P, 4, S], F32R)
        mtD = place("mtD", [P, DC, S], at=d0)
        addD = place("addD", [P, 2, S], at=d0 + 4 * DC * S)
        mg2L = place("mg2L", [P, DC, S], F32R, at=d0 + 4 * (DC + 2) * S)
        mg2H = place("mg2H", [P, DC, S], F32R, at=late0 + 4 * 8 * S)
        sgD = place("sgD", [P, 4, S], at=late0 + 4 * 16 * S)

        pair = [ctx.enter_context(nc.psum_tensor(f"pair{i}", [P, 2 * S], F32)) for i in range(4)]

        def bank(b):
            return pair[b // 2][:, S * (b % 2):S * (b % 2) + S]

        def vcol(name, c):
            i = VEC[name] + c
            return vec[:, i:i + 1]

        def c_a(name, a, b):
            return cA[:, AT_A[name] + a:AT_A[name] + b]

        def c_r(name, a=0, b=P):
            return cR[:, AT_R[name] + a:AT_R[name] + b]

        def c_d(name, a, b):
            return cD[:, AT_D[name] + a:AT_D[name] + b]

        landed = [sem(f"landed{i}") for i in range(RAW)]
        high_done = sem("high_done")
        split_done = sem("split_done")
        multiplied = sem("multiplied")
        freed = [sem("freed0"), sem("freed1")]
        phase = sem("phase")
        ld_x, ld_vec, ld_a, ld_pos, ld_mem, ld_d, ld_toep, st_gvec, st_out = (
            sem(n) for n in ("ld_x", "ld_vec", "ld_a", "ld_pos", "ld_mem", "ld_d", "ld_toep", "st_gvec", "st_out"))
        ones_set, borders, angle_s, angle_c, tables, lb_diff, lb_exp = (
            sem(n) for n in ("ones_set", "borders", "angle_s", "angle_c", "tables", "lb_diff", "lb_exp"))
        ld_late = [sem(f"ld_late{h}") for h in range(4)]
        ld_r = sem("ld_r")
        dve_own = sem("dve_own")
        sq_made, sq_added, sum_done, std_made, r_made = (
            sem(n) for n in ("sq_made", "sq_added", "sum_done", "std_made", "r_made"))
        v_turned = sem("v_turned")
        nt_made, nh_made, nl_made = sem("nt_made"), sem("nh_made"), sem("nl_made")
        sg_made = sem("sg_made")
        x1_made, y_made = sem("x1_made"), sem("y_made")
        rot_done, rot_used, rotated = sem("rot_done"), sem("rot_used"), sem("rotated")
        f_made, lf_made, lf_turned, lh_made, lft_made, zero_one = (
            sem(n) for n in ("f_made", "lf_made", "lf_turned", "lh_made", "lft_made", "zero_one"))
        dec_done, exp_done, x_made, k_made = (sem(n) for n in ("dec_done", "exp_done", "x_made", "k_made"))
        kiz_made, kpz_made = sem("kiz_made"), sem("kpz_made")
        sc_done, masked, s_made = sem("sc_done"), sem("masked"), sem("s_made")
        cross_done, cross_out, o_done, o_out = (sem(n) for n in ("cross_done", "cross_out", "o_done", "o_out"))
        o_sq, o_sum, o_std, o_norm = (sem(n) for n in ("o_sq", "o_sum", "o_std", "o_norm"))
        conv_made, fsg_made = sem("conv_made"), sem("fsg_made")
        a_sc, a_max, a_neg, a_exp, a_prob, a_turn, a_pt, a_pv = (
            sem("a_" + n) for n in ("sc", "max", "neg", "exp", "prob", "turn", "pt", "pv"))
        t_sc, t_relu, t_acc = sem("t_sc"), sem("t_relu"), sem("t_acc")
        gv_done, gv_out = sem("gv_done"), sem("gv_out")

        def out_of_bank(eng, g):
            eng.wait_ge(freed[g % 2], g // 2 + 1)

        block = ctx.enter_context(nc.Block())

        @block.sync
        def _(sp):
            for c in range(0, DC, 2):
                sp.dma_start(hT[:, c:c + 2, :], xT[:, c:c + 2, :]).then_inc(ld_x, 16)
            slots = stream.rearrange("(n r) p m -> n r p m", r=RAW)
            for r in range(RAW):
                sp.dma_start(ring[:, r, :], slots[0, r]).then_inc(landed[r], 16)
            with sp.Fori(0, SLOTS // RAW - 1) as n:
                for r in range(RAW):
                    sp.wait_ge(split_done, RAW * n + r + 1)
                    sp.dma_start(ring[:, r, :], slots[n + 1, r]).then_inc(landed[r], 16)

        @block.gpsimd
        def _(pool):
            pool.memset(ones[:, :], 1.0).then_inc(ones_set, 1)
            pool.memset(tick[:, :], 0.0).then_inc(ones_set, 1)
            pool.wait_ge(ones_set, 2)

            def split(r, turn_, n, used):
                pool.wait_ge(landed[r], 16 * turn_)
                if used is not None:
                    pool.wait_ge(multiplied, used)
                pool.tensor_tensor(tick[:, 1:2], tick[:, 0:1], tick[:, 0:1], ALU.add).then_inc(high_done, 1)
                pool.tensor_scalar(wH[:, r % SPL, :], ring[:, r, :], 1.0, 0.0, ALU.mult, ALU.add).then_inc(high_done, 1)
                pool.wait_ge(high_done, 2 * n)
                pool.tensor_tensor(wL[:, r % SPL, :], ring[:, r, :], wH[:, r % SPL, :].bitcast(F32),
                                   ALU.subtract).then_inc(split_done, 1)

            for r in range(RAW):
                split(r, 1, r + 1, r - SPL + 1 if r >= SPL else None)
            with pool.Fori(1, SLOTS // RAW) as n:
                for r in range(RAW):
                    split(r, n + 1, RAW * n + r + 1, RAW * n + r - SPL + 1)

        @block.tensor
        def _(pe):
            mm = nc.tensor.matmul
            n_slot, n_phase = [0], [0]

            def barrier():
                n_phase[0] += 1
                pe.drain().then_inc(phase, 1)
                pe.wait_ge(phase, 3 * n_phase[0])

            def norm_sum(name, width=S):
                pe.wait_ge(sq_added, ADDED[name] + CHUNKS[name] - 1)
                if NORMS.index(name):
                    pe.wait_ge(std_made, NORMS.index(name))
                mm(bank(7)[:, :width], ones[:, :], sums[:, :width], start=True, stop=True).then_inc(sum_done, 1)

            def open_slot():
                r = n_slot[0] % SPL
                n_slot[0] += 1
                pe.wait_ge(split_done, n_slot[0])
                return r

            def open_bank(g):
                if g >= 2:
                    out_of_bank(pe, g - 2)
                return bank(g % 2)

            def three(out, a, b, first, last):
                mm(out, a[0], b[0], start=first, stop=False)
                mm(out, a[0], b[1], start=False, stop=False)
                return mm(out, a[1], b[0], start=False, stop=last)

            def weight(r, j):
                return wH[:, r, P * j:P * j + P], wL[:, r, P * j:P * j + P]

            def parts(h, l, n):
                return [(h[:, k, :], l[:, k, :]) for k in range(n)]

            def project(stage, c0, n, xs, width=S, inputs=None):
                for c in range(c0, c0 + n):
                    out = open_bank(FIRST[stage] + c)[:, :width]
                    for k, x in enumerate(xs):
                        if k % BLK == 0:
                            r = open_slot()
                        if inputs is not None and c == c0:
                            pe.wait_ge(nl_made, SPLIT[inputs] + k + 1)
                        last = three(out, weight(r, k % BLK), x, k == 0, k == len(xs) - 1)
                        if k % BLK == BLK - 1 or k == len(xs) - 1:
                            last.then_inc(multiplied, 1)

            def turn_chunk(stage, raw, at, k, tiles=ST):
                out_of_bank(pe, FIRST[stage] + raw)
                out = open_bank(FIRST[stage] + at)
                for t in range(tiles):
                    cs = slice(P * t, P * t + P)
                    last = nc.tensor.transpose(out[:, cs], vraw[:, k % 2, cs], ident[:, :])
                last.then_inc(v_turned, 1)

            def values(stage, j):
                if j in RAW_AT:
                    project(stage, j, 1, n_parts)
                else:
                    c = TURN_AT.index(j)
                    turn_chunk(stage, RAW_AT[c], j, TURNED[stage] + c)

            def halves(stage, first, n_slots, k_n, xs, then=None):
                for s in range(n_slots):
                    g = FIRST[stage] + first(s)
                    r = open_slot()
                    for half in range(2):
                        out = open_bank(g + half)
                        for k in range(k_n):
                            last = three(out, weight(r, k_n * half + k), xs[k], k == 0, k == k_n - 1)
                    last.then_inc(multiplied, 1)
                    if then is not None:
                        then(s)

            def rotate(name, n, src, raw, perm):
                m = ROTATE[name] + n
                out_of_bank(pe, raw)
                if m >= 2:
                    pe.wait_ge(rot_used, m - 1)
                mm(bank(2 + m % 2), perm, src, start=True, stop=True).then_inc(rot_done, 1)

            def head_step(h, j):
                if j < 4:
                    project(f"head{h}", j, 1, n_parts, inputs="mix" if h + j == 0 else None)
                else:
                    turn_chunk(f"head{h}", 3, 4, TURNED[f"head{h}"])

            def recurrence(beside):
                def sums_of(out, d, i, m, first=True, last=True):
                    mm(out, lftH[:, d, i, :], m, start=first, stop=False)
                    return mm(out, lftL[:, d, i, :], m, start=False, stop=last)

                def turn_logs(h):
                    pe.wait_ge(lf_made, h + 1)
                    if h:
                        pe.wait_ge(exp_done, UNITS * h)
                    for d in range(2):
                        for i in range(ST):
                            cs = slice(P * i, P * i + P)
                            last = nc.tensor.transpose(bank(2 + d)[:, cs], lf[:, d, cs], ident[:, :])
                    last.then_inc(lf_turned, 1)

                def cross_decays(h):
                    pe.wait_ge(lft_made, h + 1)
                    for i in range(ST):
                        cs = slice(P * i, P * i + P)
                        d = 0 if i % 2 else 1
                        sums_of(bank(2)[:, cs], d, i, c_r("Pb" if d else "Pf"))
                        sums_of(bank(3)[:, cs], 1 - d, i, c_r("Uf" if d else "Ub"))
                        d = 0 if i >= 2 else 1
                        far = {3: 2, 0: 1}.get(i)
                        for b, dd, name in ((4, d, "Pb" if d else "Pf"), (5, 1 - d, "Uf" if d else "Ub")):
                            last = sums_of(bank(b)[:, cs], dd, i, c_r(name), last=far is None)
                            if far is not None:
                                last = sums_of(bank(b)[:, cs], dd, far, c_r("all"), first=False)
                    last.then_inc(dec_done, 1)

                def tile_decays(h, i):
                    if i == 1:
                        pe.wait_ge(cross_out, h + 1)
                    else:
                        pe.wait_ge(exp_done, UNITS * h + 1 + i)
                    for b, (d, name) in enumerate([(0, "Qf"), (1, "Qb"), (0, "Kf"), (1, "Kb")]):
                        last = sums_of(bank(2 + b)[:, :LQ], d, i, c_r(name, 0, LQ))
                    last.then_inc(dec_done, 1)

                def tile_scores(h, i):
                    n = ST * h + i
                    pe.wait_ge(x_made, UNITS * h + 2 + i)
                    if n:
                        pe.wait_ge(masked, n)
                    for l in range(LEVELS):
                        cs = slice(P * l, P * l + P)
                        mm(pair[3][:, cs], X[:, n % 2, 1, cs], X[:, n % 2, 0, cs], start=True, stop=True)
                    cs = slice(P * i, P * i + P)
                    if i == 0:
                        pe.wait_ge(k_made, h + 1)
                    mm(pair[3][:, P * LEVELS:], kfb[:, cs], qT[:, h, cs], start=True, stop=True).then_inc(sc_done, 1)

                def cross_scores(h):
                    b = (UNITS * h) % 2
                    pe.wait_ge(x_made, UNITS * h + 1)
                    if h:
                        pe.wait_ge(o_out, h)
                    else:
                        pe.wait_ge(exp_done, 2)
                    for j in range(ST):
                        out, cs, t = bank(2 + j), slice(P * j, P * j + P), j ^ 1
                        ts = slice(P * t, P * t + P)
                        mm(out[:, ts], E[:, b, 1, cs], E[:, b, 0, ts], start=True, stop=True)
                        far = slice(2 * P, 4 * P) if j < 2 else slice(0, 2 * P)
                        last = mm(out[:, far], E[:, b, 3, cs], E[:, b, 2, far], start=True, stop=True)
                    last.then_inc(cross_done, 1)

                def output(h):
                    pe.wait_ge(cross_out, h + 1)
                    pe.wait_ge(s_made, ST * (h + 1))
                    pe.wait_ge(exp_done, UNITS * (h + 1) + (2 if h + 1 < HG_HEADS else 0))
                    for j in range(ST):
                        last = mm(bank(2), vr[:, j, P * h:P * h + P], Sg[:, j, :], start=j == 0, stop=j == ST - 1)
                    last.then_inc(o_done, 1)

                turn_logs(0)
                cross_decays(0)
                tile_decays(0, 0)
                for h in range(HG_HEADS):
                    more = h + 1 < HG_HEADS
                    beside(h, 0)
                    cross_scores(h)
                    tile_scores(h, 0)
                    tile_decays(h, 1)
                    beside(h, 1)
                    tile_decays(h, 2)
                    tile_scores(h, 1)
                    beside(h, 2)
                    tile_decays(h, 3)
                    tile_scores(h, 2)
                    if more:
                        turn_logs(h + 1)
                    beside(h, 3)
                    tile_scores(h, 3)
                    if more:
                        cross_decays(h + 1)
                    beside(h, 4)
                    if more:
                        tile_decays(h + 1, 0)
                    output(h)
                for h in range(HG_HEADS):
                    pe.wait_ge(o_sq, h + 1)
                    if h:
                        pe.wait_ge(o_std, h)
                    mm(bank(7), ones[:, :], sq[:, h % 2, :], start=True, stop=True).then_inc(o_sum, 1)

            def attention(name, terms, value, probs, turned, beside=lambda x: None):
                kind = KINDS[name]
                units, u0, n = kind["units"], kind["first"], len(kind["units"])
                per, banks, k0 = kind["per_round"], kind["banks"], SPLIT[kind["out"]]

                def scores(x):
                    (h, i), u = units[x], u0 + x
                    a, b = kind["keys"](i)
                    if x >= 2:
                        pe.wait_ge(a_max, u - 1)
                    pairs = terms(h, i, slice(P * a, P * b))
                    for t, (w, m) in enumerate(pairs):
                        last = mm(bank(2 + u % 2)[:, :P * (b - a)], w, m, start=t == 0, stop=t == len(pairs) - 1)
                    last.then_inc(a_sc, 1)

                def turn_probs(x):
                    (h, i), u = units[x], u0 + x
                    a, b = kind["keys"](i)
                    pe.wait_ge(a_prob, u + 1)
                    if x >= 2:
                        pe.wait_ge(a_pt, u - 1)
                    for t in range(b - a):
                        cs = slice(P * t, P * t + P)
                        last = nc.tensor.transpose(bank(4 + u % 2)[:, cs], probs[:, u % 4, cs], ident[:, :])
                    last.then_inc(a_turn, 1)

                def weigh(j):
                    h = kind["heads"][j]
                    rnd = ST * j // per
                    pe.wait_ge(a_pt, u0 + ST * (j + 1))
                    ahead = 2 if banks == 1 else 1
                    if ST * j % per == 0 and rnd >= ahead:
                        pe.wait_ge(nt_made, k0 + banks * (rnd - ahead + 1))
                    for bk in range(banks):
                        out = bank(6 + (rnd % 2 if banks == 1 else bk))
                        for n_t, (t, qs) in enumerate(kind["serves"]):
                            w, rows = value(h, t, bk)
                            last = mm(out[rows, qs], w, turned[:, j % 2, t, qs], start=n_t == 0,
                                      stop=n_t == len(kind["serves"]) - 1)
                    last.then_inc(a_pv, 1)

                for x in range(n + PV_LAG):
                    if x < n:
                        scores(x)
                        beside(x)
                    if 0 <= x - TURN_LAG < n:
                        turn_probs(x - TURN_LAG)
                    y = x - PV_LAG
                    if y >= 0 and units[y][1] == ST - 1:
                        weigh(y // ST)

            def mix_step(stage, k, branch):
                if k % 4 < 2:
                    project(stage, k, 1, n_parts)
                    return
                half = k % 4 - 2
                out = open_bank(FIRST[stage] + k)
                if half == 0:
                    open_slot()
                r = (n_slot[0] - 1) % SPL
                for i in range(4):
                    last = three(out, weight(r, 4 * half + i), branch[i], i == 0, i == 3)
                if half == 1:
                    last.then_inc(multiplied, 1)

            def head_rows(h):
                return slice(64 * (h % 2), 64 * (h % 2) + 64)

            n_parts = parts(nH, nL, DC)

            pe.wait_ge(ones_set, 2)
            norm_sum("mix")
            pe.wait_ge(ld_a, 48)
            for j in range(5):
                head_step(0, j)
            pe.wait_ge(zero_one, 1)

            def head_beside(h, j):
                if h + 1 < HG_HEADS:
                    head_step(h + 1, j)
                elif j < 4:
                    project("q_a", j, 1, n_parts)

            recurrence(head_beside)
            project("g_r", 0, 4, n_parts)
            project("k_a", 0, 1, n_parts)
            project("v_a", 0, 1, n_parts)
            turn_chunk("v_a", 0, 1, TURNED["v_a"])
            barrier()
            for c in range(4):
                rotate("first", c, qa[:, c, :], FIRST["q_a"] + c, c_a("perm", 0, P))
            rotate("first", 4, ka[:, :], FIRST["k_a"], c_a("perm", 0, P))
            pe.wait_ge(rotated, 5)

            def window_terms(h, i, keys):
                rows = slice(64 * (h // 4), 64 * (h // 4) + 64)
                return [(qa[rows, h % 4, P * i:P * i + P], ka[rows, keys])]

            def window_value(h, t, bk):
                rows = slice(64 * (h // 4), 64 * (h // 4) + 64)
                return va[:, t, rows], rows

            rec, att = parts(recH, recL, 4), parts(attH, attL, 4)

            def rec_beside(x):
                if x % 2 == 0:
                    mix_step("rec_mix", x // 2, rec)

            attention("window", window_terms, window_value, wx, wPT, rec_beside)
            barrier()
            for k in range(16):
                mix_step("att_mix", k, att)
                if k == 0:
                    norm_sum("memory", MEM)
            project("mix_out", 0, DC, parts(mgH, mgL, DC), inputs="merged")

            mn_parts = parts(mnH, mnL, DC)

            def mem_step(h, j):
                stage, k0 = f"mem{h}", TURNED[f"mem{h}"]
                if j in (4, 6):
                    c = (j - 4) // 2
                    turn_chunk(stage, 2 + c, j, k0 + c, 2)
                elif j < 4:
                    project(stage, j, 1, mn_parts, MEM)
                else:
                    project(stage, j, 1, n_parts, inputs="mem" if h == 0 and j == 5 else None)

            pe.wait_ge(nl_made, SPLIT["memory"] + DC)
            for j in range(8):
                mem_step(0, j)
                if j == 1:
                    norm_sum("mem")

            def mem_beside(x):
                h = x // ST + 1
                if h < MEM_HEADS:
                    for j in ((0, 1, 2), (3, 4), (5, 6), (7,))[x % ST]:
                        mem_step(h, j)

            def mem_terms(h, i, keys):
                if i == 0:
                    for j in (6, 7):
                        out_of_bank(pe, FIRST[f"mem{h}"] + j)
                return [(mq[:, 2 * h + b, P * i:P * i + P], mk[:, 2 * h + b, :]) for b in range(2)]

            def mem_value(h, t, bk):
                return mv[:, t, 256 * h + P * bk:256 * h + P * bk + P], slice(0, P)

            attention("memory", mem_terms, mem_value, mx, mPT, mem_beside)
            project("mem_o", 0, DC, parts(moH, moL, DC), inputs="mem_out")
            norm_sum("ffn")
            barrier()

            project("up", 0, 2 * FC, n_parts, inputs="ffn")
            project("down", 0, DC, parts(aH, aL, FC), inputs="hidden")
            norm_sum("final")
            norm_sum("mix2")

            project("q_idx", 0, 2, n_parts, inputs="mix2")
            project("w_idx", 0, 1, n_parts)
            project("k_idx", 0, 1, n_parts)
            turn_chunk("w_idx", 0, FIRST["w_turn"] - FIRST["w_idx"], TURNED["w_idx"])
            pe.wait_ge(ld_d, 32)
            rows = slice(0, REL_BUCKETS)
            mm(bank(4)[0:8, :], relb[:, :], c_d("onehot", 0, S)[rows, :], start=True, stop=True)
            mm(bank(5)[0:8, :TOEP - S], relb[:, :], c_d("onehot", S, TOEP)[rows, :], start=True, stop=True).then_inc(gv_done, 1)
            project("q_lat", 0, 3, n_parts)
            project("c_kv", 0, 2, n_parts)
            project("k_rope", 0, 1, n_parts)
            norm_sum("q_lat")
            norm_sum("c_kv")
            pe.wait_ge(kiz_made, 4)
            n = 0
            for i in range(1, ST):
                for h in range(IDX_HEADS):
                    if n >= 2:
                        pe.wait_ge(t_relu, n - 1)
                    mm(bank(2 + n % 2)[:, :P * (i + 1)], qi[:, h // 4, P * i:P * i + P], kiz[:, h % 4, :P * (i + 1)],
                       start=True, stop=True).then_inc(t_sc, 1)
                    n += 1
            ql, ck = parts(qlH, qlL, 3), parts(ckH, ckL, 2)
            pe.wait_ge(nl_made, SPLIT["c_kv"] + 2)
            halves("uq", lambda s: 2 * s, 3, 3, ql)
            halves("ukv_k", lambda s: 2 * s, 2, 2, ck)

            def turn_pair(s):
                for c in range(2):
                    turn_chunk("ukv_v", 4 * s + c, 4 * s + 2 + c, TURNED["ukv_v"] + 2 * s + c)

            halves("ukv_v", lambda s: 4 * s, 2, 2, ck, turn_pair)
            project("z_a", 0, 4, n_parts)
            rotate("second", 0, kp[:, :], FIRST["k_rope"], c_d("perm", 0, P))
            for c in range(2):
                rotate("second", 1 + c, qp[:, c, :], FIRST["uq"] + 4 + c, c_d("perm", 0, P))
            barrier()

            def mla_terms(h, i, keys):
                qs = slice(P * i, P * i + P)
                return [(qn[head_rows(h), h // 2, qs], kn[head_rows(h), h // 2, keys]),
                        (qp[:, h // 4, qs], kpz[:, h % 4, keys])]

            attention("mla", mla_terms, lambda h, t, bk: (vA[:, t, 64 * h:64 * h + 64], head_rows(h)), dx, dPT)
            barrier()
            project("q_b", 0, 4, n_parts)
            project("k_b", 0, 4, n_parts)
            for j in range(8):
                values("v_b", j)
            project("z_b", 0, 4, n_parts)
            barrier()

            def dsa_terms(h, i, keys):
                return [(qb[head_rows(h), h // 2, P * i:P * i + P], kb[head_rows(h), h // 2, keys])]

            attention("dsa", dsa_terms, lambda h, t, bk: (vB[:, t, 64 * h:64 * h + 64], head_rows(h)), dx, dPT)
            barrier()
            for stage, branch in (("a_mix", parts(yaH, yaL, 4)), ("b_mix", parts(ybH, ybL, 4))):
                for k in range(16):
                    mix_step(stage, k, branch)
            project("out2", 0, DC, parts(mg2H, mg2L, DC), inputs="merged2")
            norm_sum("out")

        @block.scalar
        def _(act):
            A = nc.scalar.activation
            n_phase = [0]

            def barrier():
                n_phase[0] += 1
                act.drain().then_inc(phase, 1)
                act.wait_ge(phase, 3 * n_phase[0])

            def product(stage, c):
                g = FIRST[stage] + c
                act.wait_ge(multiplied, ENDS[g])
                return bank(g % 2), freed[g % 2]

            def copy_out(stage, c, dst, cols=None, scale=1.0):
                b, free = product(stage, c)
                A(dst, b if cols is None else cols(b), ACT.Copy, scale=scale).then_inc(free, 1)

            def squares(name, x, ready, width=S):
                for c in range(CHUNKS[name]):
                    a = ADDED[name] + c - 1
                    ready(c)
                    if c and a >= 2:
                        act.wait_ge(sq_added, a - 1)
                    A(sq[:, a % 2, :width] if c else sums[:, :width], x[:, c, :], ACT.Square).then_inc(sq_made, 1)

            def deviation(name, width=S):
                i = NORMS.index(name)
                act.wait_ge(sum_done, i + 1)
                if i:
                    act.wait_ge(r_made, i)
                A(std[:, :width], bank(7)[:, :width], ACT.Sqrt, scale=1.0 / (P * CHUNKS[name]), bias=EPS).then_inc(std_made, 1)

            def norm(name, x, ready):
                squares(name, x, ready)
                deviation(name)

            def raw_out(stage, at, k, width=S):
                copy_out(stage, at, vraw[:, k % 2, :width], lambda b: b[:, :width])

            def turned_out(stage, at, k, dst, width=S, scale=1.0, few=P):
                act.wait_ge(v_turned, k + 1)
                copy_out(stage, at, dst, lambda b: b[:, :width].rearrange("p (t k) -> p t k", k=P)[:, :, :few], scale)

            def values_out(stage, dst):
                for j in range(8):
                    if j in RAW_AT:
                        raw_out(stage, j, TURNED[stage] + RAW_AT.index(j))
                    else:
                        c = TURN_AT.index(j)
                        turned_out(stage, j, TURNED[stage] + c, dst[:, :, P * c:P * c + P])

            def high(name, c, dst, width=S):
                k = SPLIT[name] + c
                act.wait_ge(nt_made, k + 1)
                A(dst, nt[:, k % 2, :width], ACT.Copy).then_inc(nh_made, 1)

            def highs(name, dst, chunks, width=S):
                for c in range(chunks):
                    high(name, c, dst[:, c, :], width)

            def sigmoids(stage, n):
                for c in range(n):
                    b, _ = product(stage, c)
                    y = SILU[stage] + c
                    if c >= 2:
                        out_of_bank(act, FIRST[stage] + c - 2)
                    A(sgb[:, y % 2, :], b, ACT.Sigmoid).then_inc(sg_made, 1)

            def head_out(h, j):
                stage = f"head{h}"
                if j < 2:
                    b, free = product(stage, j)
                    A(kk[:, j, h, :], b, ACT.Sigmoid).then_inc(free, 1)
                elif j == 2:
                    b, _ = product(stage, j)
                    if h:
                        out_of_bank(act, FIRST[f"head{h - 1}"] + 2)
                    A(sgb[:, h % 2, :], b, ACT.Sigmoid).then_inc(sg_made, 1)
                elif j == 3:
                    raw_out(stage, 3, TURNED[stage])
                else:
                    turned_out(stage, 4, TURNED[stage], vr[:, :, P * h:P * h + P])

            def recurrence(beside):
                two = [x[:, :].rearrange("p (b t) -> p b t", b=2) for x in pair]

                def logs(h):
                    act.wait_ge(f_made, h + 1)
                    A(lf[:, :, :], lf[:, :, :], ACT.Ln).then_inc(lf_made, 1)

                def logs_high(h):
                    act.wait_ge(lf_turned, h + 1)
                    A(lftH[:, :, :, :].rearrange("p d t k -> p (d t k)"), pair[1][:, :], ACT.Copy).then_inc(lh_made, 1)

                def decays(n, width):
                    act.wait_ge(dec_done, n + 1)
                    if n >= 2:
                        act.wait_ge(x_made, n - 1)
                        if (n - 2) % UNITS == 0:
                            act.wait_ge(cross_done, (n - 2) // UNITS + 1)
                    for b in range(2):
                        last = A(E[:, n % 2, 2 * b:2 * b + 2, :width], two[1 + b][:, :, :width], ACT.Exp)
                    last.then_inc(exp_done, 1)

                def cross_copies(h):
                    act.wait_ge(cross_done, h + 1)
                    if h:
                        act.wait_ge(o_done, h)
                    for j in range(ST):
                        for a, b in ((0, P * j), (P * j + P, S)):
                            if b > a:
                                last = A(Sg[:, j, a:b], bank(2 + j)[:, a:b], ACT.Copy)
                    last.then_inc(cross_out, 1)

                logs(0)
                logs_high(0)
                decays(0, S)
                decays(1, LQ)
                for h in range(HG_HEADS):
                    n, more = UNITS * h, h + 1 < HG_HEADS
                    beside(h, 0)
                    cross_copies(h)
                    decays(n + 2, LQ)
                    beside(h, 1)
                    decays(n + 3, LQ)
                    decays(n + 4, LQ)
                    if more:
                        logs(h + 1)
                        logs_high(h + 1)
                    beside(h, 2)
                    beside(h, 3)
                    if more:
                        decays(n + UNITS, S)
                    beside(h, 4)
                    if more:
                        decays(n + UNITS + 1, LQ)
                    act.wait_ge(o_done, h + 1)
                    A(qT[:, h, :], bank(2), ACT.Copy).then_inc(o_out, 1)
                for h in range(HG_HEADS):
                    act.wait_ge(o_out, h + 1)
                    if h >= 2:
                        act.wait_ge(o_sum, h - 1)
                    A(sq[:, h % 2, :], qT[:, h, :], ACT.Square).then_inc(o_sq, 1)
                    act.wait_ge(o_sum, h + 1)
                    A(E[:, 0, h, :], bank(7), ACT.Sqrt, scale=1.0 / P, bias=EPS).then_inc(o_std, 1)

            def attention(name, probs, turned, dst, sink=False, beside=lambda x: None):
                kind = KINDS[name]
                units, u0, n = kind["units"], kind["first"], len(kind["units"])
                per, banks = kind["per_round"], kind["banks"]

                for x in range(n + OUT_LAG + 2):
                    if x < n:
                        (h, i), u = units[x], u0 + x
                        a, b = kind["keys"](i)
                        st = stat[:, u % 4, :]
                        act.wait_ge(a_neg, u + 1)
                        if sink:
                            A(st[:, 3:4], sinks[:, h:h + 1], ACT.Exp, bias=st[:, 1:2])
                        px = probs[:, u % 4, :P * (b - a)]
                        A(px, px, ACT.Exp, bias=st[:, 1:2], accum_out=st[:, 2:3]).then_inc(a_exp, 1)
                        beside(x)
                    y = x - TURN_LAG
                    if 0 <= y < n:
                        (h, i), u = units[y], u0 + y
                        a, b = kind["keys"](i)
                        act.wait_ge(a_turn, u + 1)
                        j = y // ST
                        if i == 0 and j >= 2:
                            act.wait_ge(a_pv, kind["first_head"] + j - 1)
                        A(turned[:, j % 2, a:b, P * i:P * i + P],
                          bank(4 + u % 2)[:, :P * (b - a)].rearrange("p (t q) -> p t q", q=P), ACT.Copy).then_inc(a_pt, 1)
                    y = x - OUT_LAG - 1
                    if 0 <= y < n and y % per == per - 1:
                        for bk in range(banks):
                            c = (y // per) * banks + bk
                            high(kind["out"], c, dst[:, c, :])

            def mix_out(stage, k, sg, before=None):
                if k % 4 < 2:
                    c = 2 * (k // 4) + k % 4
                    y = 4 * (c // 2) + 2 + c % 2
                    if c >= 4:
                        out_of_bank(act, FIRST[stage] + y - 8)
                    elif before is not None:
                        out_of_bank(act, FIRST[before] + y + 8)
                    bk, free = product(stage, k)
                    A(sg[:, c % 4, :], bk, ACT.Sigmoid).then_inc(free, 1)

            def merge(stage, sg, dst, name, before):
                for k in range(16):
                    mix_out(stage, k, sg, before)
                    if k % 4 == 1 and k >= 4:
                        for c in (k // 2 - 2, k // 2 - 1):
                            high(name, c, dst[:, c, :])
                for c in (DC - 2, DC - 1):
                    high(name, c, dst[:, c, :])

            def residual(stage):
                return lambda c: out_of_bank(act, FIRST[stage] + c)

            act.dma_start(vec[:, :], vecs).then_inc(ld_vec, 16)
            act.dma_start(posi[:, :], pos.partition_broadcast(P)).then_inc(ld_pos, 16)
            act.dma_start(ident[:, :], ident_d).then_inc(ld_a, 16)
            act.dma_start(landing[:, :], const_r).then_inc(ld_r, 16)
            act.dma_start(sinks[:, :], sink_d.partition_broadcast(P)).then_inc(ld_a, 16)
            act.dma_start(cA[:, :], const_a).then_inc(ld_a, 16)

            act.wait_ge(lb_diff, 1)
            A(lbs[:, 16:32], lbs[:, 16:32], ACT.Exp).then_inc(lb_exp, 1)
            norm("mix", hT, lambda c: act.wait_ge(ld_x, 16 * DC // 2) if c == 0 else None)
            highs("mix", nH, DC)
            for j in range(5):
                head_out(0, j)
            act.wait_ge(angle_s, 1)
            A(sinA[:, :], sinA[:, :], ACT.Sin).then_inc(tables, 1)
            act.wait_ge(angle_c, 1)
            A(cosA[:, :], cosA[:, :], ACT.Sin, bias=float(np.pi / 2)).then_inc(tables, 1)

            def head_beside(h, j):
                if h + 1 < HG_HEADS:
                    head_out(h + 1, j)
                elif j < 4:
                    copy_out("q_a", j, qa[:, j, :])

            recurrence(head_beside)
            for c in (2, 3):
                out_of_bank(act, FIRST[f"head{c}"] + 2)
            sigmoids("g_r", 4)
            highs("rec", recH, 4)
            copy_out("k_a", 0, ka[:, :])
            raw_out("v_a", 0, TURNED["v_a"])
            turned_out("v_a", 1, TURNED["v_a"], va[:, :, :])
            barrier()
            attention("window", wx, wPT, attH, sink=True,
                      beside=lambda x: mix_out("rec_mix", x // 2, sgA) if x % 2 == 0 else None)
            barrier()
            act.dma_start(memx[:, :, :], memT).then_inc(ld_mem, 16)
            squares("memory", memx, lambda c: act.wait_ge(ld_mem, 16), MEM)
            deviation("memory", MEM)
            merge("att_mix", sgA, mgH, "merged", "rec_mix")
            highs("memory", mnH, DC, MEM)
            squares("mem", hT, residual("mix_out"))

            def mem_out(h, j):
                stage, k0, c = f"mem{h}", TURNED[f"mem{h}"], 2 * h + j % 2
                if j < 2:
                    copy_out(stage, j, mk[:, c, :], lambda b: b[:, :MEM])
                elif j < 4:
                    raw_out(stage, j, k0 + j - 2, MEM)
                elif j in (4, 6):
                    c = 2 * h + (j - 4) // 2
                    turned_out(stage, j, k0 + (j - 4) // 2, mv[:, :, P * c:P * c + P], MEM)
                else:
                    c = 2 * h + (j - 5) // 2
                    copy_out(stage, j, mq[:, c, :])

            mem_out(0, 0)
            deviation("mem")
            mem_out(0, 1)
            highs("mem", nH, DC)
            for j in range(2, 8):
                mem_out(0, j)

            def mem_beside(x):
                h = x // ST + 1
                if h < MEM_HEADS:
                    for j in ((0, 1, 2), (3, 4), (5, 6), (7,))[x % ST]:
                        mem_out(h, j)

            attention("memory", mx, mPT, moH, beside=mem_beside)
            norm("ffn", hT, residual("mem_o"))
            barrier()

            highs("ffn", nH, DC)
            act.wait_ge(borders, 2)
            for j in range(FC):
                if j >= 2:
                    act.wait_ge(conv_made, j - 1)
                copy_out("up", 2 * j, gpad[:, j % 2, 1:S + 1])
                act.wait_ge(conv_made, j + 1)
                if j >= 2:
                    out_of_bank(act, FIRST["up"] + 2 * (j - 2) + 1)
                A(sgb[:, j % 2, :], cv[:, j % 2, :], ACT.Sigmoid).then_inc(fsg_made, 1)
                if j >= 1:
                    high("hidden", j - 1, aH[:, j - 1, :])
            high("hidden", FC - 1, aH[:, FC - 1, :])
            norm("final", hT, residual("down"))

            act.dma_start(cD[:, :], const_d).then_inc(ld_d, 16)
            act.dma_start(relb[:, :], relb_d).then_inc(ld_d, 16)
            norm("mix2", hT, lambda c: act.wait_ge(x1_made, c + 1))
            highs("mix2", nH, DC)
            for c in range(2):
                copy_out("q_idx", c, qi[:, c, :])
            raw_out("w_idx", 0, TURNED["w_idx"])
            copy_out("k_idx", 0, ki[:, :])
            turned_out("w_turn", 0, TURNED["w_idx"], wtok[:, :, :], scale=IDXW_SCALE, few=IDX_HEADS)
            act.wait_ge(gv_done, 1)
            A(gv[:, :S], bank(4)[0:8, :], ACT.Copy).then_inc(gv_out, 1)
            A(gv[:, S:], bank(5)[0:8, :TOEP - S], ACT.Copy).then_inc(gv_out, 1)
            act.wait_ge(gv_out, 2)
            act.dma_start(gvec, gv[:, None, :].broadcast_to([8, P, TOEP])).then_inc(st_gvec, 16)
            for c in range(3):
                copy_out("q_lat", c, qlat[:, c, :])
            for c in range(2):
                copy_out("c_kv", c, ckv[:, c, :])
            copy_out("k_rope", 0, kp[:, :])
            norm("q_lat", qlat, lambda c: out_of_bank(act, FIRST["q_lat"] + c))
            squares("c_kv", ckv, lambda c: out_of_bank(act, FIRST["c_kv"] + c))
            highs("q_lat", qlH, 3)
            deviation("c_kv")
            highs("c_kv", ckH, 2)
            n = 0
            for i in range(1, ST):
                for h in range(IDX_HEADS):
                    act.wait_ge(t_sc, n + 1)
                    if n >= 2:
                        act.wait_ge(t_acc, n - 1)
                    A(rl[:, n % 2, :P * (i + 1)], bank(2 + n % 2)[:, :P * (i + 1)], ACT.Relu,
                      scale=IDX_SCALE).then_inc(t_relu, 1)
                    n += 1
            for c in range(6):
                copy_out("uq", c, qn[:, c, :] if c < 4 else qp[:, c - 4, :])
            for c in range(4):
                copy_out("ukv_k", c, kn[:, c, :])
            for s in range(2):
                for c in range(2):
                    raw_out("ukv_v", 4 * s + c, TURNED["ukv_v"] + 2 * s + c)
                for c in range(2):
                    h = 2 * s + c
                    turned_out("ukv_v", 4 * s + 2 + c, TURNED["ukv_v"] + h, vA[:, :, P * h:P * h + P])
            sigmoids("z_a", 4)
            barrier()
            attention("mla", dx, dPT, yaH)
            barrier()
            act.wait_ge(st_gvec, 16)

            def load_bias(h, done):
                act.dma_start(toep[:, h % 4, :], bass.AP(gvec.tensor, h * P * TOEP + P - 1, [[TOEP - 1, P], [1, S]])).then_inc(done, 16)

            for h in range(4):
                load_bias(h, ld_toep)
            for c in range(4):
                copy_out("q_b", c, qb[:, c, :])
            for c in range(4):
                copy_out("k_b", c, kb[:, c, :])
            values_out("v_b", vB)
            sigmoids("z_b", 4)
            barrier()

            def bias_beside(x):
                h = x // ST
                if x % ST == ST - 1 and h < 4:
                    load_bias(h + 4, ld_late[h])

            attention("dsa", dx, dPT, ybH, beside=bias_beside)
            barrier()
            for k in range(16):
                mix_out("a_mix", k, sgD)
            merge("b_mix", sgD, mg2H, "merged2", "a_mix")
            norm("out", hT, residual("out2"))
            for c in range(DC):
                act.wait_ge(y_made, c + 1)
                act.dma_start(outT[:, c, :], hT[:, c, :]).then_inc(st_out, 16)
            act.wait_ge(st_out, 16 * DC)

        @block.vector
        def _(dve):
            V = nc.vector
            n_phase, n_own = [0], [0]

            def barrier():
                n_phase[0] += 1
                dve.drain().then_inc(phase, 1)
                dve.wait_ge(phase, 3 * n_phase[0])

            def own(ins):
                n_own[0] += 1
                ins.then_inc(dve_own, 1)
                dve.wait_ge(dve_own, n_own[0])

            def product(stage, c):
                g = FIRST[stage] + c
                dve.wait_ge(multiplied, ENDS[g])
                return bank(g % 2), freed[g % 2]

            def open_split(name, c, width=S):
                k = SPLIT[name] + c
                if k >= 2:
                    dve.wait_ge(nl_made, k - 1)
                return nt[:, k % 2, :width]

            def low(name, c, hi, lo, width=S):
                k = SPLIT[name] + c
                dve.wait_ge(nh_made, k + 1)
                V.tensor_tensor(lo[:, c, :], nt[:, k % 2, :width], hi[:, c, :].bitcast(F32),
                                ALU.subtract).then_inc(nl_made, 1)

            def accumulate(name, c, width=S):
                a = ADDED[name] + c - 1
                dve.wait_ge(sq_made, SQUARE[name] + c + 1)
                if a:
                    dve.wait_ge(sq_added, a)
                V.tensor_tensor(sums[:, :width], sums[:, :width], sq[:, a % 2, :width], ALU.add).then_inc(sq_added, 1)

            def accumulate_all(name, width=S):
                for c in range(1, CHUNKS[name]):
                    accumulate(name, c, width)

            def inverse(name, width=S):
                i = NORMS.index(name)
                dve.wait_ge(std_made, i + 1)
                V.reciprocal(rstd[:, :width], std[:, :width]).then_inc(r_made, 1)
                dve.wait_ge(r_made, i + 1)

            def normed(out, x, gain, c, width=S):
                return V.scalar_tensor_tensor(out=out, in0=x[:, c, :], scalar=vcol(gain, c), in1=rstd[:, :width],
                                              op0=ALU.mult, op1=ALU.mult)

            def norm(name, x, gain, hi, lo, width=S):
                chunks = CHUNKS[name]
                for c in range(chunks):
                    normed(open_split(name, c, width), x, gain, c, width).then_inc(nt_made, 1)
                    if c:
                        low(name, c - 1, hi, lo, width)
                low(name, chunks - 1, hi, lo, width)

            def silu(stage, n, dst, scale=None):
                for c in range(n):
                    dve.wait_ge(sg_made, SILU[stage] + c + 1)
                    b, free = product(stage, c)
                    sg = sgb[:, (SILU[stage] + c) % 2, :]
                    if scale is None:
                        V.tensor_tensor(dst[:, c, :], b, sg, ALU.mult).then_inc(free, 1)
                    else:
                        V.scalar_tensor_tensor(out=dst[:, c, :], in0=b, scalar=scale, in1=sg,
                                               op0=ALU.mult, op1=ALU.mult).then_inc(free, 1)

            def rotate(name, n, x, cos, sin):
                m = ROTATE[name] + n
                dve.wait_ge(rot_done, m + 1)
                if m:
                    dve.wait_ge(rotated, m)
                V.tensor_tensor(sgb[:, m % 2, :], bank(2 + m % 2), sin, ALU.mult).then_inc(rot_used, 1)
                own(V.tensor_tensor(x, x, cos, ALU.mult))
                V.tensor_tensor(x, x, sgb[:, m % 2, :], ALU.add).then_inc(rotated, 1)

            def residual(stage, name):
                for c in range(DC):
                    b, free = product(stage, c)
                    V.tensor_tensor(hT[:, c, :], b, hT[:, c, :], ALU.add).then_inc(free, 1)
                    if c >= 2:
                        accumulate(name, c - 1)
                accumulate(name, DC - 1)

            def lower_bounds():
                dve.wait_ge(ld_vec, 16)
                a = vec[:, VEC["lower"]:VEC["lower"] + 16].rearrange("p (d l h) -> p d l h", d=2, l=2)
                m = lbs[:, 0:8].rearrange("p (d h) -> p d h", d=2)
                e = lbs[:, 16:32].rearrange("p (d l h) -> p d l h", d=2, l=2)
                own(V.tensor_tensor(m, a[:, :, 0, :], a[:, :, 1, :], ALU.max))
                own(V.tensor_tensor(e[:, :, 0, :], a[:, :, 0, :], m, ALU.subtract))
                V.tensor_tensor(e[:, :, 1, :], a[:, :, 1, :], m, ALU.subtract).then_inc(lb_diff, 1)
                dve.wait_ge(lb_exp, 1)
                own(V.tensor_tensor(m, e[:, :, 0, :], e[:, :, 1, :], ALU.add))
                own(V.reciprocal(m, m))
                own(V.tensor_tensor(lbs[:, 32:40].rearrange("p (d h) -> p d h", d=2), e[:, :, 0, :], m, ALU.mult))
                own(V.tensor_scalar(lbs[:, 40:48], lbs[:, 32:40], -1.0, 1.0, ALU.mult, ALU.add))
                own(V.tensor_scalar(lbs[:, 48:56], lbs[:, 32:40], 1.0, None, ALU.subtract))

            def lb(which, d, h):
                i = 32 + 8 * which + 4 * d + h
                return lbs[:, i:i + 1]

            def recurrence():
                def forget(h):
                    for d in range(2):
                        out_of_bank(dve, FIRST[f"head{h}"] + d)
                        own(V.tensor_scalar(lf[:, d, :], kk[:, d, h, :], lb(1, d, h), lb(0, d, h), ALU.mult, ALU.add))
                    V.tensor_scalar(lf[:, :, :], lf[:, :, :], LN_FLOOR, None, ALU.max).then_inc(f_made, 1)

                def keys(h):
                    for d in range(2):
                        own(V.tensor_scalar(kk[:, d, h, :], kk[:, d, h, :], lb(2, d, h), lb(1, d, h), ALU.mult, ALU.add))
                    if h:
                        dve.wait_ge(sc_done, ST * h)
                    V.tensor_tensor(kfb[:, :], kk[:, 0, h, :], kk[:, 1, h, :], ALU.add).then_inc(k_made, 1)

                def cross(h):
                    n = UNITS * h
                    dve.wait_ge(exp_done, n + 1)
                    e = E[:, n % 2, :, :]
                    V.tensor_tensor(e[:, 0, :], e[:, 0, :], qT[:, h, :], ALU.mult)
                    V.tensor_tensor(e[:, 2, :], e[:, 2, :], qT[:, h, :], ALU.mult)
                    for b, view in ((1, "p (a two k) -> p two a k"), (3, "p (two a k) -> p two a k")):
                        for d in range(2):
                            x = e[:, b, :].rearrange(view, two=2, k=P)[:, d]
                            last = V.tensor_tensor(x, x, kk[:, d, h, :].rearrange(view, two=2, k=P)[:, d], ALU.mult)
                    last.then_inc(x_made, 1)

                def tile(h, i):
                    n, m = UNITS * h + 1 + i, ST * h + i
                    dve.wait_ge(exp_done, n + 1)
                    if m >= 2:
                        dve.wait_ge(sc_done, m - 1)
                    cs = slice(P * i, P * i + P)
                    for l in range(LEVELS):
                        c = 1 << l

                        def two(x):
                            return x.rearrange("p (b two c) -> p two b c", two=2, c=c)

                        ls, xs = slice(HALF * l, HALF * l + HALF), slice(P * l, P * l + P)
                        for kind, half, b, src in ((0, 1, 0, qT[:, h, cs]), (0, 0, 1, qT[:, h, cs]),
                                                   (1, 0, 2, kk[:, 0, h, cs]), (1, 1, 3, kk[:, 1, h, cs])):
                            last = V.tensor_tensor(two(X[:, m % 2, kind, xs])[:, half],
                                                   E[:, n % 2, b, ls].rearrange("p (b c) -> p b c", c=c),
                                                   two(src)[:, half], ALU.mult)
                    last.then_inc(x_made, 1)

                def select(h, i):
                    m = ST * h + i
                    dve.wait_ge(sc_done, m + 1)
                    if m:
                        dve.wait_ge(s_made, m)
                    V.tensor_tensor(lev[:, :, :], pair[3][:, :].rearrange("p (l t) -> p l t", l=8),
                                    c_a("level", 0, 8 * P).rearrange("p (l t) -> p l t", l=8),
                                    ALU.mult).then_inc(masked, 1)
                    dve.wait_ge(masked, m + 1)
                    if h and i == 0:
                        dve.wait_ge(o_done, h)
                    V.tensor_reduce(Sg[:, i, P * i:P * i + P], lev[:, :, :].rearrange("p l t -> p t l"),
                                    AX.X, ALU.add).then_inc(s_made, 1)

                def logs_low(h):
                    dve.wait_ge(lh_made, h + 1)
                    V.tensor_tensor(lftL[:, :, :, :].rearrange("p d t k -> p (d t k)"), pair[1][:, :],
                                    lftH[:, :, :, :].rearrange("p d t k -> p (d t k)").bitcast(F32),
                                    ALU.subtract).then_inc(lft_made, 1)

                def queries(h):
                    dve.wait_ge(sg_made, SILU["q_r"] + h + 1)
                    b, free = product(f"head{h}", 2)
                    V.scalar_tensor_tensor(out=qT[:, h, :], in0=b, scalar=HG_SCALE, in1=sgb[:, h % 2, :],
                                           op0=ALU.mult, op1=ALU.mult).then_inc(free, 1)

                def start(h):
                    keys(h)
                    out_of_bank(dve, FIRST[f"head{h}"] + 2)
                    cross(h)
                    tile(h, 0)

                forget(0)
                queries(0)
                logs_low(0)
                start(0)
                for h in range(HG_HEADS):
                    more = h + 1 < HG_HEADS
                    tile(h, 1)
                    select(h, 0)
                    tile(h, 2)
                    if more:
                        forget(h + 1)
                    select(h, 1)
                    tile(h, 3)
                    select(h, 2)
                    if more:
                        logs_low(h + 1)
                        queries(h + 1)
                    select(h, 3)
                    if more:
                        start(h + 1)
                for h in range(HG_HEADS):
                    dve.wait_ge(o_std, h + 1)
                    own(V.reciprocal(E[:, 0, h, :], E[:, 0, h, :]))
                    V.scalar_tensor_tensor(out=qT[:, h, :], in0=qT[:, h, :], scalar=vcol("hg_norm", h), in1=E[:, 0, h, :],
                                           op0=ALU.mult, op1=ALU.mult).then_inc(o_norm, 1)

            def rotary_angles():
                dve.wait_ge(ld_pos, 16)
                own(V.tensor_copy(ang[:, :], posi[:, :]))
                own(V.tensor_scalar(ang[:, :], ang[:, :], vcol("inv_freq", 0), None, ALU.mult))
                pi = float(np.float32(3.1415925))
                for out, shift, lo, hi, done in ((sinA, 0.0, -pi, pi, angle_s),
                                                 (cosA, 0.25, -1.5 * np.pi + 1e-6, 0.5 * np.pi - 1e-6, angle_c)):
                    own(V.tensor_scalar(turn[:, :], ang[:, :], 1.0 / TWO_PI, shift, ALU.mult, ALU.add))
                    own(V.tensor_scalar(turn[:, :], turn[:, :], ROUND, None, ALU.add))
                    own(V.tensor_scalar(turn[:, :], turn[:, :], ROUND, None, ALU.subtract))
                    src = ang
                    for part in (PI_A, PI_B, PI_C):
                        own(V.scalar_tensor_tensor(out=out[:, :], in0=turn[:, :], scalar=-part, in1=src[:, :],
                                                   op0=ALU.mult, op1=ALU.add))
                        src = out
                    V.tensor_scalar(out[:, :], out[:, :], lo, hi, ALU.max, ALU.min).then_inc(done, 1)

            def attention(name, x_buf, scale, mask, hi, lo, bias=None, sink=False, gate=None,
                          beside=lambda x: None):
                kind = KINDS[name]
                units, u0, n = kind["units"], kind["first"], len(kind["units"])
                per, banks = kind["per_round"], kind["banks"]

                def row_max(x):
                    (h, i), u = units[x], u0 + x
                    a, b = kind["keys"](i)
                    w, st = P * (b - a), stat[:, u % 4, :]
                    dve.wait_ge(a_sc, u + 1)
                    if x >= 4:
                        dve.wait_ge(a_turn, u - 3)
                    sx, src, by = x_buf[:, u % 4, :w], bank(2 + u % 2)[:, :w], scale
                    if bias is not None:
                        own(V.scalar_tensor_tensor(out=sx, in0=src, scalar=scale, in1=bias(h, i),
                                                   op0=ALU.mult, op1=ALU.add))
                        src, by = sx, 1.0
                    V.tensor_tensor_reduce(out=sx, in0=src, in1=mask(i), scale=by, scalar=LOWEST, op0=ALU.add,
                                           op1=ALU.max, accum_out=st[:, 0:1]).then_inc(a_max, 1)
                    dve.wait_ge(a_max, u + 1)
                    if sink:
                        V.tensor_scalar(st[:, 1:2], st[:, 0:1], sinks[:, h:h + 1], -1.0, ALU.max, ALU.mult).then_inc(a_neg, 1)
                    else:
                        V.tensor_scalar(st[:, 1:2], st[:, 0:1], -1.0, None, ALU.mult).then_inc(a_neg, 1)

                def normalise(x):
                    (h, i), u = units[x], u0 + x
                    a, b = kind["keys"](i)
                    px, st = x_buf[:, u % 4, :P * (b - a)], stat[:, u % 4, :]
                    dve.wait_ge(a_exp, u + 1)
                    total = st[:, 2:3]
                    if sink:
                        own(V.tensor_tensor(st[:, 4:5], st[:, 2:3], st[:, 3:4], ALU.add))
                        total = st[:, 4:5]
                    own(V.reciprocal(st[:, 5:6], total))
                    V.tensor_scalar(px, px, st[:, 5:6], None, ALU.mult).then_inc(a_prob, 1)

                for x in range(n + OUT_LAG + 3):
                    if x < n:
                        row_max(x)
                    if 0 <= x - NORM_LAG < n:
                        normalise(x - NORM_LAG)
                    if x < n:
                        beside(x)
                    y = x - OUT_LAG
                    if 0 <= y < n and y % per == per - 1:
                        rnd = y // per
                        for bk in range(banks):
                            c = rnd * banks + bk
                            out = open_split(kind["out"], c)
                            dve.wait_ge(a_pv, kind["first_head"] + y // ST + 1)
                            src = bank(6 + (rnd % 2 if banks == 1 else bk))
                            if gate is None:
                                V.tensor_copy(out, src).then_inc(nt_made, 1)
                            else:
                                V.tensor_tensor(out, src, gate[:, c, :], ALU.mult).then_inc(nt_made, 1)
                    y = x - OUT_LAG - 2
                    if 0 <= y < n and y % per == per - 1:
                        for bk in range(banks):
                            low(kind["out"], (y // per) * banks + bk, hi, lo)

            def mix_pair(stage, p, sg, use):
                for c in (2 * p, 2 * p + 1):
                    out_of_bank(dve, FIRST[stage] + 4 * p + c % 2)
                    src, free = product(stage, 4 * p + 2 + c % 2)
                    use(c, src, sg[:, c % 4, :], free)

            def first_branch(stage, p, sg, mt):
                mix_pair(stage, p, sg, lambda c, src, g, free:
                         V.tensor_tensor(mt[:, c, :], src, g, ALU.mult).then_inc(free, 1))

            def merge(stage, sg, mt, add, name, hi, lo):
                def use(c, src, g, free):
                    out = open_split(name, c)
                    V.tensor_tensor(add[:, c % 2, :], src, g, ALU.mult).then_inc(free, 1)
                    out_of_bank(dve, FIRST[stage] + 4 * (c // 2) + 2 + c % 2)
                    V.tensor_tensor(out, add[:, c % 2, :], mt[:, c, :], ALU.add).then_inc(nt_made, 1)
                    if c:
                        low(name, c - 1, hi, lo)

                for p in range(DC // 2):
                    mix_pair(stage, p, sg, use)
                low(name, DC - 1, hi, lo)

            lower_bounds()
            accumulate_all("mix")
            inverse("mix")
            norm("mix", hT, "norm_mix", nH, nL)
            dve.wait_ge(ld_r, 16)
            V.tensor_copy(cR[:, :], landing[:, :]).then_inc(zero_one, 1)
            rotary_angles()
            dve.wait_ge(ld_a, 48)
            recurrence()
            for c in range(4):
                y, g = SILU["g_r"] + c, FIRST["g_r"] + c
                dve.wait_ge(sg_made, y + 1)
                b, free = product("g_r", c)
                out = open_split("rec", c)
                V.tensor_tensor(X[:, c % 2, 0, :S], b, sgb[:, y % 2, :], ALU.mult).then_inc(free, 1)
                out_of_bank(dve, g)
                dve.wait_ge(o_norm, c + 1)
                V.tensor_tensor(out, X[:, c % 2, 0, :S], qT[:, c, :], ALU.mult).then_inc(nt_made, 1)
                if c:
                    low("rec", c - 1, recH, recL)
            low("rec", 3, recH, recL)
            barrier()
            dve.wait_ge(tables, 2)
            for c in range(4):
                rotate("first", c, qa[:, c, :], cosA[:, :], sinA[:, :])
            rotate("first", 4, ka[:, :], cosA[:, :], sinA[:, :])
            own(V.memset(wPT[:, :, 1, S - P:], 0.0))

            def band_mask(i):
                a, b = band(i)
                return c_a("band", P * (a - i + 1), P * (b - i + 1))

            attention("window", wx, ATT_SCALE, band_mask, attH, attL, sink=True,
                      beside=lambda x: first_branch("rec_mix", x // 8, sgA, mtA) if x % 8 == 6 else None)
            barrier()
            accumulate_all("memory", MEM)
            inverse("memory", MEM)
            merge("att_mix", sgA, mtA, addA, "merged", mgH, mgL)
            norm("memory", memx, "norm_mem_kv", mnH, mnL, MEM)
            residual("mix_out", "mem")
            inverse("mem")
            norm("mem", hT, "norm_mem", nH, nL)

            own(V.memset(nomask[:, :], 0.0))
            attention("memory", mx, MEM_SCALE, lambda i: nomask[:, :], moH, moL)
            residual("mem_o", "ffn")
            barrier()

            for c in (0, S + 1):
                V.memset(gpad[:, :, c:c + 1], 0.0).then_inc(borders, 1)
            dve.wait_ge(borders, 2)
            inverse("ffn")
            norm("ffn", hT, "norm_ffn", nH, nL)
            for j in range(FC):
                w = [vcol("conv_w", 3 * j + t) for t in range(3)]
                x, y = gpad[:, j % 2, :], cv[:, j % 2, :]
                out_of_bank(dve, FIRST["up"] + 2 * j)
                own(V.tensor_scalar(y, x[:, 1:S + 1], w[1], vcol("conv_b", j), ALU.mult, ALU.add))
                own(V.scalar_tensor_tensor(out=y, in0=x[:, 0:S], scalar=w[0], in1=y, op0=ALU.mult, op1=ALU.add))
                V.scalar_tensor_tensor(out=y, in0=x[:, 2:S + 2], scalar=w[2], in1=y,
                                       op0=ALU.mult, op1=ALU.add).then_inc(conv_made, 1)
                dve.wait_ge(fsg_made, j + 1)
                out = open_split("hidden", j)
                b, free = product("up", 2 * j + 1)
                V.tensor_tensor(fu[:, j % 2, :], b, sgb[:, j % 2, :], ALU.mult).then_inc(free, 1)
                out_of_bank(dve, FIRST["up"] + 2 * j + 1)
                V.tensor_tensor(out, fu[:, j % 2, :], y, ALU.mult).then_inc(nt_made, 1)
                if j:
                    low("hidden", j - 1, aH, aL)
            low("hidden", FC - 1, aH, aL)
            residual("down", "final")

            inverse("final")
            for c in range(DC):
                normed(hT[:, c, :], hT, "final_norm", c).then_inc(x1_made, 1)
                if c >= 2:
                    accumulate("mix2", c - 1)
            accumulate("mix2", DC - 1)
            inverse("mix2")
            norm("mix2", hT, "norm_g_2", nH, nL)
            dve.wait_ge(ld_d, 32)
            out_of_bank(dve, FIRST["k_idx"])
            for g in range(4):
                V.tensor_scalar(kiz[:, g, :], ki[:, :], c_d("group", g, g + 1), None, ALU.mult).then_inc(kiz_made, 1)
            accumulate_all("q_lat")
            inverse("q_lat")
            norm("q_lat", qlat, "g_q_lat_2", qlH, qlL)
            accumulate_all("c_kv")
            inverse("c_kv")
            norm("c_kv", ckv, "g_kv_lat_2", ckH, ckL)
            out_of_bank(dve, FIRST["w_turn"])
            at = {1: 0, 2: 2 * P, 3: 5 * P}
            n = 0
            for i in range(1, ST):
                w, acc = P * (i + 1), selm[:, at[i]:at[i] + P * (i + 1)]
                for h in range(IDX_HEADS):
                    dve.wait_ge(t_relu, n + 1)
                    if h:
                        dve.wait_ge(t_acc, n)
                    V.scalar_tensor_tensor(out=acc, in0=rl[:, n % 2, :w], scalar=wtok[:, i, h:h + 1],
                                           in1=acc if h else c_d("causal", S - w, S),
                                           op0=ALU.mult, op1=ALU.add).then_inc(t_acc, 1)
                    n += 1
            dve.wait_ge(t_acc, n)

            def top_keys(i):
                acc = selm[:, at[i]:at[i] + P * (i + 1)]
                for _r in range(TOPK // 8):
                    own(V.max(best[:, :], acc))
                    own(V.match_replace(acc, best[:, :], acc, TAKEN))
                own(V.tensor_scalar(acc, acc, 0.9 * TAKEN, NEG, ALU.is_gt, ALU.mult))

            top_keys(1)
            silu("z_a", 4, za)
            for c in (2, 3):
                out_of_bank(dve, FIRST["z_a"] + c)
            rotate("second", 0, kp[:, :], c_d("cos", 0, S), c_d("sin", 0, S))
            for c in range(2):
                rotate("second", 1 + c, qp[:, c, :], c_d("cos", 0, S), c_d("sin", 0, S))
            dve.wait_ge(rotated, ROTATE["second"] + 1)
            for g in range(4):
                V.tensor_scalar(kpz[:, g, :], kp[:, :], c_d("group", g, g + 1), None, ALU.mult).then_inc(kpz_made, 1)
            barrier()

            def causal_mask(i):
                return c_d("causal", S - P * (i + 1), S)

            attention("mla", dx, MLA_SCALE, causal_mask, yaH, yaL, gate=za)
            barrier()
            top_keys(2)
            top_keys(3)
            silu("z_b", 4, zb)
            dve.wait_ge(ld_toep, 16 * 4)
            barrier()

            def top_mask(i):
                if i == 0:
                    return causal_mask(0)
                return selm[:, at[i]:at[i] + P * (i + 1)]

            def head_bias(h, i):
                if h >= 4 and i == 0:
                    dve.wait_ge(ld_late[h - 4], 16)
                return toep[:, h % 4, S - P * (i + 1):]

            attention("dsa", dx, ATT_SCALE, top_mask, ybH, ybL, gate=zb, bias=head_bias)
            barrier()
            for p in range(DC // 2):
                first_branch("a_mix", p, sgD, mtD)
            merge("b_mix", sgD, mtD, addD, "merged2", mg2H, mg2L)
            residual("out2", "out")
            inverse("out")
            for c in range(DC):
                normed(hT[:, c, :], hT, "final_g_2", c).then_inc(y_made, 1)


def level_constants():
    out = {n: np.zeros((P, LQ), np.float32) for n in ("Qf", "Qb", "Kf", "Kb")}
    masks = np.zeros((P, 8, P), np.float32)
    u = np.arange(P)
    for l in range(LEVELS):
        c = 1 << l
        for b in range(HALF // c):
            mid = 2 * c * b + c
            for j in range(c):
                col, late, early = l * HALF + b * c + j, mid + j, mid - c + j
                out["Qf"][:, col] = (u >= mid) & (u <= late)
                out["Qb"][:, col] = (u >= early) & (u < mid)
                out["Kf"][:, col] = (u > early) & (u < mid)
                out["Kb"][:, col] = (u >= mid) & (u < late)
            lo, hi = slice(mid - c, mid), slice(mid, mid + c)
            masks[lo, l, hi] = 1.0
            masks[hi, l, lo] = 1.0
    masks[:, LEVELS, :] = np.eye(P)
    s, t = u[:, None], u[None, :]
    out["Pf"], out["Uf"] = s <= t, s > t
    out["Pb"], out["Ub"] = s >= t, s < t
    out["level"] = masks.reshape(P, -1)
    return out


def rotary_partners(group, half):
    m = np.zeros((P, P), np.float32)
    for g in range(0, P, group):
        for r in range(half):
            m[g + half + r, g + r] = -1.0
            m[g + r, g + half + r] = 1.0
    return m


def constants_a():
    c = level_constants()
    c["perm"] = rotary_partners(64, ROT_HALF)
    q, k = np.arange(P)[:, None], np.arange(3 * P)[None, :] - P
    c["band"] = np.where(np.abs(q - k) <= 128, 0.0, NEG)
    c["all"] = np.ones((P, P))
    return [np.concatenate([np.asarray(c[n], np.float32) for n, _ in table], 1) for table in (CONST_R, CONST_A)]


def constants_d():
    c = {"perm": rotary_partners(32, 16)}
    freqs = np.float32(10000.0) ** (-np.arange(16, dtype=np.float32) / np.float32(16))
    angle = np.arange(S, dtype=np.float32)[None, :] * freqs[np.arange(P) % 16][:, None]
    c["cos"], c["sin"] = np.cos(angle), np.sin(angle)
    q, k = np.arange(P)[:, None], np.arange(S)[None, :] - (S - P)
    c["causal"] = np.where((k < 0) | (k // 64 <= q // 64), 0.0, NEG)
    rel = np.arange(TOEP) - (S - 1)
    nb, exact = REL_BUCKETS // 2, REL_BUCKETS // 4
    n = np.abs(rel)
    far = np.log(np.maximum(n, 1).astype(np.float32) / np.float32(exact)) / np.log(REL_MAX / exact) * (nb - exact)
    far = np.minimum(exact + far.astype(np.float32).astype(np.int32), nb - 1)
    bucket = (rel > 0) * nb + np.where(n < exact, n, far)
    onehot = np.zeros((P, TOEP), np.float32)
    onehot[bucket, np.arange(TOEP)] = 1.0
    c["onehot"] = onehot
    c["group"] = np.arange(P)[:, None] // 32 == np.arange(4)[None, :]
    return np.concatenate([np.asarray(c[n], np.float32) for n, _ in CONST_D], 1)


def blocks(w, pad_to=None):
    k, n = w.shape
    x = w.reshape(k // P, P, n // P, P).transpose(2, 1, 0, 3).reshape(n // P, P, k)
    if pad_to is not None:
        x = np.concatenate([x, np.zeros((n // P, P, pad_to - k), w.dtype)], 2)
    return x


def wide(w):
    return np.concatenate([w, np.zeros((w.shape[0], P - w.shape[1]), w.dtype)], 1)


def weight_stream(a):
    SLOT = BLK * P

    def per_slot(x, count):
        n, p, k = x.shape
        x = x.reshape(n // count, count, p, k).transpose(0, 2, 1, 3).reshape(n // count, p, count * k)
        return np.concatenate([x, np.zeros((n // count, p, SLOT - count * k), x.dtype)], 2)

    def mixed(gate, branch):
        g, y = blocks(gate), blocks(branch)
        g = g.reshape(DC // 2, 2, P, SLOT)
        y = y.reshape(DC // 2, 2, P, SLOT // 2).transpose(0, 2, 1, 3).reshape(DC // 2, 1, P, SLOT)
        return np.concatenate([g, y], 1).reshape(-1, P, SLOT)

    w = a["w_in"][0]
    cuts = np.cumsum([512] * 6 + [128, 128, 1024])
    q_r, fz_f, fz_b, i_r, g_r, q_a, k_a, v_a, gate_r, gate_a = np.split(w, cuts, 1)
    q_a = q_a.reshape(D, 2, 4, 64).transpose(0, 2, 1, 3).reshape(D, 512)
    br_att = a["w_br_att"][0].reshape(2, 4, 64, D).transpose(1, 0, 2, 3).reshape(512, D)
    mem_k, mem_v = np.split(a["w_mem_kv"][0], 2, 1)
    up, gate = (blocks(x) for x in np.split(a["w_up"][0], 2, 1))
    w2 = a["w_in_2"][0]
    cuts = np.cumsum([384, 256, 32, 512, 512, 512, 512, 512, 256, 32, 8, 1024])
    q_lat, c_kv, k_rope, z_a, q_b, k_b, v_b, z_b, q_idx, k_idx, w_idx, gate_a2, gate_b2 = np.split(w2, cuts, 1)
    uq = a["w_uq_2"][0].reshape(384, 8, 96)
    uq = np.concatenate([uq[:, :, :64].reshape(384, 512), uq[:, :, 64:].reshape(384, 256)], 1)
    ukv = a["w_ukv_2"][0].reshape(256, 8, 128)
    ukv_k, ukv_v = ukv[:, :, :64].reshape(256, 512), ukv[:, :, 64:].reshape(256, 512)
    parts = {
        "g_r": blocks(g_r),
        "q_a": blocks(q_a), "k_a": blocks(k_a), "v_a": blocks(v_a),
        "rec_mix": mixed(gate_r, a["w_br_rec"][0]), "att_mix": mixed(gate_a, br_att),
        "mix_out": blocks(a["w_mix_out"][0]),
        "mem_o": blocks(a["w_mem_o"][0]),
        "up": np.stack([gate, up], 1).reshape(-1, P, SLOT),
        "down": blocks(a["w_down"][0], 3 * SLOT).reshape(DC, P, 3, SLOT).transpose(0, 2, 1, 3).reshape(-1, P, SLOT),
        "q_idx": blocks(q_idx), "k_idx": blocks(np.tile(k_idx, (1, 4))), "w_idx": blocks(wide(w_idx)),
        "q_lat": blocks(q_lat), "c_kv": blocks(c_kv), "k_rope": blocks(np.tile(k_rope, (1, 4))),
        "uq": per_slot(blocks(uq), 2), "ukv_k": per_slot(blocks(ukv_k), 2), "ukv_v": per_slot(blocks(ukv_v), 2),
        "z_a": blocks(z_a), "q_b": blocks(q_b), "k_b": blocks(k_b), "v_b": blocks(v_b), "z_b": blocks(z_b),
        "w_turn": np.zeros((0, P, SLOT), np.float32),
        "a_mix": mixed(gate_a2, a["w_o_a_2"][0]), "b_mix": mixed(gate_b2, a["w_o_b_2"][0]), "out2": blocks(a["w_out_2"][0]),
    }
    for h in range(HG_HEADS):
        cs = slice(P * h, P * h + P)
        parts[f"head{h}"] = np.concatenate([blocks(w[:, cs]) for w in (fz_f, fz_b, q_r, i_r)], 0)
    for h in range(MEM_HEADS):
        cs = slice(256 * h, 256 * h + 256)
        parts[f"mem{h}"] = np.concatenate([blocks(w[:, cs]) for w in (mem_k, mem_v, a["w_mem_q"][0])], 0)
    out = [parts[name] for name, _ in STREAM]
    n = sum(len(x) for x in out)
    return np.concatenate(out + [np.zeros((SLOTS - n, P, SLOT), np.float32)], 0)


def columns(x):
    return np.asarray(x).reshape(-1, P).T


def feature_vectors(a):
    inv = np.zeros((P, 1), np.float32)
    freq = (1.0 / (np.float32(ROPE_THETA) ** (np.arange(0, 16, 2, dtype=np.float32) / np.float32(16)))).astype(np.float32)
    for g in (0, 64):
        for r in range(2):
            inv[g + ROT_HALF * r:g + ROT_HALF * (r + 1), 0] = freq
    conv = a["conv_w"][0].reshape(3, FC, P).transpose(2, 1, 0).reshape(P, 3 * FC)
    lower = a["lower_bounds"].reshape(2, 2, HG_HEADS, P).transpose(3, 0, 1, 2).reshape(P, 16)
    named = {n: columns(a[n]) for n, _ in [("norm_mix", 0), ("norm_mem", 0), ("norm_mem_kv", 0), ("norm_ffn", 0),
                                            ("final_norm", 0), ("norm_g_2", 0), ("final_g_2", 0), ("g_q_lat_2", 0),
                                            ("g_kv_lat_2", 0), ("hg_norm", 0), ("conv_b", 0)]}
    named.update(conv_w=conv, lower=lower, inv_freq=inv)
    return np.concatenate([named[n] for n in VEC], 1)


def features_first(x):
    x = np.asarray(x)[0]
    return np.ascontiguousarray(x.T.reshape(-1, P, x.shape[0]).transpose(1, 0, 2))


def kernel(**inputs):
    import concourse.bacc as bacc
    from concourse.bass_utils import run_bass_kernel_spmd

    a = {k: np.asarray(v) for k, v in inputs.items()}
    const_r, const_a = constants_a()
    arrays = {
        "stream": weight_stream(a), "xT": features_first(a["x"]), "memT": features_first(a["mem"]),
        "pos": a["positions"].astype(np.int32).reshape(S), "vecs": feature_vectors(a),
        "ident": np.eye(P, dtype=np.float32), "const_r": const_r, "const_a": const_a, "const_d": constants_d(),
        "sink": a["attn_sink"].reshape(8), "relb": a["rel_bias_2"],
    }
    arrays = {k: np.ascontiguousarray(v) for k, v in arrays.items()}
    nc = bacc.Bacc("TRN2", target_bir_lowering=False, num_devices=1, dynamic_dma_scratch_size=1024)
    ins = [nc.dram_tensor(k, v.shape, mybir.dt.from_np(v.dtype), kind="ExternalInput").ap() for k, v in arrays.items()]
    gvec = nc.dram_tensor("gvec", (8, P, TOEP), F32).ap()
    outT = nc.dram_tensor("outT", (P, DC, S), F32, kind="ExternalOutput").ap()
    build(nc, *ins, gvec, outT)
    r = run_bass_kernel_spmd(nc, [arrays], core_ids=[0])
    y = r.results[0]["outT"]
    return np.ascontiguousarray(y.transpose(2, 1, 0).reshape(1, S, D))
```

```python
from contextlib import ExitStack

import numpy as np

import concourse.bass as bass
from concourse import mybir

F32, F32R, I32 = mybir.dt.float32, mybir.dt.float32r, mybir.dt.int32
ACT = mybir.ActivationFunctionType
ALU = mybir.AluOpType
AX = mybir.AxisListType

P = 128
S = 512
ST = S // P
D = 1024
DC = D // P
MEM = 256
EPS = 1e-6
NEG = -1e30
TAKEN = -3e38
LOWEST = -3.4e38

HG_HEADS = 4
HG_SCALE = 128 ** -0.5
LEVELS = 7
HALF = P // 2
LQ = LEVELS * HALF
UNITS = ST + 1
LN_FLOOR = 1e-19

ATT_SCALE = 64 ** -0.5
ROT_HALF = 8
ROPE_THETA = 500000.0
MEM_HEADS = 4
MEM_SCALE = 256 ** -0.5
FF = 2816
FC = FF // P

MLA_SCALE = 96 ** -0.5
IDX_HEADS = 8
IDX_SCALE = 32 ** -0.5
IDXW_SCALE = IDX_HEADS ** -0.5
TOPK = 128
REL_BUCKETS = 32
REL_MAX = 128
TOEP = 640

BLK = 8
RAW = 4
SPL = 2

TWO_PI = 2 * np.pi
PI_A = 6.28125
PI_B = int((TWO_PI - PI_A) * 2 ** 20) / 2 ** 20
PI_C = TWO_PI - PI_A - PI_B
ROUND = 12582912.0

VALUES = [1, 1, 0, 1, 0, 1, 0, 0]
RAW_AT, TURN_AT = [0, 1, 3, 5], [2, 4, 6, 7]
MIX = [1, 1, 1, 0] * (DC // 2)
MEM_HEAD = [1, 1, 1, 1, 1, 0, 1, 0]
HEAD = [1, 1, 1, 1, 0]
STREAM = [
    ("head0", HEAD), ("head1", HEAD), ("head2", HEAD), ("head3", HEAD), ("q_a", [1] * 4),
    ("q_turn", [0] * 2), ("k_a", [1]), ("q_turn2", [0] * 2), ("g_first", [1]), ("v_a", [1, 0]),
    ("k_turn", [0]), ("g_rest", [1] * 3),
    ("rec_mix", MIX), ("att_mix", MIX), ("mix_out", [1] * DC),
    ("mem0", MEM_HEAD), ("mem1", MEM_HEAD), ("mem2", MEM_HEAD), ("mem3", MEM_HEAD), ("mem_o", [1] * DC),
    ("up", [1] * (2 * FC)), ("down", [3] * DC),
    ("q_idx", [1] * 2), ("w_idx", [1]), ("k_idx", [1]), ("w_turn", [0]), ("q_lat", [1] * 3), ("c_kv", [1] * 2),
    ("k_rope", [1]), ("z_a", [1] * 4), ("uq", [1, 0] * 3), ("ukv_k", [1, 0] * 2), ("ukv_v", [1, 0, 0, 0] * 2),
    ("q_b", [1] * 4), ("k_b", [1] * 4), ("v_b", VALUES), ("z_b", [1] * 4),
    ("a_mix", MIX), ("b_mix", MIX), ("out2", [1] * DC),
]
FIRST, ENDS = {}, []
_slots = 0
for _name, _need in STREAM:
    FIRST[_name] = len(ENDS)
    for _k in _need:
        _slots += _k
        ENDS.append(_slots)
SLOTS = -(-_slots // RAW) * RAW


def running(table):
    at, n = {}, 0
    for name, count in table:
        at[name] = n
        n += count
    return at, n


def q_turn(c):
    return FIRST["q_turn"] + c if c < 2 else FIRST["q_turn2"] + c - 2


def g_r(c):
    return FIRST["g_rest"] + c - 1 if c else FIRST["g_first"]


SPLIT, _ = running([("mix", DC), ("rec", 4), ("att", 4), ("merged", DC), ("memory", DC), ("mem", DC),
                    ("mem_out", DC), ("ffn", DC), ("hidden", FC), ("mix2", DC), ("q_lat", 3),
                    ("c_kv", 2), ("y_a", 4), ("y_b", 4), ("merged2", DC)])
NORMS = ["mix", "memory", "mem", "ffn", "final", "mix2", "q_lat", "c_kv", "out"]
CHUNKS = {n: {"q_lat": 3, "c_kv": 2}.get(n, DC) for n in NORMS}
SQUARE, _ = running([(n, CHUNKS[n]) for n in NORMS])
ADDED, _ = running([(n, CHUNKS[n] - 1) for n in NORMS])
TURNED, _ = running([(f"head{h}", 1) for h in range(HG_HEADS)] + [("v_a", 1)] + [(f"mem{h}", 2) for h in range(MEM_HEADS)]
                    + [("w_idx", 1), ("ukv_v", 4), ("v_b", 4)])
SILU, _ = running([("q_r", 4), ("g_r", 4), ("z_a", 4), ("z_b", 4)])
HALF_DONE, _ = running([("rec_mix", DC // 2), ("att_mix", DC // 2), ("uq", 3), ("ukv_k", 2), ("ukv_v", 2),
                        ("a_mix", DC // 2), ("b_mix", DC // 2)])
ROTATE, _ = running([("first", 5), ("second", 3)])

def band(i):
    return max(0, i - 1), min(ST, i + 2)


def causal(i):
    return 0, i + 1


KINDS = {
    "window": dict(heads=[0, 4, 1, 5, 2, 6, 3, 7], keys=band, per_round=8, banks=1, out="att"),
    "memory": dict(heads=list(range(MEM_HEADS)), keys=lambda i: (0, 2), per_round=4, banks=2, out="mem_out"),
    "mla": dict(heads=list(range(8)), keys=causal, per_round=8, banks=1, out="y_a"),
    "dsa": dict(heads=list(range(8)), keys=causal, per_round=8, banks=1, out="y_b"),
}
KINDS["window"]["serves"] = [(1, slice(0, S)), (0, slice(0, 2 * P)), (2, slice(P, S)), (3, slice(2 * P, S))]
KINDS["memory"]["serves"] = [(0, slice(0, S)), (1, slice(0, S))]
for _n in ("mla", "dsa"):
    KINDS[_n]["serves"] = [(t, slice(P * t, S)) for t in range(ST)]
_u = 0
for _k in KINDS.values():
    _k["units"] = [(h, i) for h in _k["heads"] for i in range(ST)]
    _k["first"], _k["first_head"] = _u, _u // ST
    _u += len(_k["units"])
for _n, _k in KINDS.items():
    _k["ring"] = 2 if _n in ("window", "memory") else 1
DSA_ITEMS = [("q_b", c) for c in range(4)] + [("k_b", c) for c in range(4)] + [("v_b", j) for j in range(8)] + [
    ("z_b", c) for c in range(4)]


def dsa_item(x):
    return DSA_ITEMS[2 + x // 2] if x % 2 == 0 else (None, 0)


STEP_AT = [32 * i // 12 for i in range(12)]


def mix_steps(x):
    return [2 + STEP_AT.index(x)] if x in STEP_AT else []


def mix_pairs(x):
    return [k // 4 for k in mix_steps(x) if k % 4 == 3]


NORM_LAG, TURN_LAG, PV_LAG, OUT_LAG = 1, 3, 5, 7

VEC, VEC_COLS = running([
    ("norm_mix", 8), ("norm_mem", 8), ("norm_mem_kv", 8), ("norm_ffn", 8), ("final_norm", 8),
    ("norm_g_2", 8), ("final_g_2", 8), ("g_q_lat_2", 3), ("g_kv_lat_2", 2), ("hg_norm", 4),
    ("conv_w", 3 * FC), ("conv_b", FC), ("lower", 16), ("inv_freq", 1)])
CONST_R = [("Qf", LQ), ("Qb", LQ), ("Kf", LQ), ("Kb", LQ), ("Pf", P), ("Uf", P), ("Pb", P), ("Ub", P), ("all", P)]
CONST_A = [("level", 8 * P), ("perm", P), ("band", 3 * P)]
CONST_D = [("perm", P), ("cos", S), ("sin", S), ("causal", S), ("onehot", TOEP), ("group", 4)]
AT_R, COLS_R = running(CONST_R)
AT_A, COLS_A = running(CONST_A)
AT_D, COLS_D = running(CONST_D)


def build(nc, stream, xT, memT, pos, vecs, ident_d, const_r, const_a, const_d, sink_d, relb_d, gvec, x1_d, outT):
    with ExitStack() as ctx:
        def sem(name):
            return ctx.enter_context(nc.semaphore(name))

        top = [1152]

        def place(name, shape, dt=F32, at=None):
            size = 4 * int(np.prod(shape[1:]))
            off = -(-top[0] // 32) * 32 if at is None else at
            assert off + size <= 229344, (name, off + size)
            if at is None:
                top[0] = off + size
            return nc.alloc_sbuf_tensor_at(name, shape, dt, offset=off)

        hT0 = top[0]
        hT = place("hT", [P, DC, S])
        nH = place("nH", [P, DC, S], F32R)
        nL = place("nL", [P, DC, S], F32R)
        ring = place("ring", [P, RAW, BLK * P])
        wH = place("wH", [P, SPL, BLK * P], F32R)
        wL = place("wL", [P, SPL, BLK * P], F32R)
        ident = place("ident", [P, P])
        ones = place("ones", [P, P])
        vec = place("vec", [P, VEC_COLS])
        sq0 = -(-top[0] // 32) * 32
        sq = place("sq", [P, 2, S])
        sums0 = -(-top[0] // 32) * 32
        sums = place("sums", [P, S])
        std = place("std", [P, S])
        rstd = place("rstd", [P, S])
        nt = place("nt", [P, 2, S])
        sgb = place("sgb", [P, 2, S])
        vraw = place("vraw", [P, 2, S])
        stat = place("stat", [P, 4, 8])
        lbs = place("lbs", [P, 64])
        sinks = place("sinks", [P, 8])
        tick = place("tick", [P, 2])
        warm = place("warm", [P, len(NORMS)])
        OVER = top[0]

        cA = place("cA", [P, COLS_A])
        cR = place("cR", [P, COLS_R], F32R)
        qT = place("qT", [P, HG_HEADS, S])
        kk = place("kk", [P, 2, HG_HEADS, S])
        vr = place("vr", [P, ST, S])
        qa0 = top[0]
        qa = place("qa", [P, 4, S])
        ka = place("ka", [P, S], at=sums0)
        va = place("va", [P, ST, P])
        cosA = place("cosA", [P, S])
        sinA = place("sinA", [P, S])
        gla0 = top[0]
        lf = place("lf", [P, 2, S])
        lftH = place("lftH", [P, 2, ST, P], F32R)
        lftL = place("lftL", [P, 2, ST, P], F32R)
        landing = place("landing", [P, COLS_R], at=top[0])
        E = place("E", [P, 2, 4, S])
        X = place("X", [P, 2, 2, LEVELS * P])
        Sg = place("Sg", [P, ST, S])
        kfb = place("kfb", [P, S])
        lev = place("lev", [P, 8, P])
        gr = place("gr", [P, 4, S], at=gla0 + 4 * (4 * S + 2 * S + 8 * S))
        gs = place("gs", [P, 4, S], at=gla0 + 4 * (4 * S + 2 * S + 8 * S + 4 * S))
        top[0] = gla0
        recH = place("recH", [P, 4, S], F32R)
        recL = place("recL", [P, 4, S], F32R)
        attH = place("attH", [P, 4, S], F32R)
        attL = place("attL", [P, 4, S], F32R)
        wx0 = top[0]
        wx = place("wx", [P, 4, S])
        wPT = place("wPT", [P, 2, ST, S])
        posi = place("posi", [P, S], I32, at=sq0)
        ang = place("ang", [P, S], at=sq0 + 4 * S)
        turn = place("turn", [P, S], at=sums0 + 4 * S)
        mtA = place("mtA", [P, DC, S], at=qa0 - 4 * 12 * S)
        sgA = place("sgA", [P, 4, S], at=qa0 - 4 * 4 * S)
        mgH = place("mgH", [P, DC, S], F32R, at=qa0)
        mgL = place("mgL", [P, DC, S], F32R, at=wx0)

        top[0] = OVER
        memx = place("memx", [P, DC, MEM])
        mnH = place("mnH", [P, DC, MEM], F32R)
        mnL = place("mnL", [P, DC, MEM], F32R, at=wx0 + 4 * DC * S)
        addA = place("addA", [P, 2, S])
        mk = place("mk", [P, DC, MEM])
        mv = place("mv", [P, 2, D])
        mq = place("mq", [P, DC, S])
        moH = place("moH", [P, DC, S], F32R)
        moL = place("moL", [P, DC, S], F32R)
        mx = place("mx", [P, 4, S])
        mPT = place("mPT", [P, 2, 2, S])
        nomask = place("nomask", [P, MEM])
        assert top[0] <= wx0 + 4 * DC * S

        top[0] = OVER
        aH = place("aH", [P, FC, S], F32R)
        aL = place("aL", [P, FC, S], F32R)
        gpad = place("gpad", [P, 2, S + 2])
        cv = place("cv", [P, 2, S])
        fu = place("fu", [P, 2, S])
        sums2 = place("sums2", [P, S], at=229344 - 4 * S)

        top[0] = OVER
        cD = place("cD", [P, COLS_D])
        selm = place("selm", [P, 9 * P])
        wtok = place("wtok", [P, ST, IDX_HEADS])
        gv = place("gv", [8, TOEP])
        relb = place("relb", [REL_BUCKETS, 8])
        best = place("best", [P, 8])
        rl = place("rl", [P, 2, S])
        late0 = top[0]
        yaH = place("yaH", [P, 4, S], F32R)
        yaL = place("yaL", [P, 4, S], F32R)
        dx = place("dx", [P, 4, S])
        dPT = place("dPT", [P, 1, ST, S])
        d0 = top[0]
        top[0] = late0
        qlat = place("qlat", [P, 3, S])
        ckv = place("ckv", [P, 2, S])
        qlH = place("qlH", [P, 3, S], F32R)
        qlL = place("qlL", [P, 3, S], F32R)
        ckH = place("ckH", [P, 2, S], F32R)
        ckL = place("ckL", [P, 2, S], F32R)
        qi = place("qi", [P, 2, S], at=d0 + 4 * (4 + 2 + 4 + 4 + 4 + 4 + 6) * S)
        assert top[0] <= d0
        top[0] = d0
        qn = place("qn", [P, 4, S])
        qp = place("qp", [P, 2, S])
        kn = place("kn", [P, 4, S])
        kpz = place("kpz", [P, 4, S])
        vA = place("vA", [P, ST, S])
        za = place("za", [P, 4, S])
        b0 = top[0]
        kp = place("kp", [P, S])
        ki = place("ki", [P, S])
        kiz = place("kiz", [P, 4, S])
        top[0] = b0
        qb = place("qb", [P, 4, S])
        kb = place("kb", [P, 4, S])
        vB = place("vB", [P, ST, S], at=hT0)
        zb = place("zb", [P, 4, S], at=hT0 + 16 * S)
        top[0] = d0
        toep = place("toep", [P, 4, S])
        ybH = place("ybH", [P, 4, S], F32R)
        ybL = place("ybL", [P, 4, S], F32R)
        mtD = place("mtD", [P, DC, S])
        sgD = place("sgD", [P, 2, S])
        assert top[0] <= b0
        addD = place("addD", [P, 2, S], at=d0)
        mg2L = place("mg2L", [P, DC, S], F32R, at=b0)
        mg2H = place("mg2H", [P, DC, S], F32R, at=late0 + 4 * 8 * S)

        pair = [ctx.enter_context(nc.psum_tensor(f"pair{i}", [P, 2 * S], F32)) for i in range(4)]

        def bank(b):
            return pair[b // 2][:, S * (b % 2):S * (b % 2) + S]

        def vcol(name, c):
            i = VEC[name] + c
            return vec[:, i:i + 1]

        def c_a(name, a, b):
            return cA[:, AT_A[name] + a:AT_A[name] + b]

        def c_r(name, a=0, b=P):
            return cR[:, AT_R[name] + a:AT_R[name] + b]

        def c_d(name, a, b):
            return cD[:, AT_D[name] + a:AT_D[name] + b]

        landed = [sem(f"landed{i}") for i in range(RAW)]
        high_done = sem("high_done")
        split_done = sem("split_done")
        multiplied = sem("multiplied")
        freed = [sem("freed0"), sem("freed1")]
        phase = sem("phase")
        ld_vec, ld_a, ld_pos, ld_mem, ld_d, ld_toep, st_gvec, st_out = (
            sem(n) for n in ("ld_vec", "ld_a", "ld_pos", "ld_mem", "ld_d", "ld_toep", "st_gvec", "st_out"))
        ones_set, borders, angle_s, angle_c, tables, lb_diff, lb_exp = (
            sem(n) for n in ("ones_set", "borders", "angle_s", "angle_c", "tables", "lb_diff", "lb_exp"))
        ld_late = [sem(f"ld_late{h}") for h in range(4)]
        ld_x = [sem(f"ld_input{i}") for i in range(DC // 2)]
        half_done = sem("half_done")
        hg_made, var_made = sem("hg_made"), sem("var_made")
        ld_r, st_x1, ld_x1 = sem("ld_r"), sem("st_x1"), sem("ld_x1")
        dve_own = sem("dve_own")
        sq_made, sq_added, sum_done, std_made, r_made = (
            sem(n) for n in ("sq_made", "sq_added", "sum_done", "std_made", "r_made"))
        v_turned = sem("v_turned")
        nt_made, nh_made, nl_made = sem("nt_made"), sem("nh_made"), sem("nl_made")
        sg_made = sem("sg_made")
        x1_made, y_made = sem("x1_made"), sem("y_made")
        rot_done, rot_used, rotated = sem("rot_done"), sem("rot_used"), sem("rotated")
        f_made, lf_made, lf_turned, lh_made, lft_made, zero_one = (
            sem(n) for n in ("f_made", "lf_made", "lf_turned", "lh_made", "lft_made", "zero_one"))
        dec_done, exp_done, x_made, k_made = (sem(n) for n in ("dec_done", "exp_done", "x_made", "k_made"))
        kiz_made, kpz_made = sem("kiz_made"), sem("kpz_made")
        sc_done, masked, s_made = sem("sc_done"), sem("masked"), sem("s_made")
        cross_done, cross_out, o_done, o_out = (sem(n) for n in ("cross_done", "cross_out", "o_done", "o_out"))
        o_sq, o_sum, o_std, o_norm = (sem(n) for n in ("o_sq", "o_sum", "o_std", "o_norm"))
        conv_made, fsg_made = sem("conv_made"), sem("fsg_made")
        a_sc, a_max, a_neg, a_exp, a_prob, a_turn, a_pt, a_pv = (
            sem("a_" + n) for n in ("sc", "max", "neg", "exp", "prob", "turn", "pt", "pv"))
        t_sc, t_relu, t_acc = sem("t_sc"), sem("t_relu"), sem("t_acc")
        gv_done, gv_out = sem("gv_done"), sem("gv_out")

        def out_of_bank(eng, g):
            eng.wait_ge(freed[g % 2], g // 2 + 1)

        block = ctx.enter_context(nc.Block())

        @block.sync
        def _(sp):
            for c in range(0, DC, 2):
                sp.dma_start(hT[:, c:c + 2, :], xT[:, c:c + 2, :]).then_inc(ld_x[c // 2], 16)
            slots = stream.rearrange("(n r) p m -> n r p m", r=RAW)
            for r in range(RAW):
                if r == 1:
                    sp.wait_ge(ld_x[-1], 16)
                sp.dma_start(ring[:, r, :], slots[0, r]).then_inc(landed[r], 16)
            with sp.Fori(0, SLOTS // RAW - 1) as n:
                for r in range(RAW):
                    sp.wait_ge(split_done, RAW * n + r + 1)
                    sp.dma_start(ring[:, r, :], slots[n + 1, r]).then_inc(landed[r], 16)

        @block.gpsimd
        def _(pool):
            pool.memset(ones[:, :], 1.0).then_inc(ones_set, 1)
            pool.memset(tick[:, :], 0.0).then_inc(ones_set, 1)
            pool.wait_ge(ones_set, 2)

            def split(r, turn_, n, used):
                pool.wait_ge(landed[r], 16 * turn_)
                if used is not None:
                    pool.wait_ge(multiplied, used)
                pool.tensor_tensor(tick[:, 1:2], tick[:, 0:1], tick[:, 0:1], ALU.add).then_inc(high_done, 1)
                pool.tensor_scalar(wH[:, r % SPL, :], ring[:, r, :], 1.0, 0.0, ALU.mult, ALU.add).then_inc(high_done, 1)
                pool.wait_ge(high_done, 2 * n)
                pool.tensor_tensor(wL[:, r % SPL, :], ring[:, r, :], wH[:, r % SPL, :].bitcast(F32),
                                   ALU.subtract).then_inc(split_done, 1)

            for r in range(RAW):
                split(r, 1, r + 1, r - SPL + 1 if r >= SPL else None)
            with pool.Fori(1, SLOTS // RAW) as n:
                for r in range(RAW):
                    split(r, n + 1, RAW * n + r + 1, RAW * n + r - SPL + 1)

        @block.tensor
        def _(pe):
            mm = nc.tensor.matmul
            n_slot, n_phase = [0], [0]

            def past_phase():
                n_phase[0] += 1
                pe.drain().then_inc(phase, 1)

            def barrier():
                past_phase()
                pe.wait_ge(phase, 3 * n_phase[0])

            def norm_sum(name, width=S):
                pe.wait_ge(sq_added, ADDED[name] + CHUNKS[name] - 1)
                if NORMS.index(name):
                    pe.wait_ge(std_made, NORMS.index(name))
                mm(bank(7)[:, :width], ones[:, :], sums[:, :width], start=True, stop=True).then_inc(sum_done, 1)

            def open_slot():
                r = n_slot[0] % SPL
                n_slot[0] += 1
                pe.wait_ge(split_done, n_slot[0])
                return r

            def open_bank(g):
                if g >= 2:
                    out_of_bank(pe, g - 2)
                return bank(g % 2)

            def three(out, a, b, first, last):
                mm(out, a[0], b[0], start=first, stop=False)
                mm(out, a[0], b[1], start=False, stop=False)
                return mm(out, a[1], b[0], start=False, stop=last)

            def weight(r, j):
                return wH[:, r, P * j:P * j + P], wL[:, r, P * j:P * j + P]

            def parts(h, l, n):
                return [(h[:, k, :], l[:, k, :]) for k in range(n)]

            def project(stage, c0, n, xs, width=S, inputs=None):
                for c in range(c0, c0 + n):
                    out = open_bank(FIRST[stage] + c)[:, :width]
                    for k, x in enumerate(xs):
                        if k % BLK == 0:
                            r = open_slot()
                        if inputs is not None and c == c0:
                            pe.wait_ge(nl_made, SPLIT[inputs] + k + 1)
                        last = three(out, weight(r, k % BLK), x, k == 0, k == len(xs) - 1)
                        if k % BLK == BLK - 1 or k == len(xs) - 1:
                            last.then_inc(multiplied, 1)

            def turn_chunk(stage, raw, at, k, tiles=ST):
                out_of_bank(pe, FIRST[stage] + raw)
                out = open_bank(FIRST[stage] + at)
                for t in range(tiles):
                    cs = slice(P * t, P * t + P)
                    last = nc.tensor.transpose(out[:, cs], vraw[:, k % 2, cs], ident[:, :])
                last.then_inc(v_turned, 1)

            def values(stage, j):
                if j in RAW_AT:
                    project(stage, j, 1, n_parts)
                else:
                    c = TURN_AT.index(j)
                    turn_chunk(stage, RAW_AT[c], j, TURNED[stage] + c)

            def halves(stage, first, n_slots, k_n, xs, then=None):
                for s in range(n_slots):
                    g = FIRST[stage] + first(s)
                    r = open_slot()
                    for half in range(2):
                        out = open_bank(g + half)
                        for k in range(k_n):
                            last = three(out, weight(r, k_n * half + k), xs[k], k == 0, k == k_n - 1)
                        if half == 0:
                            last.then_inc(half_done, 1)
                    last.then_inc(multiplied, 1)
                    if then is not None:
                        then(s)

            def rotate(name, n, src, raw, perm, at=None):
                m = ROTATE[name] + n
                out_of_bank(pe, raw)
                if at is not None:
                    out = open_bank(at)
                else:
                    if n >= 2:
                        pe.wait_ge(rot_used, n - 1)
                    out = bank(4 + m % 2)
                mm(out, perm, src, start=True, stop=True).then_inc(rot_done, 1)

            def head_step(h, j):
                if j < 4:
                    project(f"head{h}", j, 1, n_parts, inputs="mix" if h + j == 0 else None)
                else:
                    turn_chunk(f"head{h}", 3, 4, TURNED[f"head{h}"])

            def half_step(h, half):
                g = FIRST[f"head{h}"] + 3
                if half == 0:
                    open_bank(g)
                    open_slot()
                r = (n_slot[0] - 1) % SPL
                for k in range(4 * half, 4 * half + 4):
                    last = three(bank(g % 2), weight(r, k), n_parts[k], k == 0, k == DC - 1)
                if half:
                    last.then_inc(multiplied, 1)

            def recurrence(beside):
                def sums_of(out, d, i, m, first=True, last=True):
                    mm(out, lftH[:, d, i, :], m, start=first, stop=False)
                    return mm(out, lftL[:, d, i, :], m, start=False, stop=last)

                def turn_logs(h):
                    pe.wait_ge(lf_made, h + 1)
                    if h:
                        pe.wait_ge(exp_done, UNITS * h)
                    for d in range(2):
                        for i in range(ST):
                            cs = slice(P * i, P * i + P)
                            last = nc.tensor.transpose(bank(2 + d)[:, cs], lf[:, d, cs], ident[:, :])
                    last.then_inc(lf_turned, 1)

                def cross_decays(h):
                    if h == 0:
                        pe.wait_ge(zero_one, 1)
                    pe.wait_ge(lft_made, h + 1)
                    for i in range(ST):
                        cs = slice(P * i, P * i + P)
                        d = 0 if i % 2 else 1
                        sums_of(bank(2)[:, cs], d, i, c_r("Pb" if d else "Pf"))
                        sums_of(bank(3)[:, cs], 1 - d, i, c_r("Uf" if d else "Ub"))
                        d = 0 if i >= 2 else 1
                        far = {3: 2, 0: 1}.get(i)
                        for b, dd, name in ((4, d, "Pb" if d else "Pf"), (5, 1 - d, "Uf" if d else "Ub")):
                            last = sums_of(bank(b)[:, cs], dd, i, c_r(name), last=far is None)
                            if far is not None:
                                last = sums_of(bank(b)[:, cs], dd, far, c_r("all"), first=False)
                    last.then_inc(dec_done, 1)

                def tile_decays(h, i):
                    if i == 1:
                        pe.wait_ge(cross_out, h + 1)
                    else:
                        pe.wait_ge(exp_done, UNITS * h + 1 + i)
                    for b, (d, name) in enumerate([(0, "Qf"), (1, "Qb"), (0, "Kf"), (1, "Kb")]):
                        last = sums_of(bank(2 + b)[:, :LQ], d, i, c_r(name, 0, LQ))
                    last.then_inc(dec_done, 1)

                def tile_scores(h, i):
                    n = ST * h + i
                    pe.wait_ge(x_made, UNITS * h + 2 + i)
                    if n:
                        pe.wait_ge(masked, n)
                    for l in range(LEVELS):
                        cs = slice(P * l, P * l + P)
                        mm(pair[3][:, cs], X[:, n % 2, 1, cs], X[:, n % 2, 0, cs], start=True, stop=True)
                    cs = slice(P * i, P * i + P)
                    if i == 0:
                        pe.wait_ge(k_made, h + 1)
                    mm(pair[3][:, P * LEVELS:], kfb[:, cs], qT[:, h, cs], start=True, stop=True).then_inc(sc_done, 1)

                def cross_scores(h):
                    b = (UNITS * h) % 2
                    pe.wait_ge(x_made, UNITS * h + 1)
                    pe.wait_ge(exp_done, UNITS * h + 2)
                    for j in range(ST):
                        if h and j == ST - 1:
                            pe.wait_ge(o_out, h)
                        out, cs, t = bank(2 + (j + 1) % ST), slice(P * j, P * j + P), j ^ 1
                        ts = slice(P * t, P * t + P)
                        mm(out[:, ts], E[:, b, 1, cs], E[:, b, 0, ts], start=True, stop=True)
                        far = slice(2 * P, 4 * P) if j < 2 else slice(0, 2 * P)
                        last = mm(out[:, far], E[:, b, 3, cs], E[:, b, 2, far], start=True, stop=True)
                    last.then_inc(cross_done, 1)

                def output(h):
                    pe.wait_ge(cross_out, h + 1)
                    pe.wait_ge(s_made, ST * (h + 1))
                    pe.wait_ge(exp_done, UNITS * (h + 1) + (2 if h + 1 < HG_HEADS else 0))
                    if h + 1 == HG_HEADS:
                        pe.wait_ge(o_sq, h)
                        for i in range(h):
                            last = mm(bank(3 + i), ones[:, :], kk[:, 0, i, :], start=True, stop=True)
                        last.then_inc(o_sum, 1)
                    for j in range(ST):
                        last = mm(bank(2), vr[:, j, P * h:P * h + P], Sg[:, j, :], start=j == 0, stop=j == ST - 1)
                    last.then_inc(o_done, 1)

                turn_logs(0)
                head_step(1, 0)
                cross_decays(0)
                head_step(1, 1)
                tile_decays(0, 0)
                for j in range(2, 5):
                    head_step(1, j)
                beside(0, 0)
                for h in range(HG_HEADS):
                    more = h + 1 < HG_HEADS
                    cross_scores(h)
                    tile_scores(h, 0)
                    tile_decays(h, 1)
                    beside(h, 1)
                    tile_decays(h, 2)
                    tile_scores(h, 1)
                    if more:
                        beside(h, 2)
                    else:
                        project("g_first", 0, 1, n_parts)
                    tile_decays(h, 3)
                    tile_scores(h, 2)
                    if more:
                        turn_logs(h + 1)
                    if h + 2 < HG_HEADS:
                        half_step(h + 2, 0)
                    else:
                        beside(h, 3 if more else 2)
                    tile_scores(h, 3)
                    if more:
                        cross_decays(h + 1)
                    if h + 2 < HG_HEADS:
                        half_step(h + 2, 1)
                    if not more:
                        beside(h, 3)
                    if more:
                        tile_decays(h + 1, 0)
                    beside(h, 4)
                    if more:
                        beside(h + 1, 0)
                    output(h)

            def attention(name, terms, value, probs, turned, beside=lambda x: None, after=lambda: None):
                kind = KINDS[name]
                units, u0, n = kind["units"], kind["first"], len(kind["units"])
                per, banks, k0 = kind["per_round"], kind["banks"], SPLIT[kind["out"]]

                def scores(x):
                    (h, i), u = units[x], u0 + x
                    a, b = kind["keys"](i)
                    if x >= 2:
                        pe.wait_ge(a_max, u - 1)
                    pairs = terms(h, i, slice(P * a, P * b))
                    for t, (w, m) in enumerate(pairs):
                        last = mm(bank(2 + u % 2)[:, :P * (b - a)], w, m, start=t == 0, stop=t == len(pairs) - 1)
                    last.then_inc(a_sc, 1)

                def turn_probs(x):
                    (h, i), u = units[x], u0 + x
                    a, b = kind["keys"](i)
                    pe.wait_ge(a_prob, u + 1)
                    if x >= 2:
                        pe.wait_ge(a_pt, u - 1)
                    for t in range(b - a):
                        cs = slice(P * t, P * t + P)
                        last = nc.tensor.transpose(bank(4 + u % 2)[:, cs], probs[:, u % 4, cs], ident[:, :])
                    last.then_inc(a_turn, 1)

                def weigh(j):
                    h = kind["heads"][j]
                    rnd = ST * j // per
                    pe.wait_ge(a_pt, u0 + ST * (j + 1))
                    ahead = 2 if banks == 1 else 1
                    if ST * j % per == 0 and rnd >= ahead:
                        pe.wait_ge(nt_made, k0 + banks * (rnd - ahead + 1))
                    for bk in range(banks):
                        out = bank(6 + (rnd % 2 if banks == 1 else bk))
                        for n_t, (t, qs) in enumerate(kind["serves"]):
                            w, rows = value(h, t, bk)
                            last = mm(out[rows, qs], w, turned[:, j % kind["ring"], t, qs], start=n_t == 0,
                                      stop=n_t == len(kind["serves"]) - 1)
                    last.then_inc(a_pv, 1)

                for x in range(n + PV_LAG):
                    if x < n:
                        scores(x)
                        beside(x)
                    elif x == n:
                        after()
                    if 0 <= x - TURN_LAG < n:
                        turn_probs(x - TURN_LAG)
                    y = x - PV_LAG
                    if y >= 0 and units[y][1] == ST - 1:
                        weigh(y // ST)

            def mix_step(stage, k, branch):
                if k % 4 < 2:
                    project(stage, k, 1, n_parts)
                    return
                half = k % 4 - 2
                out = open_bank(FIRST[stage] + k)
                if half == 0:
                    open_slot()
                r = (n_slot[0] - 1) % SPL
                for i in range(4):
                    last = three(out, weight(r, 4 * half + i), branch[i], i == 0, i == 3)
                last.then_inc(multiplied if half else half_done, 1)

            def head_rows(h):
                return slice(64 * (h % 2), 64 * (h % 2) + 64)

            n_parts = parts(nH, nL, DC)

            pe.wait_ge(ones_set, 2)
            norm_sum("mix")
            for j in range(5):
                if j == 4:
                    pe.wait_ge(ld_a, 48)
                head_step(0, j)

            def head_beside(h, j):
                if h + 2 < HG_HEADS:
                    head_step(h + 2, j)
                elif h + 2 == HG_HEADS and j < 4:
                    project("q_a", j, 1, n_parts)
                elif h + 1 == HG_HEADS:
                    if j == 1:
                        project("k_a", 0, 1, n_parts)
                    if j < 2:
                        for c in (2 * j, 2 * j + 1):
                            rotate("first", c, qa[:, c, :], FIRST["q_a"] + c, c_a("perm", 0, P), q_turn(c))
                    elif j == 2:
                        project("v_a", 0, 1, n_parts)
                    elif j == 3:
                        turn_chunk("v_a", 0, 1, TURNED["v_a"])
                        rotate("first", 4, ka[:, :], FIRST["k_a"], c_a("perm", 0, P), FIRST["k_turn"])
                    elif j == 4:
                        project("g_rest", 0, 1, n_parts)

            recurrence(head_beside)
            pe.wait_ge(o_sq, HG_HEADS)
            pe.wait_ge(o_std, 1)
            mm(bank(3), ones[:, :], kk[:, 0, HG_HEADS - 1, :], start=True, stop=True).then_inc(o_sum, 1)
            project("g_rest", 1, 2, n_parts)
            rec, att = parts(recH, recL, 4), parts(attH, attL, 4)
            mix_step("rec_mix", 0, rec)
            mix_step("rec_mix", 1, rec)
            pe.wait_ge(o_std, 2)
            pe.wait_ge(rotated, 5)

            def window_terms(h, i, keys):
                rows = slice(64 * (h // 4), 64 * (h // 4) + 64)
                return [(qa[rows, h % 4, P * i:P * i + P], ka[rows, keys])]

            def window_value(h, t, bk):
                rows = slice(64 * (h // 4), 64 * (h // 4) + 64)
                return va[:, t, rows], rows

            def rec_beside(x):
                for k in mix_steps(x):
                    if k == 2:
                        pe.wait_ge(nl_made, SPLIT["rec"] + 4)
                    mix_step("rec_mix", k, rec)

            attention("window", window_terms, window_value, wx, wPT, rec_beside, lambda: mix_step("rec_mix", 14, rec))
            mix_step("rec_mix", 15, rec)
            past_phase()
            for k in range(16):
                mix_step("att_mix", k, att)
            norm_sum("memory", MEM)
            project("mix_out", 0, DC, parts(mgH, mgL, DC), inputs="merged")

            mn_parts = parts(mnH, mnL, DC)

            def mem_step(h, j):
                stage, k0 = f"mem{h}", TURNED[f"mem{h}"]
                if j in (5, 7):
                    c = (j - 5) // 2
                    turn_chunk(stage, 2 + c, j, k0 + c, 2)
                elif j < 4:
                    project(stage, j, 1, mn_parts, MEM)
                else:
                    project(stage, j, 1, n_parts, inputs="mem" if h == 0 and j == 4 else None)

            pe.wait_ge(nl_made, SPLIT["memory"] + DC)
            for j in range(8):
                mem_step(0, j)
                if j == 1:
                    norm_sum("mem")

            def mem_beside(x):
                h = x // ST + 1
                if h < MEM_HEADS:
                    for j in ((0, 1), (2, 3), (4, 5), (6, 7))[x % ST]:
                        mem_step(h, j)

            def mem_terms(h, i, keys):
                if i == 0:
                    for j in (6, 7):
                        out_of_bank(pe, FIRST[f"mem{h}"] + j)
                return [(mq[:, 2 * h + b, P * i:P * i + P], mk[:, 2 * h + b, :]) for b in range(2)]

            def mem_value(h, t, bk):
                return mv[:, t, 256 * h + P * bk:256 * h + P * bk + P], slice(0, P)

            attention("memory", mem_terms, mem_value, mx, mPT, mem_beside)
            project("mem_o", 0, DC, parts(moH, moL, DC), inputs="mem_out")

            project("up", 0, 1, n_parts, inputs="ffn")
            norm_sum("ffn")
            project("up", 1, 2 * FC - 1, n_parts)
            project("down", 0, DC, parts(aH, aL, FC), inputs="hidden")
            pe.wait_ge(sq_added, ADDED["mix2"] + CHUNKS["mix2"] - 1)
            norm_sum("final")
            mm(bank(6), ones[:, :], sums2[:, :], start=True, stop=True).then_inc(sum_done, 1)

            pe.wait_ge(ld_d, 32)
            rows = slice(0, REL_BUCKETS)
            mm(bank(4)[0:8, :], relb[:, :], c_d("onehot", 0, S)[rows, :], start=True, stop=True)
            mm(bank(5)[0:8, :TOEP - S], relb[:, :], c_d("onehot", S, TOEP)[rows, :], start=True, stop=True).then_inc(gv_done, 1)
            project("q_idx", 0, 2, n_parts, inputs="mix2")
            project("w_idx", 0, 1, n_parts)
            project("k_idx", 0, 1, n_parts)
            turn_chunk("w_idx", 0, FIRST["w_turn"] - FIRST["w_idx"], TURNED["w_idx"])
            project("q_lat", 0, 3, n_parts)
            project("c_kv", 0, 2, n_parts)
            project("k_rope", 0, 1, n_parts)
            project("z_a", 0, 1, n_parts)
            norm_sum("q_lat")
            project("z_a", 1, 1, n_parts)
            norm_sum("c_kv")
            pe.wait_ge(kiz_made, 4)
            project("z_a", 2, 1, n_parts)
            for n in range(3 * IDX_HEADS):
                i, h = n // IDX_HEADS + 1, n % IDX_HEADS
                if n == 2:
                    project("z_a", 3, 1, n_parts)
                if n >= 2:
                    pe.wait_ge(t_relu, n - 1)
                mm(bank(2 + n % 2)[:, :P * (i + 1)], qi[:, h // 4, P * i:P * i + P], kiz[:, h % 4, :P * (i + 1)],
                   start=True, stop=True).then_inc(t_sc, 1)
            pe.wait_ge(t_relu, 3 * IDX_HEADS)
            rotate("second", 0, kp[:, :], FIRST["k_rope"], c_d("perm", 0, P))
            ql, ck = parts(qlH, qlL, 3), parts(ckH, ckL, 2)
            pe.wait_ge(nl_made, SPLIT["c_kv"] + 2)
            halves("uq", lambda s: 2 * s, 3, 3, ql)
            halves("ukv_k", lambda s: 2 * s, 2, 2, ck)
            for c in range(2):
                rotate("second", 1 + c, qp[:, c, :], FIRST["uq"] + 4 + c, c_d("perm", 0, P))

            def dsa_product(stage, j):
                if stage == "v_b":
                    values(stage, j)
                elif stage is not None:
                    project(stage, j, 1, n_parts)

            def turn_pair(s):
                for c in range(2):
                    turn_chunk("ukv_v", 4 * s + c, 4 * s + 2 + c, TURNED["ukv_v"] + 2 * s + c)

            halves("ukv_v", lambda s: 4 * s, 2, 2, ck, turn_pair)
            for item in DSA_ITEMS[:2]:
                dsa_product(*item)
            barrier()

            def mla_terms(h, i, keys):
                qs = slice(P * i, P * i + P)
                return [(qn[head_rows(h), h // 2, qs], kn[head_rows(h), h // 2, keys]),
                        (qp[:, h // 4, qs], kpz[:, h % 4, keys])]

            attention("mla", mla_terms, lambda h, t, bk: (vA[:, t, 64 * h:64 * h + 64], head_rows(h)), dx, dPT,
                      lambda x: dsa_product(*dsa_item(x)))
            for item in DSA_ITEMS[-2:]:
                dsa_product(*item)
            ya, yb = parts(yaH, yaL, 4), parts(ybH, ybL, 4)
            past_phase()
            mix_step("a_mix", 0, ya)
            mix_step("a_mix", 1, ya)
            pe.wait_ge(phase, 3 * n_phase[0])

            def dsa_terms(h, i, keys):
                return [(qb[head_rows(h), h // 2, P * i:P * i + P], kb[head_rows(h), h // 2, keys])]

            attention("dsa", dsa_terms, lambda h, t, bk: (vB[:, t, 64 * h:64 * h + 64], head_rows(h)), dx, dPT,
                      lambda x: [mix_step("a_mix", k, ya) for k in mix_steps(x)], lambda: mix_step("a_mix", 14, ya))
            mix_step("a_mix", 15, ya)
            past_phase()
            for k in range(16):
                mix_step("b_mix", k, yb)
            project("out2", 0, DC, parts(mg2H, mg2L, DC), inputs="merged2")
            norm_sum("out")

        @block.scalar
        def _(act):
            A = nc.scalar.activation
            n_phase = [0]

            def barrier():
                n_phase[0] += 1
                act.drain().then_inc(phase, 1)
                act.wait_ge(phase, 3 * n_phase[0])

            def product(stage, c):
                g = FIRST[stage] + c
                per = {"uq": 2, "ukv_k": 2, "ukv_v": 4}.get(stage)
                if per is not None and c % per == 0:
                    act.wait_ge(half_done, HALF_DONE[stage] + c // per + 1)
                else:
                    act.wait_ge(multiplied, ENDS[g])
                return bank(g % 2), freed[g % 2]

            def copy_out(stage, c, dst, cols=None, scale=1.0):
                b, free = product(stage, c)
                A(dst, b if cols is None else cols(b), ACT.Copy, scale=scale).then_inc(free, 1)

            def squares(name, x, ready, width=S, chunks=None):
                for c in range(CHUNKS[name]) if chunks is None else chunks:
                    a = ADDED[name] + c - 1
                    if c == (0 if name == "mix" else CHUNKS[name] - 1):
                        i = NORMS.index(name)
                        A(warm[:, i:i + 1], ones[:, 0:1], ACT.Sqrt)
                    ready(c)
                    if c and a >= 2:
                        act.wait_ge(sq_added, a - 1)
                    A(sq[:, a % 2, :width] if c else sums[:, :width], x[:, c, :], ACT.Square).then_inc(sq_made, 1)

            def deviation(name, width=S):
                i = NORMS.index(name)
                act.wait_ge(sum_done, i + 1)
                if i:
                    act.wait_ge(r_made, i)
                A(std[:, :width], bank(7)[:, :width], ACT.Sqrt, scale=1.0 / (P * CHUNKS[name]), bias=EPS).then_inc(std_made, 1)

            def norm(name, x, ready):
                squares(name, x, ready)
                deviation(name)

            def raw_out(stage, at, k, width=S):
                copy_out(stage, at, vraw[:, k % 2, :width], lambda b: b[:, :width])

            def turned_out(stage, at, k, dst, width=S, scale=1.0, few=P):
                act.wait_ge(v_turned, k + 1)
                copy_out(stage, at, dst, lambda b: b[:, :width].rearrange("p (t k) -> p t k", k=P)[:, :, :few], scale)

            def value_out(stage, j, dst):
                if j in RAW_AT:
                    raw_out(stage, j, TURNED[stage] + RAW_AT.index(j))
                else:
                    c = TURN_AT.index(j)
                    turned_out(stage, j, TURNED[stage] + c, dst[:, :, P * c:P * c + P])

            def high(name, c, dst, width=S):
                k = SPLIT[name] + c
                act.wait_ge(nt_made, k + 1)
                A(dst, nt[:, k % 2, :width], ACT.Copy).then_inc(nh_made, 1)

            def highs(name, dst, chunks, width=S):
                for c in range(chunks):
                    high(name, c, dst[:, c, :], width)

            def sigmoids(stage, chunks):
                for c in chunks:
                    b, _ = product(stage, c)
                    y = SILU[stage] + c
                    if c >= 2:
                        out_of_bank(act, FIRST[stage] + c - 2)
                    A(sgb[:, y % 2, :], b, ACT.Sigmoid).then_inc(sg_made, 1)

            def head_out(h, j):
                stage = f"head{h}"
                if j < 2:
                    b, free = product(stage, j)
                    A(kk[:, j, h, :], b, ACT.Sigmoid).then_inc(free, 1)
                elif j == 2:
                    b, _ = product(stage, j)
                    if h:
                        out_of_bank(act, FIRST[f"head{h - 1}"] + 2)
                    A(sgb[:, h % 2, :], b, ACT.Sigmoid).then_inc(sg_made, 1)
                elif j == 3:
                    raw_out(stage, 3, TURNED[stage])
                else:
                    turned_out(stage, 4, TURNED[stage], vr[:, :, P * h:P * h + P])

            def recurrence(beside):
                two = [x[:, :].rearrange("p (b t) -> p b t", b=2) for x in pair]

                def logs(h):
                    act.wait_ge(f_made, h + 1)
                    A(lf[:, :, :], lf[:, :, :], ACT.Ln).then_inc(lf_made, 1)

                def logs_high(h):
                    act.wait_ge(lf_turned, h + 1)
                    A(lftH[:, :, :, :].rearrange("p d t k -> p (d t k)"), pair[1][:, :], ACT.Copy).then_inc(lh_made, 1)

                def decays(n, width):
                    act.wait_ge(dec_done, n + 1)
                    if n >= 2:
                        act.wait_ge(x_made, n - 1)
                        if (n - 2) % UNITS == 0:
                            act.wait_ge(cross_done, (n - 2) // UNITS + 1)
                    for b in range(2):
                        last = A(E[:, n % 2, 2 * b:2 * b + 2, :width], two[1 + b][:, :, :width], ACT.Exp)
                    last.then_inc(exp_done, 1)

                def cross_copies(h):
                    act.wait_ge(cross_done, h + 1)
                    if h:
                        act.wait_ge(o_done, h)
                    for j in range(ST):
                        for a, b in ((0, P * j), (P * j + P, S)):
                            if b > a:
                                last = A(Sg[:, j, a:b], bank(2 + (j + 1) % ST)[:, a:b], ACT.Copy)
                    last.then_inc(cross_out, 1)

                logs(0)
                head_out(0, 3)
                head_out(0, 4)
                logs_high(0)
                head_out(1, 0)
                decays(0, S)
                head_out(1, 1)
                decays(1, LQ)
                for j in range(2, 5):
                    head_out(1, j)
                act.wait_ge(angle_s, 1)
                A(sinA[:, :], sinA[:, :], ACT.Sin).then_inc(tables, 1)
                act.wait_ge(angle_c, 1)
                A(cosA[:, :], cosA[:, :], ACT.Sin, bias=float(np.pi / 2)).then_inc(tables, 1)
                beside(0, 0)
                for h in range(HG_HEADS):
                    n, more = UNITS * h, h + 1 < HG_HEADS
                    cross_copies(h)
                    decays(n + 2, LQ)
                    beside(h, 1)
                    decays(n + 3, LQ)
                    if more:
                        logs(h + 1)
                    decays(n + 4, LQ)
                    beside(h, 2)
                    if more:
                        logs_high(h + 1)
                        decays(n + UNITS, S)
                    beside(h, 3)
                    if more:
                        decays(n + UNITS + 1, LQ)
                    beside(h, 4)
                    if more:
                        beside(h + 1, 0)
                    if not more:
                        act.wait_ge(o_sum, 1)
                        A(kk[:, 1, 0, :], bank(3), ACT.Sqrt, scale=1.0 / P, bias=EPS)
                        A(kk[:, 1, 1:h, :], two[2], ACT.Sqrt, scale=1.0 / P, bias=EPS).then_inc(o_std, 1)
                    act.wait_ge(o_done, h + 1)
                    A(kk[:, 0, h, :], bank(2), ACT.Square).then_inc(o_sq, 1)
                    A(qT[:, h, :], bank(2), ACT.Copy).then_inc(o_out, 1)
            def last_deviation():
                act.wait_ge(o_sum, 2)
                A(kk[:, 1, HG_HEADS - 1, :], bank(3), ACT.Sqrt, scale=1.0 / P, bias=EPS).then_inc(o_std, 1)

            def attention(name, probs, turned, dst, sink=False, beside=lambda x: None):
                kind = KINDS[name]
                units, u0, n = kind["units"], kind["first"], len(kind["units"])
                per, banks = kind["per_round"], kind["banks"]

                for x in range(n + OUT_LAG + 2):
                    if x < n:
                        (h, i), u = units[x], u0 + x
                        a, b = kind["keys"](i)
                        st = stat[:, u % 4, :]
                        act.wait_ge(a_neg, u + 1)
                        if sink:
                            A(st[:, 3:4], sinks[:, h:h + 1], ACT.Exp, bias=st[:, 1:2])
                        px = probs[:, u % 4, :P * (b - a)]
                        A(px, px, ACT.Exp, bias=st[:, 1:2], accum_out=st[:, 2:3]).then_inc(a_exp, 1)
                        beside(x)
                    y = x - TURN_LAG
                    if 0 <= y < n:
                        (h, i), u = units[y], u0 + y
                        a, b = kind["keys"](i)
                        act.wait_ge(a_turn, u + 1)
                        j = y // ST
                        if i == 0 and j >= kind["ring"]:
                            act.wait_ge(a_pv, kind["first_head"] + j - kind["ring"] + 1)
                        A(turned[:, j % kind["ring"], a:b, P * i:P * i + P],
                          bank(4 + u % 2)[:, :P * (b - a)].rearrange("p (t q) -> p t q", q=P), ACT.Copy).then_inc(a_pt, 1)
                    y = x - OUT_LAG - 1
                    if 0 <= y < n and y % per == per - 1:
                        for bk in range(banks):
                            c = (y // per) * banks + bk
                            high(kind["out"], c, dst[:, c, :])

            def mix_out(stage, k, sg, before=None):
                if k % 4 < 2:
                    c, ring = 2 * (k // 4) + k % 4, sg.shape[1]
                    y = 4 * (c // 2) + 2 + c % 2
                    if c >= ring:
                        out_of_bank(act, FIRST[stage] + y - 2 * ring)
                    elif before is not None:
                        out_of_bank(act, FIRST[before] + y + 2 * (DC - ring))
                    bk, free = product(stage, k)
                    A(sg[:, c % ring, :], bk, ACT.Sigmoid).then_inc(free, 1)

            def merge(stage, sg, dst, name, before, beside=lambda p: None):
                for k in range(16):
                    mix_out(stage, k, sg, before)
                    if k % 4 == 1:
                        beside(k // 4)
                    if k % 4 == 1 and k >= 4:
                        for c in (k // 2 - 2, k // 2 - 1):
                            high(name, c, dst[:, c, :])
                for c in (DC - 2, DC - 1):
                    high(name, c, dst[:, c, :])

            def residual(stage):
                return lambda c: out_of_bank(act, FIRST[stage] + c)

            act.dma_start(vec[:, :], vecs).then_inc(ld_vec, 16)

            act.wait_ge(ones_set, 2)
            squares("mix", hT, lambda c: act.wait_ge(ld_x[c // 2], 16))
            deviation("mix")
            act.dma_start(landing[:, :], const_r).then_inc(ld_r, 16)
            act.dma_start(ident[:, :], ident_d).then_inc(ld_a, 16)
            act.dma_start(cA[:, :], const_a).then_inc(ld_a, 16)
            act.dma_start(sinks[:, :], sink_d.partition_broadcast(P)).then_inc(ld_a, 16)
            act.dma_start(posi[:, :], pos.partition_broadcast(P)).then_inc(ld_pos, 16)
            highs("mix", nH, DC)
            act.wait_ge(lb_diff, 1)
            A(lbs[:, 16:32], lbs[:, 16:32], ACT.Exp).then_inc(lb_exp, 1)
            for j in range(3):
                head_out(0, j)

            def head_beside(h, j):
                if h + 2 < HG_HEADS:
                    head_out(h + 2, j)
                elif h + 2 == HG_HEADS and j < 4:
                    copy_out("q_a", j, qa[:, j, :])
                elif h + 1 == HG_HEADS and j == 1:
                    copy_out("k_a", 0, ka[:, :])
                elif h + 1 == HG_HEADS and j == 2:
                    raw_out("v_a", 0, TURNED["v_a"])
                elif h + 1 == HG_HEADS and j == 3:
                    act.wait_ge(sc_done, ST * HG_HEADS)
                    copy_out("g_first", 0, gr[:, 0, :])
                    turned_out("v_a", 1, TURNED["v_a"], va[:, :, :])

            recurrence(head_beside)
            for c in range(4):
                if c:
                    copy_out("g_rest", c - 1, gr[:, c, :])
                else:
                    last_deviation()
                out_of_bank(act, g_r(c))
                A(gs[:, c, :], gr[:, c, :], ACT.Sigmoid).then_inc(sg_made, 1)
            highs("rec", recH, 4)
            mix_out("rec_mix", 0, sgA)
            mix_out("rec_mix", 1, sgA)
            attention("window", wx, wPT, attH, sink=True,
                      beside=lambda x: [mix_out("rec_mix", k, sgA) for k in mix_steps(x)])
            barrier()
            act.dma_start(memx[:, :, :], memT).then_inc(ld_mem, 16)
            merge("att_mix", sgA, mgH, "merged", "rec_mix",
                  lambda p: squares("memory", memx, lambda c: act.wait_ge(ld_mem, 16), MEM, (2 * p, 2 * p + 1)))
            deviation("memory", MEM)
            highs("memory", mnH, DC, MEM)
            squares("mem", hT, residual("mix_out"))

            def mem_out(h, j):
                stage, k0, c = f"mem{h}", TURNED[f"mem{h}"], 2 * h + j % 2
                if j < 2:
                    copy_out(stage, j, mk[:, c, :], lambda b: b[:, :MEM])
                elif j < 4:
                    raw_out(stage, j, k0 + j - 2, MEM)
                elif j in (5, 7):
                    c = 2 * h + (j - 5) // 2
                    turned_out(stage, j, k0 + (j - 5) // 2, mv[:, :, P * c:P * c + P], MEM)
                else:
                    c = 2 * h + (j - 4) // 2
                    copy_out(stage, j, mq[:, c, :])

            mem_out(0, 0)
            deviation("mem")
            mem_out(0, 1)
            for c in range(DC):
                high("mem", c, nH[:, c, :])
                if c in (2, 5):
                    mem_out(0, 2 + c // 3)
            for j in range(4, 8):
                mem_out(0, j)

            def mem_beside(x):
                h = x // ST + 1
                if h < MEM_HEADS:
                    for j in ((0, 1), (2, 3), (4, 5), (6, 7))[x % ST]:
                        mem_out(h, j)

            attention("memory", mx, mPT, moH, beside=mem_beside)
            for c in range(DC):
                squares("ffn", hT, residual("mem_o"), chunks=[c])
                high("ffn", c, nH[:, c, :])
            deviation("ffn")

            for j in range(FC):
                act.wait_ge(conv_made, j + 1)
                if j >= 2:
                    out_of_bank(act, FIRST["up"] + 2 * (j - 2) + 1)
                A(sgb[:, j % 2, :], cv[:, j % 2, :], ACT.Sigmoid).then_inc(fsg_made, 1)
                if j >= 1:
                    high("hidden", j - 1, aH[:, j - 1, :])
            high("hidden", FC - 1, aH[:, FC - 1, :])
            for c in range(DC):
                for n, total in ((0, sums), (1, sums2)):
                    a = ADDED["final"] + 2 * (c - 1) + n
                    if n == 0:
                        out_of_bank(act, FIRST["down"] + c)
                    else:
                        act.wait_ge(hg_made, c + 1)
                    if c:
                        act.wait_ge(sq_added, a - 1)
                    if c == DC - 1 and n == 0:
                        i = NORMS.index("final")
                        A(warm[:, i:i + 1], ones[:, 0:1], ACT.Sqrt)
                    A(sq[:, a % 2, :] if c else total[:, :], hT[:, c, :], ACT.Square).then_inc(sq_made, 1)
            act.dma_start(cD[:, :], const_d).then_inc(ld_d, 16)
            act.dma_start(relb[:, :], relb_d).then_inc(ld_d, 16)
            act.wait_ge(var_made, 1)
            A(std[:, :], sums2[:, :], ACT.Sqrt, scale=1.0 / D, bias=EPS * EPS).then_inc(std_made, 1)
            act.wait_ge(r_made, NORMS.index("final") + 1)
            A(std[:, :], bank(7), ACT.Sqrt, scale=1.0 / D, bias=EPS).then_inc(std_made, 1)

            highs("mix2", nH, DC)
            for c in range(2):
                copy_out("q_idx", c, qi[:, c, :])
            raw_out("w_idx", 0, TURNED["w_idx"])
            copy_out("k_idx", 0, ki[:, :])
            turned_out("w_turn", 0, TURNED["w_idx"], wtok[:, :, :], scale=IDXW_SCALE, few=IDX_HEADS)
            act.wait_ge(x1_made, DC)
            act.dma_start(x1_d, hT[:, :, :]).then_inc(st_x1, 16)
            act.wait_ge(gv_done, 1)
            A(gv[:, :S], bank(4)[0:8, :], ACT.Copy).then_inc(gv_out, 1)
            A(gv[:, S:], bank(5)[0:8, :TOEP - S], ACT.Copy).then_inc(gv_out, 1)
            act.wait_ge(gv_out, 2)
            for c in range(3):
                copy_out("q_lat", c, qlat[:, c, :])
            squares("q_lat", qlat, lambda c: out_of_bank(act, FIRST["q_lat"] + c))
            for c in range(2):
                copy_out("c_kv", c, ckv[:, c, :])
            copy_out("k_rope", 0, kp[:, :])
            sigmoids("z_a", [0])
            deviation("q_lat")
            squares("c_kv", ckv, lambda c: out_of_bank(act, FIRST["c_kv"] + c))
            highs("q_lat", qlH, 3)
            sigmoids("z_a", [1])
            deviation("c_kv")
            highs("c_kv", ckH, 2)
            sigmoids("z_a", [2])
            for n in range(3 * IDX_HEADS):
                if n == 2:
                    sigmoids("z_a", [3])
                w = P * (n // IDX_HEADS + 2)
                act.wait_ge(t_sc, n + 1)
                if n >= 2:
                    act.wait_ge(t_acc, n - 1)
                A(rl[:, n % 2, :w], bank(2 + n % 2)[:, :w], ACT.Relu, scale=IDX_SCALE).then_inc(t_relu, 1)
            for c in range(6):
                copy_out("uq", c, qn[:, c, :] if c < 4 else qp[:, c - 4, :])
            for c in range(4):
                copy_out("ukv_k", c, kn[:, c, :])
            for s in range(2):
                for c in range(2):
                    raw_out("ukv_v", 4 * s + c, TURNED["ukv_v"] + 2 * s + c)
                for c in range(2):
                    h = 2 * s + c
                    turned_out("ukv_v", 4 * s + 2 + c, TURNED["ukv_v"] + h, vA[:, :, P * h:P * h + P])
            barrier()
            act.wait_ge(st_x1, 16)

            act.dma_start(gvec, gv[:, None, :].broadcast_to([8, P, TOEP])).then_inc(st_gvec, 16)

            def dsa_copy(stage, j):
                if stage in ("q_b", "k_b"):
                    copy_out(stage, j, (qb if stage == "q_b" else kb)[:, j, :])
                elif stage == "v_b":
                    value_out(stage, j, vB)
                elif stage == "z_b":
                    sigmoids(stage, [j])

            for item in DSA_ITEMS[:2]:
                dsa_copy(*item)
            attention("mla", dx, dPT, yaH, beside=lambda x: dsa_copy(*dsa_item(x)))
            for item in DSA_ITEMS[-2:]:
                dsa_copy(*item)
            barrier()
            act.wait_ge(st_gvec, 16)

            def load_bias(h, done):
                act.dma_start(toep[:, h % 4, :], bass.AP(gvec.tensor, h * P * TOEP + P - 1, [[TOEP - 1, P], [1, S]])).then_inc(done, 16)

            for h in range(4):
                load_bias(h, ld_toep)
            mix_out("a_mix", 0, sgD)
            mix_out("a_mix", 1, sgD)

            def dsa_beside(x):
                h = x // ST
                if x % ST == ST - 1 and h < 4:
                    load_bias(h + 4, ld_late[h])
                for k in mix_steps(x):
                    mix_out("a_mix", k, sgD)

            attention("dsa", dx, dPT, ybH, beside=dsa_beside)
            barrier()
            act.dma_start(hT[:, :, :], x1_d).then_inc(ld_x1, 16)
            merge("b_mix", sgD, mg2H, "merged2", "a_mix")
            norm("out", hT, residual("out2"))
            for c in range(DC):
                act.wait_ge(y_made, c + 1)
                act.dma_start(outT[:, c, :], hT[:, c, :]).then_inc(st_out, 16)
            act.wait_ge(st_out, 16 * DC)

        @block.vector
        def _(dve):
            V = nc.vector
            n_phase, n_own = [0], [0]

            def barrier():
                n_phase[0] += 1
                dve.drain().then_inc(phase, 1)
                dve.wait_ge(phase, 3 * n_phase[0])

            def own(ins):
                n_own[0] += 1
                ins.then_inc(dve_own, 1)
                dve.wait_ge(dve_own, n_own[0])

            def product(stage, c):
                g = FIRST[stage] + c
                dve.wait_ge(multiplied, ENDS[g])
                return bank(g % 2), freed[g % 2]

            def open_split(name, c, width=S):
                k = SPLIT[name] + c
                if k >= 2:
                    dve.wait_ge(nl_made, k - 1)
                return nt[:, k % 2, :width]

            def low(name, c, hi, lo, width=S):
                k = SPLIT[name] + c
                dve.wait_ge(nh_made, k + 1)
                V.tensor_tensor(lo[:, c, :], nt[:, k % 2, :width], hi[:, c, :].bitcast(F32),
                                ALU.subtract).then_inc(nl_made, 1)

            def accumulate(name, c, width=S):
                a = ADDED[name] + c - 1
                dve.wait_ge(sq_made, SQUARE[name] + c + 1)
                if a:
                    dve.wait_ge(sq_added, a)
                V.tensor_tensor(sums[:, :width], sums[:, :width], sq[:, a % 2, :width], ALU.add).then_inc(sq_added, 1)

            def accumulate_all(name, width=S):
                for c in range(1, CHUNKS[name]):
                    accumulate(name, c, width)

            def inverse(name, width=S):
                i = NORMS.index(name)
                dve.wait_ge(std_made, i + 1)
                V.reciprocal(rstd[:, :width], std[:, :width]).then_inc(r_made, 1)
                dve.wait_ge(r_made, i + 1)

            def normed(out, x, gain, c, width=S):
                return V.scalar_tensor_tensor(out=out, in0=x[:, c, :], scalar=vcol(gain, c), in1=rstd[:, :width],
                                              op0=ALU.mult, op1=ALU.mult)

            def norm(name, x, gain, hi, lo, width=S, beside=lambda c: None):
                chunks = CHUNKS[name]
                for c in range(chunks):
                    beside(c)
                    normed(open_split(name, c, width), x, gain, c, width).then_inc(nt_made, 1)
                    if c:
                        low(name, c - 1, hi, lo, width)
                low(name, chunks - 1, hi, lo, width)

            def silu(stage, chunks, dst, scale=None):
                for c in chunks:
                    dve.wait_ge(sg_made, SILU[stage] + c + 1)
                    b, free = product(stage, c)
                    sg = sgb[:, (SILU[stage] + c) % 2, :]
                    if scale is None:
                        V.tensor_tensor(dst[:, c, :], b, sg, ALU.mult).then_inc(free, 1)
                    else:
                        V.scalar_tensor_tensor(out=dst[:, c, :], in0=b, scalar=scale, in1=sg,
                                               op0=ALU.mult, op1=ALU.mult).then_inc(free, 1)

            def rotate(name, n, x, cos, sin, at=None):
                m = ROTATE[name] + n
                dve.wait_ge(rot_done, m + 1)
                if m:
                    dve.wait_ge(rotated, m)
                partners, read = (bank(4 + m % 2), rot_used) if at is None else (bank(at % 2), freed[at % 2])
                V.tensor_tensor(sgb[:, m % 2, :], partners, sin, ALU.mult).then_inc(read, 1)
                own(V.tensor_tensor(x, x, cos, ALU.mult))
                if at is not None:
                    out_of_bank(dve, at)
                V.tensor_tensor(x, x, sgb[:, m % 2, :], ALU.add).then_inc(rotated, 1)

            def residual(stage, name, chunks=range(DC), after=lambda c: None):
                for c in chunks:
                    b, free = product(stage, c)
                    V.tensor_tensor(hT[:, c, :], b, hT[:, c, :], ALU.add).then_inc(free, 1)
                    after(c)
                    if c >= 2:
                        accumulate(name, c - 1)
                if DC - 1 in chunks:
                    accumulate(name, DC - 1)

            def lower_bounds():
                dve.wait_ge(ld_vec, 16)
                a = vec[:, VEC["lower"]:VEC["lower"] + 16].rearrange("p (d l h) -> p d l h", d=2, l=2)
                m = lbs[:, 0:8].rearrange("p (d h) -> p d h", d=2)
                e = lbs[:, 16:32].rearrange("p (d l h) -> p d l h", d=2, l=2)
                own(V.tensor_tensor(m, a[:, :, 0, :], a[:, :, 1, :], ALU.max))
                own(V.tensor_tensor(e[:, :, 0, :], a[:, :, 0, :], m, ALU.subtract))
                V.tensor_tensor(e[:, :, 1, :], a[:, :, 1, :], m, ALU.subtract).then_inc(lb_diff, 1)
                dve.wait_ge(lb_exp, 1)
                own(V.tensor_tensor(m, e[:, :, 0, :], e[:, :, 1, :], ALU.add))
                own(V.reciprocal(m, m))
                own(V.tensor_tensor(lbs[:, 32:40].rearrange("p (d h) -> p d h", d=2), e[:, :, 0, :], m, ALU.mult))
                own(V.tensor_scalar(lbs[:, 40:48], lbs[:, 32:40], -1.0, 1.0, ALU.mult, ALU.add))
                own(V.tensor_scalar(lbs[:, 48:56], lbs[:, 32:40], 1.0, None, ALU.subtract))

            def lb(which, d, h):
                i = 32 + 8 * which + 4 * d + h
                return lbs[:, i:i + 1]

            def recurrence():
                def forget(h):
                    for d in range(2):
                        out_of_bank(dve, FIRST[f"head{h}"] + d)
                        own(V.tensor_scalar(lf[:, d, :], kk[:, d, h, :], lb(1, d, h), lb(0, d, h), ALU.mult, ALU.add))
                    V.tensor_scalar(lf[:, :, :], lf[:, :, :], LN_FLOOR, None, ALU.max).then_inc(f_made, 1)

                def keys(h):
                    for d in range(2):
                        own(V.tensor_scalar(kk[:, d, h, :], kk[:, d, h, :], lb(2, d, h), lb(1, d, h), ALU.mult, ALU.add))
                    if h:
                        dve.wait_ge(sc_done, ST * h)
                    V.tensor_tensor(kfb[:, :], kk[:, 0, h, :], kk[:, 1, h, :], ALU.add).then_inc(k_made, 1)

                def cross(h):
                    n = UNITS * h
                    dve.wait_ge(exp_done, n + 1)
                    e = E[:, n % 2, :, :]
                    V.tensor_tensor(e[:, 0, :], e[:, 0, :], qT[:, h, :], ALU.mult)
                    V.tensor_tensor(e[:, 2, :], e[:, 2, :], qT[:, h, :], ALU.mult)
                    for b, view in ((1, "p (a two k) -> p two a k"), (3, "p (two a k) -> p two a k")):
                        for d in range(2):
                            x = e[:, b, :].rearrange(view, two=2, k=P)[:, d]
                            last = V.tensor_tensor(x, x, kk[:, d, h, :].rearrange(view, two=2, k=P)[:, d], ALU.mult)
                    last.then_inc(x_made, 1)

                def tile(h, i):
                    n, m = UNITS * h + 1 + i, ST * h + i
                    dve.wait_ge(exp_done, n + 1)
                    if m >= 2:
                        dve.wait_ge(sc_done, m - 1)
                    cs = slice(P * i, P * i + P)
                    for l in range(LEVELS):
                        c = 1 << l

                        def two(x):
                            return x.rearrange("p (b two c) -> p two b c", two=2, c=c)

                        ls, xs = slice(HALF * l, HALF * l + HALF), slice(P * l, P * l + P)
                        for kind, half, b, src in ((0, 1, 0, qT[:, h, cs]), (0, 0, 1, qT[:, h, cs]),
                                                   (1, 0, 2, kk[:, 0, h, cs]), (1, 1, 3, kk[:, 1, h, cs])):
                            last = V.tensor_tensor(two(X[:, m % 2, kind, xs])[:, half],
                                                   E[:, n % 2, b, ls].rearrange("p (b c) -> p b c", c=c),
                                                   two(src)[:, half], ALU.mult)
                    last.then_inc(x_made, 1)

                def select(h, i):
                    m = ST * h + i
                    dve.wait_ge(sc_done, m + 1)
                    if m:
                        dve.wait_ge(s_made, m)
                    V.tensor_tensor(lev[:, :, :], pair[3][:, :].rearrange("p (l t) -> p l t", l=8),
                                    c_a("level", 0, 8 * P).rearrange("p (l t) -> p l t", l=8),
                                    ALU.mult).then_inc(masked, 1)
                    dve.wait_ge(masked, m + 1)
                    if h and i == 0:
                        dve.wait_ge(o_done, h)
                    V.tensor_reduce(Sg[:, i, P * i:P * i + P], lev[:, :, :].rearrange("p l t -> p t l"),
                                    AX.X, ALU.add).then_inc(s_made, 1)

                def logs_low(h):
                    dve.wait_ge(lh_made, h + 1)
                    V.tensor_tensor(lftL[:, :, :, :].rearrange("p d t k -> p (d t k)"), pair[1][:, :],
                                    lftH[:, :, :, :].rearrange("p d t k -> p (d t k)").bitcast(F32),
                                    ALU.subtract).then_inc(lft_made, 1)

                def queries(h):
                    dve.wait_ge(sg_made, SILU["q_r"] + h + 1)
                    b, free = product(f"head{h}", 2)
                    V.scalar_tensor_tensor(out=qT[:, h, :], in0=b, scalar=HG_SCALE, in1=sgb[:, h % 2, :],
                                           op0=ALU.mult, op1=ALU.mult).then_inc(free, 1)

                def start(h):
                    keys(h)
                    out_of_bank(dve, FIRST[f"head{h}"] + 2)
                    cross(h)
                    tile(h, 0)

                forget(0)
                queries(0)
                logs_low(0)
                start(0)
                queries(1)
                rotary_angles()
                def turn_queries(c):
                    rotate("first", c, qa[:, c, :], cosA[:, :], sinA[:, :], q_turn(c))

                for h in range(HG_HEADS):
                    more = h + 1 < HG_HEADS
                    if not more:
                        dve.wait_ge(tables, 2)
                        for c in (0, 1):
                            out_of_bank(dve, FIRST[f"head{2 + c}"] + 2)
                            turn_queries(c)
                    tile(h, 1)
                    select(h, 0)
                    if more:
                        forget(h + 1)
                    else:
                        turn_queries(2)
                        turn_queries(3)
                    tile(h, 2)
                    select(h, 1)
                    tile(h, 3)
                    select(h, 2)
                    if more:
                        logs_low(h + 1)
                    if h + 2 < HG_HEADS:
                        queries(h + 2)
                    select(h, 3)
                    if more:
                        start(h + 1)
                    else:
                        rotate("first", 4, ka[:, :], cosA[:, :], sinA[:, :], FIRST["k_turn"])

            def output_norm(h):
                dve.wait_ge(o_std, 1 if h + 1 < HG_HEADS else 2)
                dve.wait_ge(o_out, h + 1)
                own(V.reciprocal(kk[:, 1, h, :], kk[:, 1, h, :]))
                V.scalar_tensor_tensor(out=qT[:, h, :], in0=qT[:, h, :], scalar=vcol("hg_norm", h), in1=kk[:, 1, h, :],
                                       op0=ALU.mult, op1=ALU.mult).then_inc(o_norm, 1)

            def rotary_angles():
                dve.wait_ge(ld_pos, 16)
                own(V.tensor_copy(ang[:, :], posi[:, :]))
                own(V.tensor_scalar(ang[:, :], ang[:, :], vcol("inv_freq", 0), None, ALU.mult))
                pi = float(np.float32(3.1415925))
                for out, shift, lo, hi, done in ((sinA, 0.0, -pi, pi, angle_s),
                                                 (cosA, 0.25, -1.5 * np.pi + 1e-6, 0.5 * np.pi - 1e-6, angle_c)):
                    own(V.tensor_scalar(turn[:, :], ang[:, :], 1.0 / TWO_PI, shift, ALU.mult, ALU.add))
                    own(V.tensor_scalar(turn[:, :], turn[:, :], ROUND, None, ALU.add))
                    own(V.tensor_scalar(turn[:, :], turn[:, :], ROUND, None, ALU.subtract))
                    src = ang
                    for part in (PI_A, PI_B, PI_C):
                        own(V.scalar_tensor_tensor(out=out[:, :], in0=turn[:, :], scalar=-part, in1=src[:, :],
                                                   op0=ALU.mult, op1=ALU.add))
                        src = out
                    V.tensor_scalar(out[:, :], out[:, :], lo, hi, ALU.max, ALU.min).then_inc(done, 1)

            def attention(name, x_buf, scale, mask, hi, lo, bias=None, sink=False, gate=None,
                          beside=lambda x: None):
                kind = KINDS[name]
                units, u0, n = kind["units"], kind["first"], len(kind["units"])
                per, banks = kind["per_round"], kind["banks"]

                def row_max(x):
                    (h, i), u = units[x], u0 + x
                    a, b = kind["keys"](i)
                    w, st = P * (b - a), stat[:, u % 4, :]
                    dve.wait_ge(a_sc, u + 1)
                    if x >= 4:
                        dve.wait_ge(a_turn, u - 3)
                    sx, src, by = x_buf[:, u % 4, :w], bank(2 + u % 2)[:, :w], scale
                    if bias is not None:
                        own(V.scalar_tensor_tensor(out=sx, in0=src, scalar=scale, in1=bias(h, i),
                                                   op0=ALU.mult, op1=ALU.add))
                        src, by = sx, 1.0
                    V.tensor_tensor_reduce(out=sx, in0=src, in1=mask(i), scale=by, scalar=LOWEST, op0=ALU.add,
                                           op1=ALU.max, accum_out=st[:, 0:1]).then_inc(a_max, 1)
                    dve.wait_ge(a_max, u + 1)
                    if sink:
                        V.tensor_scalar(st[:, 1:2], st[:, 0:1], sinks[:, h:h + 1], -1.0, ALU.max, ALU.mult).then_inc(a_neg, 1)
                    else:
                        V.tensor_scalar(st[:, 1:2], st[:, 0:1], -1.0, None, ALU.mult).then_inc(a_neg, 1)

                def normalise(x):
                    (h, i), u = units[x], u0 + x
                    a, b = kind["keys"](i)
                    px, st = x_buf[:, u % 4, :P * (b - a)], stat[:, u % 4, :]
                    dve.wait_ge(a_exp, u + 1)
                    total = st[:, 2:3]
                    if sink:
                        own(V.tensor_tensor(st[:, 4:5], st[:, 2:3], st[:, 3:4], ALU.add))
                        total = st[:, 4:5]
                    own(V.reciprocal(st[:, 5:6], total))
                    V.tensor_scalar(px, px, st[:, 5:6], None, ALU.mult).then_inc(a_prob, 1)

                for x in range(n + OUT_LAG + 3):
                    if x < n:
                        row_max(x)
                    if 0 <= x - NORM_LAG < n:
                        normalise(x - NORM_LAG)
                    if x < n:
                        beside(x)
                    y = x - OUT_LAG
                    if 0 <= y < n and y % per == per - 1:
                        rnd = y // per
                        for bk in range(banks):
                            c = rnd * banks + bk
                            out = open_split(kind["out"], c)
                            dve.wait_ge(a_pv, kind["first_head"] + y // ST + 1)
                            src = bank(6 + (rnd % 2 if banks == 1 else bk))
                            if gate is None:
                                V.tensor_copy(out, src).then_inc(nt_made, 1)
                            else:
                                V.tensor_tensor(out, src, gate[:, c, :], ALU.mult).then_inc(nt_made, 1)
                    y = x - OUT_LAG - 2
                    if 0 <= y < n and y % per == per - 1:
                        for bk in range(banks):
                            low(kind["out"], (y // per) * banks + bk, hi, lo)

            def mix_pair(stage, p, sg, use):
                for c in (2 * p, 2 * p + 1):
                    out_of_bank(dve, FIRST[stage] + 4 * p + c % 2)
                    g = FIRST[stage] + 4 * p + 2 + c % 2
                    if c % 2:
                        dve.wait_ge(multiplied, ENDS[g])
                    else:
                        dve.wait_ge(half_done, HALF_DONE[stage] + p + 1)
                    src, free = bank(g % 2), freed[g % 2]
                    use(c, src, sg[:, c % sg.shape[1], :], free)

            def first_branch(stage, p, sg, mt):
                mix_pair(stage, p, sg, lambda c, src, g, free:
                         V.tensor_tensor(mt[:, c, :], src, g, ALU.mult).then_inc(free, 1))

            def merge(stage, sg, mt, add, name, hi, lo, beside=lambda p: None):
                def use(c, src, g, free):
                    out = open_split(name, c)
                    V.tensor_tensor(add[:, c % 2, :], src, g, ALU.mult).then_inc(free, 1)
                    out_of_bank(dve, FIRST[stage] + 4 * (c // 2) + 2 + c % 2)
                    V.tensor_tensor(out, add[:, c % 2, :], mt[:, c, :], ALU.add).then_inc(nt_made, 1)
                    if c:
                        low(name, c - 1, hi, lo)

                for p in range(DC // 2):
                    beside(p)
                    mix_pair(stage, p, sg, use)
                low(name, DC - 1, hi, lo)

            dve.wait_ge(ld_vec, 16)
            accumulate_all("mix")
            inverse("mix")
            norm("mix", hT, "norm_mix", nH, nL)
            lower_bounds()
            dve.wait_ge(ld_r, 16)
            V.tensor_copy(cR[:, :], landing[:, :]).then_inc(zero_one, 1)
            dve.wait_ge(ld_a, 48)
            recurrence()
            for c in range(4):
                output_norm(c)
            for c in range(4):
                dve.wait_ge(sg_made, SILU["g_r"] + c + 1)
                out = open_split("rec", c)
                own(V.tensor_tensor(gs[:, c, :], gr[:, c, :], gs[:, c, :], ALU.mult))
                dve.wait_ge(o_norm, c + 1)
                V.tensor_tensor(out, gs[:, c, :], qT[:, c, :], ALU.mult).then_inc(nt_made, 1)
                if c:
                    low("rec", c - 1, recH, recL)
            low("rec", 3, recH, recL)
            own(V.memset(wPT[:, :, 1, S - P:], 0.0))

            def band_mask(i):
                a, b = band(i)
                return c_a("band", P * (a - i + 1), P * (b - i + 1))

            attention("window", wx, ATT_SCALE, band_mask, attH, attL, sink=True,
                      beside=lambda x: [first_branch("rec_mix", p, sgA, mtA) for p in mix_pairs(x)])
            first_branch("rec_mix", 3, sgA, mtA)
            barrier()
            def add_memory(p):
                for c in (2 * p, 2 * p + 1):
                    if c:
                        accumulate("memory", c, MEM)

            merge("att_mix", sgA, mtA, addA, "merged", mgH, mgL, add_memory)
            inverse("memory", MEM)
            norm("memory", memx, "norm_mem_kv", mnH, mnL, MEM, lambda c: residual("mix_out", "mem", [0]) if c == 4 else None)
            residual("mix_out", "mem", range(1, DC))
            inverse("mem")
            norm("mem", hT, "norm_mem", nH, nL)

            own(V.memset(nomask[:, :], 0.0))
            attention("memory", mx, MEM_SCALE, lambda i: nomask[:, :], moH, moL)

            def with_gain(c):
                out = open_split("ffn", c)
                out_of_bank(dve, FIRST["mem_o"] + c)
                V.tensor_scalar(out, hT[:, c, :], vcol("norm_ffn", c), None, ALU.mult).then_inc(nt_made, 1)
                if c:
                    low("ffn", c - 1, nH, nL)

            residual("mem_o", "ffn", after=with_gain)
            low("ffn", DC - 1, nH, nL)
            for c in (0, S + 1):
                V.memset(gpad[:, :, c:c + 1], 0.0).then_inc(borders, 1)
            dve.wait_ge(borders, 2)
            inverse("ffn")
            for j in range(FC):
                w = [vcol("conv_w", 3 * j + t) for t in range(3)]
                x, y = gpad[:, j % 2, :], cv[:, j % 2, :]
                b, free = product("up", 2 * j)
                V.tensor_tensor(x[:, 1:S + 1], b, rstd[:, :], ALU.mult).then_inc(free, 1)
                out_of_bank(dve, FIRST["up"] + 2 * j)
                own(V.tensor_scalar(y, x[:, 1:S + 1], w[1], vcol("conv_b", j), ALU.mult, ALU.add))
                own(V.scalar_tensor_tensor(out=y, in0=x[:, 0:S], scalar=w[0], in1=y, op0=ALU.mult, op1=ALU.add))
                V.scalar_tensor_tensor(out=y, in0=x[:, 2:S + 2], scalar=w[2], in1=y,
                                       op0=ALU.mult, op1=ALU.add).then_inc(conv_made, 1)
                dve.wait_ge(conv_made, j + 1)
                own(V.tensor_tensor(x[:, 1:S + 1], y, rstd[:, :], ALU.mult))
                dve.wait_ge(fsg_made, j + 1)
                out = open_split("hidden", j)
                b, free = product("up", 2 * j + 1)
                V.tensor_tensor(fu[:, j % 2, :], b, sgb[:, j % 2, :], ALU.mult).then_inc(free, 1)
                out_of_bank(dve, FIRST["up"] + 2 * j + 1)
                V.tensor_tensor(out, fu[:, j % 2, :], x[:, 1:S + 1], ALU.mult).then_inc(nt_made, 1)
                if j:
                    low("hidden", j - 1, aH, aL)
            low("hidden", FC - 1, aH, aL)
            def add_squares(c):
                for n, total in ((0, sums), (1, sums2)):
                    a = ADDED["final"] + 2 * (c - 1) + n
                    dve.wait_ge(sq_made, SQUARE["final"] + 2 * c + n + 1)
                    dve.wait_ge(sq_added, a)
                    V.tensor_tensor(total[:, :], total[:, :], sq[:, a % 2, :], ALU.add).then_inc(sq_added, 1)

            for c in range(DC):
                if c >= 2:
                    add_squares(c - 1)
                b, free = product("down", c)
                V.tensor_tensor(hT[:, c, :], b, hT[:, c, :], ALU.add).then_inc(free, 1)
                out_of_bank(dve, FIRST["down"] + c)
                dve.wait_ge(sq_made, SQUARE["final"] + 2 * c + 1)
                V.tensor_scalar(hT[:, c, :], hT[:, c, :], vcol("final_norm", c), None, ALU.mult).then_inc(hg_made, 1)
            add_squares(DC - 1)

            dve.wait_ge(sum_done, NORMS.index("mix2") + 1)
            own(V.tensor_scalar(sums[:, :], bank(7), EPS, None, ALU.mult))
            V.tensor_tensor(sums2[:, :], bank(6), sums[:, :], ALU.add).then_inc(var_made, 1)
            dve.wait_ge(std_made, NORMS.index("final") + 1)
            V.reciprocal(sums[:, :], std[:, :]).then_inc(r_made, 1)
            dve.wait_ge(r_made, NORMS.index("final") + 1)
            for c in range(DC):
                V.scalar_tensor_tensor(out=open_split("mix2", c), in0=hT[:, c, :], scalar=vcol("norm_g_2", c),
                                       in1=sums[:, :], op0=ALU.mult, op1=ALU.mult).then_inc(nt_made, 1)
                if c:
                    low("mix2", c - 1, nH, nL)
            low("mix2", DC - 1, nH, nL)
            inverse("mix2")
            for c in range(DC):
                V.tensor_tensor(hT[:, c, :], hT[:, c, :], rstd[:, :], ALU.mult).then_inc(x1_made, 1)
            dve.wait_ge(ld_d, 32)
            out_of_bank(dve, FIRST["k_idx"])
            for g in range(4):
                V.tensor_scalar(kiz[:, g, :], ki[:, :], c_d("group", g, g + 1), None, ALU.mult).then_inc(kiz_made, 1)
            accumulate_all("q_lat")
            silu("z_a", [0], za)
            inverse("q_lat")
            accumulate_all("c_kv")
            norm("q_lat", qlat, "g_q_lat_2", qlH, qlL)
            silu("z_a", [1], za)
            inverse("c_kv")
            norm("c_kv", ckv, "g_kv_lat_2", ckH, ckL)
            out_of_bank(dve, FIRST["w_turn"])
            at = {1: 0, 2: 2 * P, 3: 5 * P}
            silu("z_a", [2], za)
            for n in range(3 * IDX_HEADS):
                if n == 2:
                    silu("z_a", [3], za)
                i, h = n // IDX_HEADS + 1, n % IDX_HEADS
                w = P * (i + 1)
                acc = selm[:, at[i]:at[i] + w]
                dve.wait_ge(t_relu, n + 1)
                if h:
                    dve.wait_ge(t_acc, n)
                V.scalar_tensor_tensor(out=acc, in0=rl[:, n % 2, :w], scalar=wtok[:, i, h:h + 1],
                                       in1=acc if h else c_d("causal", S - w, S),
                                       op0=ALU.mult, op1=ALU.add).then_inc(t_acc, 1)
            dve.wait_ge(t_acc, 3 * IDX_HEADS)

            def top_keys(i, rnd):
                acc = selm[:, at[i]:at[i] + P * (i + 1)]
                own(V.max(best[:, :], acc))
                own(V.match_replace(acc, best[:, :], acc, TAKEN))
                if rnd == TOPK // 8 - 1:
                    own(V.tensor_scalar(acc, acc, 0.9 * TAKEN, NEG, ALU.is_gt, ALU.mult))

            for c in (2, 3):
                out_of_bank(dve, FIRST["z_a"] + c)
            rotate("second", 0, kp[:, :], c_d("cos", 0, S), c_d("sin", 0, S))
            dve.wait_ge(rotated, ROTATE["second"] + 1)
            for g in range(4):
                V.tensor_scalar(kpz[:, g, :], kp[:, :], c_d("group", g, g + 1), None, ALU.mult).then_inc(kpz_made, 1)
            for r in range(TOPK // 8 // 2):
                top_keys(1, r)
            for c in range(2):
                rotate("second", 1 + c, qp[:, c, :], c_d("cos", 0, S), c_d("sin", 0, S))
            for r in range(TOPK // 8 // 2, TOPK // 8):
                top_keys(1, r)
            barrier()

            def causal_mask(i):
                return c_d("causal", S - P * (i + 1), S)

            def dsa_gate(stage, j):
                if stage == "z_b":
                    silu(stage, [j], zb)

            def mla_beside(x):
                top_keys(2 + x // 16, x % 16)
                dsa_gate(*dsa_item(x))

            attention("mla", dx, MLA_SCALE, causal_mask, yaH, yaL, gate=za, beside=mla_beside)
            for item in DSA_ITEMS[-2:]:
                dsa_gate(*item)
            barrier()
            dve.wait_ge(ld_toep, 16 * 4)

            def top_mask(i):
                if i == 0:
                    return causal_mask(0)
                return selm[:, at[i]:at[i] + P * (i + 1)]

            def head_bias(h, i):
                if h >= 4 and i == 0:
                    dve.wait_ge(ld_late[h - 4], 16)
                return toep[:, h % 4, S - P * (i + 1):]

            attention("dsa", dx, ATT_SCALE, top_mask, ybH, ybL, gate=zb, bias=head_bias,
                      beside=lambda x: [first_branch("a_mix", p, sgD, mtD) for p in mix_pairs(x)])
            first_branch("a_mix", 3, sgD, mtD)
            barrier()
            merge("b_mix", sgD, mtD, addD, "merged2", mg2H, mg2L)
            dve.wait_ge(ld_x1, 16)
            residual("out2", "out")
            inverse("out")
            for c in range(DC):
                normed(hT[:, c, :], hT, "final_g_2", c).then_inc(y_made, 1)


def level_constants():
    out = {n: np.zeros((P, LQ), np.float32) for n in ("Qf", "Qb", "Kf", "Kb")}
    masks = np.zeros((P, 8, P), np.float32)
    u = np.arange(P)
    for l in range(LEVELS):
        c = 1 << l
        for b in range(HALF // c):
            mid = 2 * c * b + c
            for j in range(c):
                col, late, early = l * HALF + b * c + j, mid + j, mid - c + j
                out["Qf"][:, col] = (u >= mid) & (u <= late)
                out["Qb"][:, col] = (u >= early) & (u < mid)
                out["Kf"][:, col] = (u > early) & (u < mid)
                out["Kb"][:, col] = (u >= mid) & (u < late)
            lo, hi = slice(mid - c, mid), slice(mid, mid + c)
            masks[lo, l, hi] = 1.0
            masks[hi, l, lo] = 1.0
    masks[:, LEVELS, :] = np.eye(P)
    s, t = u[:, None], u[None, :]
    out["Pf"], out["Uf"] = s <= t, s > t
    out["Pb"], out["Ub"] = s >= t, s < t
    out["level"] = masks.reshape(P, -1)
    return out


def rotary_partners(group, half):
    m = np.zeros((P, P), np.float32)
    for g in range(0, P, group):
        for r in range(half):
            m[g + half + r, g + r] = -1.0
            m[g + r, g + half + r] = 1.0
    return m


def constants_a():
    c = level_constants()
    c["perm"] = rotary_partners(64, ROT_HALF)
    q, k = np.arange(P)[:, None], np.arange(3 * P)[None, :] - P
    c["band"] = np.where(np.abs(q - k) <= 128, 0.0, NEG)
    c["all"] = np.ones((P, P))
    return [np.concatenate([np.asarray(c[n], np.float32) for n, _ in table], 1) for table in (CONST_R, CONST_A)]


def constants_d():
    c = {"perm": rotary_partners(32, 16)}
    freqs = np.float32(10000.0) ** (-np.arange(16, dtype=np.float32) / np.float32(16))
    angle = np.arange(S, dtype=np.float32)[None, :] * freqs[np.arange(P) % 16][:, None]
    c["cos"], c["sin"] = np.cos(angle), np.sin(angle)
    q, k = np.arange(P)[:, None], np.arange(S)[None, :] - (S - P)
    c["causal"] = np.where((k < 0) | (k // 64 <= q // 64), 0.0, NEG)
    rel = np.arange(TOEP) - (S - 1)
    nb, exact = REL_BUCKETS // 2, REL_BUCKETS // 4
    n = np.abs(rel)
    far = np.log(np.maximum(n, 1).astype(np.float32) / np.float32(exact)) / np.log(REL_MAX / exact) * (nb - exact)
    far = np.minimum(exact + far.astype(np.float32).astype(np.int32), nb - 1)
    bucket = (rel > 0) * nb + np.where(n < exact, n, far)
    onehot = np.zeros((P, TOEP), np.float32)
    onehot[bucket, np.arange(TOEP)] = 1.0
    c["onehot"] = onehot
    c["group"] = np.arange(P)[:, None] // 32 == np.arange(4)[None, :]
    return np.concatenate([np.asarray(c[n], np.float32) for n, _ in CONST_D], 1)


def blocks(w, pad_to=None):
    k, n = w.shape
    x = w.reshape(k // P, P, n // P, P).transpose(2, 1, 0, 3).reshape(n // P, P, k)
    if pad_to is not None:
        x = np.concatenate([x, np.zeros((n // P, P, pad_to - k), w.dtype)], 2)
    return x


def wide(w):
    return np.concatenate([w, np.zeros((w.shape[0], P - w.shape[1]), w.dtype)], 1)


def weight_stream(a):
    SLOT = BLK * P

    def per_slot(x, count):
        n, p, k = x.shape
        x = x.reshape(n // count, count, p, k).transpose(0, 2, 1, 3).reshape(n // count, p, count * k)
        return np.concatenate([x, np.zeros((n // count, p, SLOT - count * k), x.dtype)], 2)

    def mixed(gate, branch):
        g, y = blocks(gate), blocks(branch)
        g = g.reshape(DC // 2, 2, P, SLOT)
        y = y.reshape(DC // 2, 2, P, SLOT // 2).transpose(0, 2, 1, 3).reshape(DC // 2, 1, P, SLOT)
        return np.concatenate([g, y], 1).reshape(-1, P, SLOT)

    w = a["w_in"][0]
    cuts = np.cumsum([512] * 6 + [128, 128, 1024])
    q_r, fz_f, fz_b, i_r, g_r, q_a, k_a, v_a, gate_r, gate_a = np.split(w, cuts, 1)
    q_a = q_a.reshape(D, 2, 4, 64).transpose(0, 2, 1, 3).reshape(D, 512)
    br_att = a["w_br_att"][0].reshape(2, 4, 64, D).transpose(1, 0, 2, 3).reshape(512, D)
    mem_k, mem_v = np.split(a["w_mem_kv"][0], 2, 1)
    up, gate = (blocks(x) for x in np.split(a["w_up"][0], 2, 1))
    w2 = a["w_in_2"][0]
    cuts = np.cumsum([384, 256, 32, 512, 512, 512, 512, 512, 256, 32, 8, 1024])
    q_lat, c_kv, k_rope, z_a, q_b, k_b, v_b, z_b, q_idx, k_idx, w_idx, gate_a2, gate_b2 = np.split(w2, cuts, 1)
    uq = a["w_uq_2"][0].reshape(384, 8, 96)
    uq = np.concatenate([uq[:, :, :64].reshape(384, 512), uq[:, :, 64:].reshape(384, 256)], 1)
    ukv = a["w_ukv_2"][0].reshape(256, 8, 128)
    ukv_k, ukv_v = ukv[:, :, :64].reshape(256, 512), ukv[:, :, 64:].reshape(256, 512)
    parts = {
        "g_first": blocks(g_r[:, :P]), "g_rest": blocks(g_r[:, P:]),
        "q_a": blocks(q_a), "k_a": blocks(k_a), "v_a": blocks(v_a),
        "rec_mix": mixed(gate_r, a["w_br_rec"][0]), "att_mix": mixed(gate_a, br_att),
        "mix_out": blocks(a["w_mix_out"][0]),
        "mem_o": blocks(a["w_mem_o"][0]),
        "up": np.stack([gate, up], 1).reshape(-1, P, SLOT),
        "down": blocks(a["w_down"][0], 3 * SLOT).reshape(DC, P, 3, SLOT).transpose(0, 2, 1, 3).reshape(-1, P, SLOT),
        "q_idx": blocks(q_idx), "k_idx": blocks(np.tile(k_idx, (1, 4))), "w_idx": blocks(wide(w_idx)),
        "q_lat": blocks(q_lat), "c_kv": blocks(c_kv), "k_rope": blocks(np.tile(k_rope, (1, 4))),
        "uq": per_slot(blocks(uq), 2), "ukv_k": per_slot(blocks(ukv_k), 2), "ukv_v": per_slot(blocks(ukv_v), 2),
        "z_a": blocks(z_a), "q_b": blocks(q_b), "k_b": blocks(k_b), "v_b": blocks(v_b), "z_b": blocks(z_b),
        "a_mix": mixed(gate_a2, a["w_o_a_2"][0]), "b_mix": mixed(gate_b2, a["w_o_b_2"][0]), "out2": blocks(a["w_out_2"][0]),
    }
    for h in range(HG_HEADS):
        cs = slice(P * h, P * h + P)
        parts[f"head{h}"] = np.concatenate([blocks(w[:, cs]) for w in (fz_f, fz_b, q_r, i_r)], 0)
    for h in range(MEM_HEADS):
        cs = slice(256 * h, 256 * h + 256)
        parts[f"mem{h}"] = np.concatenate([blocks(w[:, cs]) for w in (mem_k, mem_v, a["w_mem_q"][0])], 0)
    out = [parts[name] for name, need in STREAM if sum(need)]
    n = sum(len(x) for x in out)
    return np.concatenate(out + [np.zeros((SLOTS - n, P, SLOT), np.float32)], 0)


def columns(x):
    return np.asarray(x).reshape(-1, P).T


def feature_vectors(a):
    inv = np.zeros((P, 1), np.float32)
    freq = (1.0 / (np.float32(ROPE_THETA) ** (np.arange(0, 16, 2, dtype=np.float32) / np.float32(16)))).astype(np.float32)
    for g in (0, 64):
        for r in range(2):
            inv[g + ROT_HALF * r:g + ROT_HALF * (r + 1), 0] = freq
    conv = a["conv_w"][0].reshape(3, FC, P).transpose(2, 1, 0).reshape(P, 3 * FC)
    lower = a["lower_bounds"].reshape(2, 2, HG_HEADS, P).transpose(3, 0, 1, 2).reshape(P, 16)
    named = {n: columns(a[n]) for n, _ in [("norm_mix", 0), ("norm_mem", 0), ("norm_mem_kv", 0), ("norm_ffn", 0),
                                            ("final_norm", 0), ("norm_g_2", 0), ("final_g_2", 0), ("g_q_lat_2", 0),
                                            ("g_kv_lat_2", 0), ("hg_norm", 0), ("conv_b", 0)]}
    named.update(conv_w=conv, lower=lower, inv_freq=inv)
    return np.concatenate([named[n] for n in VEC], 1)


def features_first(x):
    x = np.asarray(x)[0]
    return np.ascontiguousarray(x.T.reshape(-1, P, x.shape[0]).transpose(1, 0, 2))


def kernel(**inputs):
    import concourse.bacc as bacc
    from concourse.bass_utils import run_bass_kernel_spmd

    a = {k: np.asarray(v) for k, v in inputs.items()}
    const_r, const_a = constants_a()
    arrays = {
        "stream": weight_stream(a), "xT": features_first(a["x"]), "memT": features_first(a["mem"]),
        "pos": a["positions"].astype(np.int32).reshape(S), "vecs": feature_vectors(a),
        "ident": np.eye(P, dtype=np.float32), "const_r": const_r, "const_a": const_a, "const_d": constants_d(),
        "sink": a["attn_sink"].reshape(8), "relb": a["rel_bias_2"],
    }
    arrays = {k: np.ascontiguousarray(v) for k, v in arrays.items()}
    nc = bacc.Bacc("TRN2", target_bir_lowering=False, num_devices=1, dynamic_dma_scratch_size=1024)
    ins = [nc.dram_tensor(k, v.shape, mybir.dt.from_np(v.dtype), kind="ExternalInput").ap() for k, v in arrays.items()]
    gvec = nc.dram_tensor("gvec", (8, P, TOEP), F32).ap()
    x1_d = nc.dram_tensor("x1_d", (P, DC, S), F32).ap()
    outT = nc.dram_tensor("outT", (P, DC, S), F32, kind="ExternalOutput").ap()
    build(nc, *ins, gvec, x1_d, outT)
    r = run_bass_kernel_spmd(nc, [arrays], core_ids=[0])
    y = r.results[0]["outT"]
    return np.ascontiguousarray(y.transpose(2, 1, 0).reshape(1, S, D))
```
